# Optimizing a Trainium2 kernel written in Bass

```python
import jax, jax.numpy as jnp
from jax import lax
import numpy as np

D_MODEL = 1024
BATCH = 1
SEQ = 2048
DEPTH = 1

D_MIX = D_MODEL
D_RWKV = D_MIX // 2
D_CONV = D_MIX - D_RWKV
HEAD_SIZE = 64
N_RWKV_HEADS = D_RWKV // HEAD_SIZE
CONV_GROUPS = 8
CONV_WIDTH = 3
D_DECAY_LORA = 64
D_AAA_LORA = 64
D_GATE_LORA = 160
D_FF = -(-(8 * D_MODEL) // (3 * 256)) * 256
D_SHIFTED = 3 * D_RWKV + D_DECAY_LORA + D_AAA_LORA + D_GATE_LORA
D_IN = D_SHIFTED + 3 * D_CONV
LOG_DECAY_SCALE = 0.606531
RMS_EPS = 1e-6
GN_EPS = 64e-5
NORM_EPS = 1e-12

kernel_name = "hybrid_rwkv7_shortconv_encoder_block"

def _rmsnorm(x, w):
    x32 = x.astype(jnp.float32)
    y = x32 * lax.rsqrt(jnp.mean(x32 * x32, axis=-1, keepdims=True) + RMS_EPS)
    return (y * w.astype(jnp.float32)).astype(x.dtype)

def _token_shift(p, mu):
    zeros = jnp.zeros_like(p[:, :1])
    prev = jnp.concatenate([zeros, p[:, :-1]], axis=1)
    nxt = jnp.concatenate([p[:, 1:], zeros], axis=1)
    return p + mu * (0.5 * (prev + nxt) - p)

def _to_heads(t):
    b, s, _ = t.shape
    return t.reshape(b, s, N_RWKV_HEADS, HEAD_SIZE)

def _wkv7_scan(r, w, k, v, kk, a, reverse):
    b = r.shape[0]
    xs = tuple(jnp.swapaxes(t, 0, 1) for t in (r, w, k, v, kk, a))

    def step(state, inp):
        r_t, w_t, k_t, v_t, kk_t, a_t = inp
        sa = jnp.einsum('bhvk,bhk->bhv', state, kk_t)
        state = (state * w_t[:, :, None, :]
                 - sa[..., None] * (kk_t * a_t)[:, :, None, :]
                 + v_t[..., None] * k_t[:, :, None, :])
        y_t = jnp.einsum('bhvk,bhk->bhv', state, r_t)
        return state, y_t

    s0 = jnp.zeros((b, N_RWKV_HEADS, HEAD_SIZE, HEAD_SIZE), jnp.float32)
    _, ys = lax.scan(step, s0, xs, reverse=reverse)
    return jnp.swapaxes(ys, 0, 1)

def _rwkv7_direction(r, k, v, kk, xw, xa, w_up, w0, a_up, a0, k_a, r_k, reverse):
    logit_w = w0 + jnp.tanh(xw) @ w_up.astype(jnp.float32)
    w = jnp.exp(-LOG_DECAY_SCALE * jax.nn.sigmoid(logit_w))
    a = jax.nn.sigmoid(a0 + xa @ a_up.astype(jnp.float32))
    kd = k * (1.0 + (a - 1.0) * k_a)
    rh, kh, vh = _to_heads(r), _to_heads(kd), _to_heads(v)
    y = _wkv7_scan(rh, _to_heads(w), kh, vh, kk, _to_heads(a), reverse)
    bonus = jnp.sum(rh * kh * r_k, axis=-1, keepdims=True) * vh
    return y, bonus

def _rwkv7_mixer(r, k, v, xw, xa, xg, w_up_f, w0_f, w_up_b, w0_b, a_up_f, a0_f,
                 a_up_b, a0_b, g_up, k_k, k_a_f, k_a_b, r_k_f, r_k_b, gn_w, gn_b):
    out_dtype = r.dtype
    r, k, v, xw, xa, xg = (t.astype(jnp.float32) for t in (r, k, v, xw, xa, xg))
    kk = _to_heads(k * k_k)
    kk = kk / jnp.maximum(jnp.linalg.norm(kk, axis=-1, keepdims=True), NORM_EPS)
    y_f, bonus_f = _rwkv7_direction(r, k, v, kk, xw, xa, w_up_f, w0_f, a_up_f, a0_f,
                                    k_a_f, r_k_f, reverse=False)
    y_b, bonus_b = _rwkv7_direction(r, k, v, kk, xw, xa, w_up_b, w0_b, a_up_b, a0_b,
                                    k_a_b, r_k_b, reverse=True)
    y = y_f + y_b
    mean = jnp.mean(y, axis=-1, keepdims=True)
    var = jnp.mean(jnp.square(y - mean), axis=-1, keepdims=True)
    y = (y - mean) * lax.rsqrt(var + GN_EPS)
    y = y * gn_w.reshape(N_RWKV_HEADS, HEAD_SIZE) + gn_b.reshape(N_RWKV_HEADS, HEAD_SIZE)
    y = y + bonus_f + bonus_b
    g = jax.nn.sigmoid(xg) @ g_up.astype(jnp.float32)
    b, s = r.shape[:2]
    return (y.reshape(b, s, D_RWKV) * g).astype(out_dtype)

def _short_conv(pc, conv_w):
    gate_b, gate_c, h = jnp.split(pc, [D_CONV, 2 * D_CONV], axis=-1)
    u = gate_c * h
    u = lax.conv_general_dilated(
        u, conv_w.reshape(CONV_WIDTH, 1, D_CONV).astype(u.dtype),
        window_strides=(1,), padding=[((CONV_WIDTH - 1) // 2, (CONV_WIDTH - 1) // 2)],
        dimension_numbers=('NWC', 'WIO', 'NWC'), feature_group_count=D_CONV)
    return gate_b * u

def _swiglu(h, w_gate, w_up, w_down):
    return (jax.nn.silu(h @ w_gate) * (h @ w_up)) @ w_down

def setup_inputs(seed: int = 0) -> dict:
    key = jax.random.key(seed)
    ks = jax.random.split(key, 32)

    def nrm(k, shape, scale):
        return jax.random.normal(k, shape, jnp.float32) * scale

    L = DEPTH
    return {
        "x": nrm(ks[0], (BATCH, SEQ, D_MODEL), 1.0),
        "norm1_w": 1.0 + nrm(ks[1], (L, D_MODEL), 0.02),
        "w_in": nrm(ks[2], (L, D_MODEL, D_IN), D_MODEL ** -0.5),
        "mu_shift": jax.random.uniform(ks[3], (L, D_SHIFTED), jnp.float32),
        "w_up_f": nrm(ks[4], (L, D_DECAY_LORA, D_RWKV), D_DECAY_LORA ** -0.5),
        "w0_f": nrm(ks[5], (L, D_RWKV), 1.0),
        "w_up_b": nrm(ks[6], (L, D_DECAY_LORA, D_RWKV), D_DECAY_LORA ** -0.5),
        "w0_b": nrm(ks[7], (L, D_RWKV), 1.0),
        "a_up_f": nrm(ks[8], (L, D_AAA_LORA, D_RWKV), D_AAA_LORA ** -0.5),
        "a0_f": nrm(ks[9], (L, D_RWKV), 0.5),
        "a_up_b": nrm(ks[10], (L, D_AAA_LORA, D_RWKV), D_AAA_LORA ** -0.5),
        "a0_b": nrm(ks[11], (L, D_RWKV), 0.5),
        "g_up": nrm(ks[12], (L, D_GATE_LORA, D_RWKV), D_GATE_LORA ** -0.5),
        "k_k": 0.85 + nrm(ks[13], (L, D_RWKV), 0.05),
        "k_a_f": 1.0 + nrm(ks[14], (L, D_RWKV), 0.05),
        "k_a_b": 1.0 + nrm(ks[15], (L, D_RWKV), 0.05),
        "r_k_f": nrm(ks[16], (L, N_RWKV_HEADS, HEAD_SIZE), 0.1),
        "r_k_b": nrm(ks[17], (L, N_RWKV_HEADS, HEAD_SIZE), 0.1),
        "gn_w": 1.0 + nrm(ks[18], (L, D_RWKV), 0.02),
        "gn_b": nrm(ks[19], (L, D_RWKV), 0.02),
        "conv_w": nrm(ks[20], (L, CONV_WIDTH, D_CONV), CONV_WIDTH ** -0.5),
        "w_out": nrm(ks[21], (L, D_MIX, D_MODEL), D_MIX ** -0.5),
        "norm2_w": 1.0 + nrm(ks[22], (L, D_MODEL), 0.02),
        "w_gate": nrm(ks[23], (L, D_MODEL, D_FF), D_MODEL ** -0.5),
        "w_up": nrm(ks[24], (L, D_MODEL, D_FF), D_MODEL ** -0.5),
        "w_down": nrm(ks[25], (L, D_FF, D_MODEL), D_FF ** -0.5),
        "norm_f_w": 1.0 + nrm(ks[26], (D_MODEL,), 0.02),
    }

def reference(x, norm1_w, w_in, mu_shift, w_up_f, w0_f, w_up_b, w0_b, a_up_f, a0_f,
              a_up_b, a0_b, g_up, k_k, k_a_f, k_a_b, r_k_f, r_k_b, gn_w, gn_b, conv_w,
              w_out, norm2_w, w_gate, w_up, w_down, norm_f_w):
    split_pts = [D_RWKV, 2 * D_RWKV, 3 * D_RWKV, 3 * D_RWKV + D_DECAY_LORA,
                 3 * D_RWKV + D_DECAY_LORA + D_AAA_LORA]
    for l in range(DEPTH):
        h = _rmsnorm(x, norm1_w[l])
        p = h @ w_in[l]
        ps, pc = p[..., :D_SHIFTED], p[..., D_SHIFTED:]
        ps = _token_shift(ps, mu_shift[l])
        r, k, v, xw, xa, xg = jnp.split(ps, split_pts, axis=-1)
        o_rwkv = _rwkv7_mixer(r, k, v, xw, xa, xg, w_up_f[l], w0_f[l], w_up_b[l], w0_b[l],
                              a_up_f[l], a0_f[l], a_up_b[l], a0_b[l], g_up[l], k_k[l],
                              k_a_f[l], k_a_b[l], r_k_f[l], r_k_b[l], gn_w[l], gn_b[l])
        o_conv = _short_conv(pc, conv_w[l])
        x = x + jnp.concatenate([o_rwkv, o_conv], axis=-1) @ w_out[l]
        x = x + _swiglu(_rmsnorm(x, norm2_w[l]), w_gate[l], w_up[l], w_down[l])
    return _rmsnorm(x, norm_f_w)


_drawn_inputs = setup_inputs


def setup_inputs(seed=0):
    import zlib

    import numpy as np

    out = dict(_drawn_inputs(seed))
    spreads = {}
    factors = {'k_k': 8.0,
     'k_a_f': 4.787,
     'k_a_b': 4.63,
     'gn_w': 8.0,
     'gn_b': 8.0,
     'norm2_w': 4.629,
     'norm_f_w': 2.801}
    for name, (base, spread) in spreads.items():
        noise = np.random.default_rng([zlib.crc32(name.encode()), seed]).standard_normal(out[name].shape)
        drawn = base * np.exp(spread * noise) if base else spread * noise
        out[name] = __import__('jax').numpy.asarray(drawn.astype(out[name].dtype))
    for name, factor in factors.items():
        out[name] = (out[name] * factor).astype(out[name].dtype)
    return out
```

```python
from contextlib import ExitStack

import numpy as np

import concourse.bass as bass
from concourse import mybir

F32 = mybir.dt.float32
F16 = mybir.dt.float16
ALU = mybir.AluOpType
ACT = mybir.ActivationFunctionType

P = 128
D = 1024
S = 2048
KT = D // P
TT = S // P
NB = S // 512
HP = 4
C = 64
NCH = S // C
F = 2816
FT = F // P
DECAY = 0.606531
RMS_EPS = 1e-6
GN_EPS = 64e-5
NORM_EPS = 1e-12
ONE = 1
WS = 64.0

(MU_R, MU_K, MU_V, K_K, W0_F, W0_B, A0_F, A0_B, KA_F, KA_B, RK_F, RK_B, GN_W, GN_B, CW0, CW1, CW2) = range(17)
NPC = 17
MU_WA, MU_G0, MU_G1 = HP * NPC, HP * NPC + 1, HP * NPC + 2
NCOL = HP * NPC + 3
T_WA, T_G0, T_G1, T_LOOP = 0, 1, 2, 3
TILES = ("r", "k", "v", "c", "h", "b")


class Chain:

    def __init__(self, eng, sem, base=0):
        self.eng, self.sem, self.base, self.n = eng, sem, base, 0

    def inc(self, ins):
        ins.then_inc(self.sem, 1)
        self.n += 1
        return self.n

    def wait(self, n):
        self.eng.wait_ge(self.sem, ONE + self.base + n)

    def link(self, ins):
        self.wait(self.inc(ins))


PASSED = []


def alone(eng, sem, value):
    eng.wait_ge(sem, ONE + value)
    eng.sem_inc(PASSED[-1], 1)


class Scope:

    def __init__(self, nc, stack, prefix):
        self.nc, self.stack, self.prefix, self.sems = nc, stack, prefix, []

    def sb(self, name, shape, dt=F32):
        return self.stack.enter_context(self.nc.sbuf_tensor(f"{self.prefix}_{name}", shape, dt))

    def ps(self, name, shape=(P, 512), dt=F32):
        return self.stack.enter_context(self.nc.psum_tensor(f"{self.prefix}_{name}", list(shape), dt))

    def sem(self, name):
        self.sems.append(self.stack.enter_context(self.nc.semaphore(f"{self.prefix}_{name}")))
        return self.sems[-1]

    def start_at_one(self, eng):
        for sem in self.sems:
            eng.sem_inc(sem, ONE)


def phase_norm1(nc, x, norm_w, ident, hT_hi, hT_lo):
    with ExitStack() as stack:
        sc = Scope(nc, stack, "n1")
        xt = [sc.sb(f"x{s}", [P, D]) for s in range(2)]
        xn = [sc.sb(f"xn{s}", [P, D]) for s in range(2)]
        wrow = sc.sb("wrow", [P, D])
        idn = sc.sb("ident", [P, P])
        ss = [sc.sb(f"ss{s}", [P, 4]) for s in range(2)]
        ps = [[sc.ps(f"t{s}{g}", (P, 4, P)) for g in range(2)] for s in range(2)]
        const_in = sc.sem("const_in")
        x_in = [sc.sem(f"x_in{s}") for s in range(2)]
        squared, rooted, scaled = sc.sem("squared"), sc.sem("rooted"), sc.sem("scaled")
        turned, hi_done, lo_done = sc.sem("turned"), sc.sem("hi_done"), sc.sem("lo_done")
        var_done, dve_own = sc.sem("var_done"), sc.sem("dve_own")
        block = stack.enter_context(nc.Block())

        @block.sync
        def _(sp):
            sc.start_at_one(sp)
            sp.dma_start(idn[:, :], ident).then_inc(const_in, 16)
            sp.dma_start(wrow[:, :], norm_w.partition_broadcast(P)).then_inc(const_in, 16)
            for s in range(2):
                sp.dma_start(xt[s][:, :], x[s * P:(s + 1) * P, :]).then_inc(x_in[s], 16)
            with sp.Fori(1, TT // 2) as i:
                for s in range(2):
                    sp.wait_ge(scaled, ONE + 2 * i + s - 1)
                    sp.dma_start(xt[s][:, :], x[bass.ds((2 * i + s) * P, P), :]).then_inc(x_in[s], 16)

        @block.scalar
        def _(act):
            with act.Fori(0, TT // 2) as i:
                for s in range(2):
                    act.wait_ge(x_in[s], ONE + 16 * i + 16)
                    act.wait_ge(turned, ONE + 4 * i)
                    nc.scalar.activation(xn[s][:, :], xt[s][:, :], ACT.Square,
                                         accum_out=ss[s][:, 0:1]).then_inc(squared, 1)
                for s in range(2):
                    act.wait_ge(var_done, ONE + 2 * i + s + 1)
                    nc.scalar.activation(ss[s][:, 2:3], ss[s][:, 1:2], ACT.Sqrt).then_inc(rooted, 1)
                for s in range(2):
                    for g in range(2):
                        act.wait_ge(turned, ONE + 4 * i + 2 * s + g + 1)
                        nc.scalar.activation(hT_hi[:, 4 * g:4 * g + 4, bass.ds((2 * i + s) * P, P)],
                                             ps[s][g][:, :, :], ACT.Copy).then_inc(hi_done, 1)

        @block.vector
        def _(dve):
            dve.wait_ge(const_in, ONE + 32)
            with dve.Fori(0, TT // 2) as i:
                own = Chain(dve, dve_own, 2 * i)
                for s in range(2):
                    dve.wait_ge(squared, ONE + 2 * i + s + 1)
                    nc.vector.tensor_scalar(ss[s][:, 1:2], ss[s][:, 0:1], 1.0 / D, RMS_EPS,
                                            ALU.mult, ALU.add).then_inc(var_done, 1)
                for s in range(2):
                    dve.wait_ge(rooted, ONE + 2 * i + s + 1)
                    own.link(nc.vector.reciprocal(ss[s][:, 3:4], ss[s][:, 2:3]))
                    nc.vector.scalar_tensor_tensor(out=xn[s][:, :], in0=xt[s][:, :], scalar=ss[s][:, 3:4],
                                                   in1=wrow[:, :], op0=ALU.mult, op1=ALU.mult).then_inc(scaled, 1)
                for s in range(2):
                    for g in range(2):
                        dve.wait_ge(hi_done, ONE + 4 * i + 2 * s + g + 1)
                        tok = bass.ds((2 * i + s) * P, P)
                        nc.vector.tensor_tensor(hT_lo[:, 4 * g:4 * g + 4, tok], ps[s][g][:, :, :],
                                                hT_hi[:, 4 * g:4 * g + 4, tok], ALU.subtract).then_inc(lo_done, 1)

        @block.tensor
        def _(pe):
            pe.wait_ge(const_in, ONE + 32)
            with pe.Fori(0, TT // 2) as i:
                for s in range(2):
                    pe.wait_ge(scaled, ONE + 2 * i + s + 1)
                    for g in range(2):
                        pe.wait_ge(lo_done, ONE + 4 * i)
                        for k in range(4):
                            kt = 4 * g + k
                            ins = nc.tensor.transpose(ps[s][g][:, k, :], xn[s][:, kt * P:(kt + 1) * P], idn[:, :])
                        ins.then_inc(turned, 1)


def phase_inproj(nc, d, hT_hi, hT_lo, oc_hi, oc_lo):
    with ExitStack() as stack:
        sc = Scope(nc, stack, "ip")
        chan = sc.sb("chan", [P, NCOL])
        half = sc.sb("half", [P, NCOL])
        rest = sc.sb("rest", [P, NCOL])
        ones = sc.sb("ones", [P, P])
        wst = [sc.sb(f"wst{s}", [P, KT, P]) for s in range(2)]
        w_hi = [sc.sb(f"whi{s}", [P, KT, P], F16) for s in range(2)]
        w_lo = [sc.sb(f"wlo{s}", [P, KT, P], F16) for s in range(2)]
        xwa_hi, xwa_lo = sc.sb("xwa_hi", [P, S], F16), sc.sb("xwa_lo", [P, S], F16)
        lw_hi, lw_lo = sc.sb("lw_hi", [P, 4, 512], F16), sc.sb("lw_lo", [P, 4, 512], F16)
        raw = sc.sb("raw", [P, S + 2])
        tmp = sc.sb("tmp", [P, S + 2])
        Cb = sc.sb("Cb", [P, S])
        Q = raw
        ring = [sc.ps(f"ring{n}") for n in range(6)]
        small = [sc.ps(f"small{n}") for n in range(2)]

        const_in = sc.sem("const_in")
        prep = sc.sem("prep")
        w_in = [sc.sem(f"w_in{s}") for s in range(2)]
        hi_ready, lo_ready = sc.sem("hi_ready"), sc.sem("lo_ready")
        tile_done = sc.sem("tile_done")
        blk_done = sc.sem("blk_done")
        act_left, dve_left = sc.sem("act_left"), sc.sem("dve_left")
        sm_done = sc.sem("sm_done")
        sm_act, sm_dve = sc.sem("sm_act"), sc.sem("sm_dve")
        raw_full, raw_free = sc.sem("raw_full"), sc.sem("raw_free")
        dve_own, act_own = sc.sem("dve_own"), sc.sem("act_own")

        def big_block(pe, slot, n, b):
            tok = slice(512 * b, 512 * b + 512)
            for k in range(KT):
                for wt, ht in ((w_hi, hT_hi), (w_hi, hT_lo), (w_lo, hT_hi)):
                    ins = nc.tensor.matmul(ring[n % 6][:, :], wt[slot][:, k, :], ht[:, k, tok],
                                           start=(k == 0 and wt is w_hi and ht is hT_hi),
                                           stop=(k == KT - 1 and wt is w_lo))
            ins.then_inc(blk_done, 1)

        with ExitStack() as st2:
            s2 = Scope(nc, st2, "ip0")
            lst = s2.sb("lst", [P, 4, 512])
            gst = s2.sb("gst", [P, 2, 512])
            lg_hi, lg_lo = s2.sb("lg_hi", [P, 2, 512], F16), s2.sb("lg_lo", [P, 2, 512], F16)
            sg_hi, sg_lo = s2.sb("sg_hi", [P, 2, S], F16), s2.sb("sg_lo", [P, 2, S], F16)
            act_t = s2.sb("act_t", [P, S])
            gout = [s2.sb(f"gout{n}", [P, 512]) for n in range(2)]
            lw_in, g_out = s2.sem("lw_in"), [s2.sem(f"g_out{n}") for n in range(2)]
            lsplit_hi, lsplit_lo = s2.sem("lsplit_hi"), s2.sem("lsplit_lo")
            shifted, bent, bent_lo = s2.sem("shifted"), s2.sem("bent"), s2.sem("bent_lo")
            zeroed = s2.sem("zeroed")
            block = st2.enter_context(nc.Block())
            GR = 32

            @block.sync
            def _(sp):
                sc.start_at_one(sp)
                s2.start_at_one(sp)
                sp.dma_start(chan[:, :], d["chan"]).then_inc(const_in, 16)
                sp.dma_start(ones[:, :], d["ones"]).then_inc(const_in, 16)
                for s in range(2):
                    sp.dma_start(wst[s][:, :, :], d["w_in"][s]).then_inc(w_in[s], 16)
                sp.wait_ge(zeroed, ONE + 1)
                for n, name in enumerate(("w_up_f", "w_up_b")):
                    sp.dma_start(lst[0:64, n, :], d[name]).then_inc(lw_in, 16)
                for n, name in enumerate(("a_up_f", "a_up_b")):
                    sp.dma_start(lst[64:128, 2 + n, :], d[name]).then_inc(lw_in, 16)
                sp.dma_start(gst[:, 0, :], d["g_up"][0:P, :]).then_inc(lw_in, 16)
                sp.dma_start(gst[0:GR, 1, :], d["g_up"][P:P + GR, :]).then_inc(lw_in, 16)
                for T in (2, 3):
                    sp.wait_ge(hi_ready, ONE + T - 1)
                    sp.wait_ge(lo_ready, ONE + T - 1)
                    sp.dma_start(wst[T % 2][:, :, :], d["w_in"][T]).then_inc(w_in[T % 2], 16)
                for n in range(4 * HP):
                    sp.wait_ge(sm_act, ONE + n + 1)
                    sp.dma_start(d["s_g"][n // 4, :, 512 * (n % 4):512 * (n % 4) + 512],
                                 gout[n % 2][:, :]).then_inc(g_out[n % 2], 16)
                for n in range(2):
                    sp.wait_ge(g_out[n], ONE + 16 * 2 * HP)

            @block.gpsimd
            def _(pool):
                nc.gpsimd.memset(lst[:, :, :], 0.0).then_inc(zeroed, 1)
                nc.gpsimd.memset(raw[:, 0:1], 0.0).then_inc(prep, 1)
                nc.gpsimd.memset(raw[:, S + 1:S + 2], 0.0).then_inc(prep, 1)
                nc.gpsimd.memset(tmp[:, 0:1], 0.0).then_inc(prep, 1)
                nc.gpsimd.memset(tmp[:, S + 1:S + 2], 0.0).then_inc(prep, 1)

            @block.scalar
            def _(act):
                def split_hi(T):
                    act.wait_ge(w_in[T % 2], ONE + 16 * (T // 2 + 1))
                    if T >= 2:
                        act.wait_ge(blk_done, ONE + NB * (T - 1))
                    nc.scalar.activation(w_hi[T % 2][:, :, :], wst[T % 2][:, :, :], ACT.Copy,
                                         scale=WS).then_inc(hi_ready, 1)

                split_hi(0)
                act.wait_ge(lw_in, ONE + 16 * 6)
                nc.scalar.activation(lw_hi[:, :, :], lst[:, :, :], ACT.Copy, scale=WS).then_inc(lsplit_hi, 1)
                nc.scalar.activation(lg_hi[:, 0, :], gst[:, 0, :], ACT.Copy, scale=WS).then_inc(lsplit_hi, 1)
                nc.scalar.activation(lg_hi[0:GR, 1, :], gst[0:GR, 1, :], ACT.Copy, scale=WS).then_inc(lsplit_hi, 1)
                for T in range(3):
                    split_hi(T + 1)
                    rows = P if T < T_G1 else GR
                    act.wait_ge(raw_free, ONE + T)
                    for b in range(NB):
                        act.wait_ge(blk_done, ONE + NB * T + b + 1)
                        nc.scalar.activation(raw[0:rows, 1 + 512 * b:513 + 512 * b],
                                             ring[(NB * T + b) % 6][0:rows, :], ACT.Copy,
                                             scale=1 / WS).then_inc(act_left, 1)
                    act.wait_ge(shifted, ONE + T + 1)
                    if T == T_WA:
                        nc.scalar.activation(act_t[0:64, :], tmp[0:64, 1:S + 1], ACT.Tanh).then_inc(act_own, 1)
                        nc.scalar.activation(act_t[64:128, :], tmp[64:128, 1:S + 1], ACT.Copy).then_inc(act_own, 1)
                        act.wait_ge(act_own, ONE + 2)
                        nc.scalar.activation(xwa_hi[:, :], act_t[:, :], ACT.Copy).then_inc(bent, 1)
                    else:
                        act.wait_ge(bent_lo, ONE + T)
                        nc.scalar.activation(act_t[0:rows, :], tmp[0:rows, 1:S + 1],
                                             ACT.Sigmoid).then_inc(act_own, 1)
                        act.wait_ge(act_own, ONE + T + 2)
                        nc.scalar.activation(sg_hi[0:rows, T - 1, :], act_t[0:rows, :], ACT.Copy).then_inc(bent, 1)
                for n in range(4 * HP):
                    act.wait_ge(sm_done, ONE + n + 1)
                    if n >= 2:
                        act.wait_ge(g_out[n % 2], ONE + 16 * (n // 2))
                    nc.scalar.activation(gout[n % 2][:, :], small[n % 2][:, :], ACT.Copy,
                                         scale=1 / WS).then_inc(sm_act, 1)

            @block.vector
            def _(dve):
                own = Chain(dve, dve_own)

                def split_lo(T):
                    dve.wait_ge(hi_ready, ONE + T + 1)
                    nc.vector.scalar_tensor_tensor(out=w_lo[T % 2][:, :, :], in0=wst[T % 2][:, :, :], scalar=WS,
                                                   in1=w_hi[T % 2][:, :, :], op0=ALU.mult,
                                                   op1=ALU.subtract).then_inc(lo_ready, 1)

                dve.wait_ge(const_in, ONE + 32)
                nc.vector.tensor_scalar(half[:, :], chan[:, :], 0.5, None, ALU.mult).then_inc(prep, 1)
                nc.vector.tensor_scalar(rest[:, :], chan[:, :], -1.0, 1.0, ALU.mult, ALU.add).then_inc(prep, 1)
                split_lo(0)
                for n, (lo, st, hi) in enumerate(((lw_lo[:, :, :], lst[:, :, :], lw_hi[:, :, :]),
                                                  (lg_lo[:, 0, :], gst[:, 0, :], lg_hi[:, 0, :]),
                                                  (lg_lo[0:GR, 1, :], gst[0:GR, 1, :], lg_hi[0:GR, 1, :]))):
                    dve.wait_ge(lsplit_hi, ONE + n + 1)
                    nc.vector.scalar_tensor_tensor(out=lo, in0=st, scalar=WS, in1=hi, op0=ALU.mult,
                                                   op1=ALU.subtract).then_inc(lsplit_lo, 1)
                dve.wait_ge(prep, ONE + 6)
                for T in range(3):
                    split_lo(T + 1)
                    rows = P if T < T_G1 else GR
                    mu = MU_WA + T
                    dve.wait_ge(act_left, ONE + NB * (T + 1))
                    if T >= 1:
                        dve.wait_ge(act_own, ONE + T + 1)
                    own.link(nc.vector.tensor_tensor(tmp[0:rows, 1:S + 1], raw[0:rows, 0:S], raw[0:rows, 2:S + 2], ALU.add))
                    own.link(nc.vector.tensor_scalar(tmp[0:rows, 1:S + 1], tmp[0:rows, 1:S + 1],
                                                     half[0:rows, mu:mu + 1], None, ALU.mult))
                    own.link(nc.vector.scalar_tensor_tensor(
                        out=tmp[0:rows, 1:S + 1], in0=raw[0:rows, 1:S + 1], scalar=rest[0:rows, mu:mu + 1],
                        in1=tmp[0:rows, 1:S + 1], op0=ALU.mult, op1=ALU.add))
                    nc.vector.sem_inc(raw_free, 1)
                    nc.vector.sem_inc(shifted, 1)
                    dve.wait_ge(bent, ONE + T + 1)
                    lo, hi = (xwa_lo[:, :], xwa_hi[:, :]) if T == T_WA else (sg_lo[0:rows, T - 1, :], sg_hi[0:rows, T - 1, :])
                    nc.vector.tensor_tensor(lo, act_t[0:rows, :], hi, ALU.subtract).then_inc(bent_lo, 1)

            @block.tensor
            def _(pe):
                def free_wait(n):
                    if n >= 6:
                        pe.wait_ge(act_left, ONE + n - 5)

                for T in range(3):
                    pe.wait_ge(hi_ready, ONE + T + 1)
                    pe.wait_ge(lo_ready, ONE + T + 1)
                    for b in range(NB):
                        free_wait(NB * T + b)
                        big_block(pe, T % 2, NB * T + b, b)
                pe.wait_ge(bent_lo, ONE + 3)
                pe.wait_ge(lsplit_lo, ONE + 3)
                for hp in range(HP):
                    ch = slice(P * hp, P * hp + P)
                    for b in range(NB):
                        n = NB * hp + b
                        tok = slice(512 * b, 512 * b + 512)
                        if n >= 2:
                            pe.wait_ge(sm_act, ONE + n - 1)
                        for g, rows in ((0, P), (1, GR)):
                            for lw, sgt in ((lg_hi, sg_hi), (lg_hi, sg_lo), (lg_lo, sg_hi)):
                                ins = nc.tensor.matmul(small[n % 2][:, :], lw[0:rows, g, ch], sgt[0:rows, g, tok],
                                                       start=(g == 0 and lw is lg_hi and sgt is sg_hi),
                                                       stop=(g == 1 and lw is lg_lo))
                        ins.then_inc(sm_done, 1)

        with ExitStack() as st2:
            s2 = Scope(nc, st2, "ip1")
            R, K, V, KK = (s2.sb(n, [P, S]) for n in ("R", "K", "V", "KK"))
            sg = [s2.sb(f"s{x}", [P, 512]) for x in range(2)]
            cum = [s2.sb(f"cum{x}", [P, 512]) for x in range(2)]
            rate = [s2.sb(f"rate{x}", [P, 512]) for x in range(2)]
            kd = [s2.sb(f"kd{x}", [P, 512]) for x in range(2)]
            bb = [s2.sb(f"bb{x}", [P, 512]) for x in range(2)]
            keep = s2.sb("keep", [P, 512], F16)
            r_st, kk_st, v_st = s2.sem("r_st"), s2.sem("kk_st"), s2.sem("v_st")
            r_ready, v_ready, kk_ready = s2.sem("r_ready"), s2.sem("v_ready"), s2.sem("kk_ready")
            kraw_ready, sq_ready = s2.sem("kraw_ready"), s2.sem("sq_ready")
            cum_ready, kd_ready, bb_ready = s2.sem("cum_ready"), s2.sem("kd_ready"), s2.sem("bb_ready")
            cum_st, kd_st, bb_st = ([s2.sem(f"{n}_st{x}") for x in range(2)] for n in ("cum", "kd", "bb"))
            sg_read, rate_read = s2.sem("sg_read"), s2.sem("rate_read")
            q_ready, bonus_ready = s2.sem("q_ready"), s2.sem("bonus_ready")
            bonus_st = s2.sem("bonus_st")
            conv_free = s2.sem("conv_free")
            o_ready, o_hi = s2.sem("o_ready"), s2.sem("o_hi")
            tmp_read = s2.sem("tmp_read")
            keep_in = s2.sem("keep_in")
            block = st2.enter_context(nc.Block())
            nt = len(TILES)
            DVE_STEPS = 76

            @block.sync
            def _(sp):
                s2.start_at_one(sp)
                sp.dma_start(keep[:, :], d["keep"]).then_inc(keep_in, 16)
                with sp.Fori(0, HP) as i:
                    def load(m):
                        T = T_LOOP + 1 + m + nt * i
                        s = (T_LOOP + 1 + m) % 2
                        sp.wait_ge(hi_ready, ONE + T - 1)
                        sp.wait_ge(lo_ready, ONE + T - 1)
                        sp.dma_start(wst[s][:, :, :], d["w_in"][T]).then_inc(w_in[s], 16)

                    load(0)
                    load(1)
                    load(2)
                    sp.wait_ge(r_ready, ONE + i + 1)
                    sp.dma_start(d["s_r"][i], R[:, :]).then_inc(r_st, 16)
                    load(3)
                    load(4)
                    sp.wait_ge(kk_ready, ONE + i + 1)
                    sp.dma_start(d["s_kk"][i], KK[:, :]).then_inc(kk_st, 16)
                    sp.wait_ge(v_ready, ONE + i + 1)
                    sp.dma_start(d["s_v"][i], V[:, :]).then_inc(v_st, 16)
                    load(5)
                    for b in range(NB):
                        tok = slice(512 * b, 512 * b + 512)
                        for x in range(2):
                            n = 2 * NB * i + 2 * b + x + 1
                            sp.wait_ge(cum_ready, ONE + n)
                            sp.dma_start(d["s_cum"][x, i][:, tok], cum[x][:, :]).then_inc(cum_st[x], 16)
                            sp.wait_ge(kd_ready, ONE + n)
                            sp.dma_start(d["s_kd"][x, i][:, tok], kd[x][:, :]).then_inc(kd_st[x], 16)
                            sp.wait_ge(bb_ready, ONE + n)
                            sp.dma_start(d["s_b"][x, i][:, tok], bb[x][:, :]).then_inc(bb_st[x], 16)
                    sp.wait_ge(bonus_ready, ONE + i + 1)
                    sp.dma_start(d["s_bonus"][i], V[:, :]).then_inc(bonus_st, 16)
                for sem in (r_st, v_st, kk_st, bonus_st):
                    sp.wait_ge(sem, ONE + 16 * HP)
                for sem in (*cum_st, *kd_st, *bb_st):
                    sp.wait_ge(sem, ONE + 16 * HP * NB)

            @block.scalar
            def _(act):
                with act.Fori(0, HP) as i:
                    def split_hi(m):
                        s = (T_LOOP + 1 + m) % 2
                        act.wait_ge(w_in[s], ONE + 16 * ((T_LOOP + 1 + m) // 2 + 1) + 16 * (nt // 2) * i)
                        act.wait_ge(blk_done, ONE + NB * (T_LOOP + m + nt * i))
                        nc.scalar.activation(w_hi[s][:, :, :], wst[s][:, :, :], ACT.Copy,
                                             scale=WS).then_inc(hi_ready, 1)

                    for m, name in enumerate(TILES):
                        T = T_LOOP + 1 + m + nt * i
                        if name != "h":
                            split_hi(m)
                        if name in "rkv":
                            if name == "r":
                                act.wait_ge(sm_dve, ONE + NB * i + NB)
                            act.wait_ge(raw_free, ONE + 3 + 3 * i + m)
                        if name == "c":
                            act.wait_ge(conv_free, ONE + i)
                        if name in "rkvc":
                            for b in range(NB):
                                dst = Cb[:, 512 * b:512 * b + 512] if name == "c" else raw[:, 1 + 512 * b:513 + 512 * b]
                                act.wait_ge(blk_done, ONE + NB * (T - 1) + b + 1)
                                nc.scalar.activation(dst, ring[(NB * m + b) % 6][:, :], ACT.Copy,
                                                     scale=1 / WS).then_inc(act_left, 1)
                        if name == "k":
                            act.wait_ge(kraw_ready, ONE + i + 1)
                            nc.scalar.activation(tmp[:, 1:S + 1], KK[:, :], ACT.Square).then_inc(sq_ready, 1)
                        if name == "v":
                            for b in range(NB):
                                act.wait_ge(sm_done, ONE + 4 * HP + 24 * i + b + 1)
                                nc.scalar.activation(tmp[:, 1 + 512 * b:513 + 512 * b], small[b % 2][:, :],
                                                     ACT.Sqrt).then_inc(sm_act, 1)
                        if name == "c":
                            split_hi(m + 1)
                            for b in range(NB):
                                for x in range(2):
                                    n = 2 * NB * i + 2 * b + x
                                    j = NB + 4 * b + 2 * x
                                    act.wait_ge(sg_read, ONE + n + 1)
                                    alone(act, sm_done, 4 * HP + 24 * i + j + 1)
                                    nc.scalar.activation(sg[x][:, :], small[j % 2][:, :], ACT.Sigmoid, scale=1 / WS,
                                                         bias=chan[:, bass.ds(i * NPC + W0_F + x, 1)]).then_inc(sm_act, 1)
                                    act.wait_ge(rate_read, ONE + n + 1)
                                    alone(act, sm_done, 4 * HP + 24 * i + j + 2)
                                    nc.scalar.activation(rate[x][:, :], small[(j + 1) % 2][:, :], ACT.Sigmoid, scale=1 / WS,
                                                         bias=chan[:, bass.ds(i * NPC + A0_F + x, 1)]).then_inc(sm_act, 1)
                        if name == "b":
                            for b in range(NB):
                                act.wait_ge(o_ready, ONE + NB * i + b + 1)
                                nc.scalar.activation(oc_hi[:, i, 512 * b:512 * b + 512], Cb[:, 512 * b:512 * b + 512],
                                                     ACT.Copy).then_inc(o_hi, 1)

            @block.vector
            def _(dve):
                dve.sem_inc(dve_left, 2 * NB)
                dve.sem_inc(sm_dve, NB)
                dve.sem_inc(sg_read, 2)
                dve.sem_inc(rate_read, 2)
                dve.wait_ge(keep_in, ONE + 16)
                with dve.Fori(0, HP) as i:
                    own = Chain(dve, dve_own, 9 + DVE_STEPS * i)

                    def col(arr, c):
                        return arr[:, bass.ds(i * NPC + c, 1)]

                    def split_lo(m):
                        s = (T_LOOP + 1 + m) % 2
                        dve.wait_ge(hi_ready, ONE + T_LOOP + 2 + m + nt * i)
                        nc.vector.scalar_tensor_tensor(out=w_lo[s][:, :, :], in0=wst[s][:, :, :], scalar=WS,
                                                       in1=w_hi[s][:, :, :], op0=ALU.mult,
                                                       op1=ALU.subtract).then_inc(lo_ready, 1)

                    def shift(m, dst, mu):
                        dve.wait_ge(act_left, ONE + 3 * NB + 4 * NB * i + NB * (m + 1))
                        own.link(nc.vector.tensor_tensor(tmp[:, 1:S + 1], raw[:, 0:S], raw[:, 2:S + 2], ALU.add))
                        own.link(nc.vector.tensor_scalar(dst[:, :], raw[:, 1:S + 1], col(rest, mu), None, ALU.mult))
                        nc.vector.sem_inc(raw_free, 1)
                        own.link(nc.vector.scalar_tensor_tensor(out=dst[:, :], in0=tmp[:, 1:S + 1], scalar=col(half, mu),
                                                                in1=dst[:, :], op0=ALU.mult, op1=ALU.add))

                    split_lo(0)
                    dve.wait_ge(r_st, ONE + 16 * i)
                    shift(0, R, MU_R)
                    nc.vector.sem_inc(r_ready, 1)
                    split_lo(1)
                    shift(1, K, MU_K)
                    dve.wait_ge(kk_st, ONE + 16 * i)
                    own.link(nc.vector.tensor_scalar(KK[:, :], K[:, :], col(chan, K_K), None, ALU.mult))
                    nc.vector.sem_inc(kraw_ready, 1)
                    split_lo(2)
                    dve.wait_ge(bonus_st, ONE + 16 * i)
                    dve.wait_ge(sm_act, ONE + 4 * HP + 20 * i + NB)
                    own.link(nc.vector.tensor_scalar(tmp[:, 1:S + 1], tmp[:, 1:S + 1], NORM_EPS, None, ALU.max))
                    own.link(nc.vector.reciprocal(tmp[:, 1:S + 1], tmp[:, 1:S + 1]))
                    own.link(nc.vector.tensor_tensor(KK[:, :], KK[:, :], tmp[:, 1:S + 1], ALU.mult))
                    nc.vector.sem_inc(kk_ready, 1)
                    shift(2, V, MU_V)
                    nc.vector.sem_inc(v_ready, 1)
                    split_lo(3)
                    split_lo(4)
                    for b in range(NB):
                        tok = slice(512 * b, 512 * b + 512)
                        ptok = slice(1 + 512 * b, 513 + 512 * b)
                        for x in range(2):
                            n = 2 * NB * i + 2 * b + x
                            j = NB + 4 * b + 2 * x
                            dve.wait_ge(cum_st[x], ONE + 16 * (NB * i + b))
                            dve.wait_ge(sm_act, ONE + 4 * HP + 20 * i + j + 1)
                            way = slice(None, None, -1) if x else slice(None)
                            own.link(nc.vector.tensor_tensor_scan(
                                out=cum[x][:, way], data0=keep[:, :], data1=sg[x][:, way],
                                initial=0.0, op0=ALU.mult, op1=ALU.add))
                            nc.vector.sem_inc(cum_ready, 1)
                            nc.vector.sem_inc(sg_read, 1)
                            dve.wait_ge(sm_act, ONE + 4 * HP + 20 * i + j + 2)
                            dve.wait_ge(kd_st[x], ONE + 16 * (NB * i + b))
                            own.link(nc.vector.tensor_scalar(kd[x][:, :], rate[x][:, :], col(chan, KA_F + x),
                                                             col(rest, KA_F + x), ALU.mult, ALU.add))
                            own.link(nc.vector.tensor_tensor(kd[x][:, :], kd[x][:, :], K[:, tok], ALU.mult))
                            nc.vector.sem_inc(kd_ready, 1)
                            dve.wait_ge(bb_st[x], ONE + 16 * (NB * i + b))
                            own.link(nc.vector.tensor_tensor(bb[x][:, :], KK[:, tok], rate[x][:, :], ALU.mult))
                            nc.vector.sem_inc(bb_ready, 1)
                            nc.vector.sem_inc(rate_read, 1)
                            if x == 0:
                                own.link(nc.vector.tensor_scalar(Q[:, ptok], kd[x][:, :], col(chan, RK_F), None, ALU.mult))
                            else:
                                own.link(nc.vector.scalar_tensor_tensor(
                                    out=Q[:, ptok], in0=kd[x][:, :], scalar=col(chan, RK_B), in1=Q[:, ptok],
                                    op0=ALU.mult, op1=ALU.add))
                        own.link(nc.vector.tensor_tensor(Q[:, ptok], Q[:, ptok], R[:, tok], ALU.mult))
                        nc.vector.sem_inc(q_ready, 1)
                        dve.wait_ge(blk_done, ONE + NB * (T_LOOP + nt * i + 4) + b + 1)
                        dve.wait_ge(act_left, ONE + 3 * NB + 4 * NB * i + 3 * NB + b + 1)
                        own.link(nc.vector.scalar_tensor_tensor(
                            out=tmp[:, ptok], in0=ring[(NB * 4 + b) % 6][:, :], scalar=1 / WS, in1=Cb[:, tok],
                            op0=ALU.mult, op1=ALU.mult))
                        nc.vector.sem_inc(dve_left, 1)
                    split_lo(5)
                    own.link(nc.vector.tensor_scalar(Cb[:, :], tmp[:, 0:S], col(chan, CW0), None, ALU.mult))
                    for t in (1, 2):
                        own.link(nc.vector.scalar_tensor_tensor(out=Cb[:, :], in0=tmp[:, t:S + t], scalar=col(chan, CW0 + t),
                                                                in1=Cb[:, :], op0=ALU.mult, op1=ALU.add))
                    for b in range(NB):
                        tok = slice(512 * b, 512 * b + 512)
                        dve.wait_ge(blk_done, ONE + NB * (T_LOOP + nt * i + 5) + b + 1)
                        own.link(nc.vector.scalar_tensor_tensor(
                            out=Cb[:, tok], in0=ring[(NB * 5 + b) % 6][:, :], scalar=1 / WS, in1=Cb[:, tok],
                            op0=ALU.mult, op1=ALU.mult))
                        nc.vector.sem_inc(dve_left, 1)
                        nc.vector.sem_inc(o_ready, 1)
                    for b in range(NB):
                        tok = slice(512 * b, 512 * b + 512)
                        dve.wait_ge(o_hi, ONE + NB * i + b + 1)
                        own.link(nc.vector.tensor_tensor(oc_lo[:, i, tok], Cb[:, tok], oc_hi[:, i, tok], ALU.subtract))
                    nc.vector.sem_inc(conv_free, 1)
                    dve.wait_ge(v_st, ONE + 16 * i + 16)
                    for b in range(NB):
                        tok = slice(512 * b, 512 * b + 512)
                        dve.wait_ge(sm_done, ONE + 4 * HP + 24 * i + 20 + b + 1)
                        own.link(nc.vector.tensor_tensor(V[:, tok], V[:, tok], small[b % 2][:, :], ALU.mult))
                        nc.vector.sem_inc(sm_dve, 1)
                    nc.vector.sem_inc(bonus_ready, 1)
                    assert own.n == DVE_STEPS

            @block.tensor
            def _(pe):
                pe.wait_ge(act_left, ONE + 3 * NB)
                pe.wait_ge(sm_act, ONE + 4 * HP)
                with pe.Fori(0, HP) as i:
                    def ring_free(n):
                        q = n - 6
                        if q < 0:
                            pe.wait_ge(dve_left, ONE + 2 * NB * i + 2 * NB + q + 1)
                        elif q < 4 * NB:
                            pe.wait_ge(act_left, ONE + 3 * NB + 4 * NB * i + q + 1)
                        else:
                            pe.wait_ge(dve_left, ONE + 2 * NB * i + 2 * NB + q - 4 * NB + 1)

                    def small_free(j):
                        q = j - 2
                        if q < 0:
                            pe.wait_ge(sm_dve, ONE + NB * i + NB + q + 1)
                        elif q < 20:
                            pe.wait_ge(sm_act, ONE + 4 * HP + 20 * i + q + 1)
                        else:
                            pe.wait_ge(sm_dve, ONE + NB * i + NB + q - 20 + 1)

                    def lora(b):
                        tok = slice(512 * b, 512 * b + 512)
                        for x in range(2):
                            for kind in range(2):
                                j = NB + 4 * b + 2 * x + kind
                                small_free(j)
                                for lw, xt in ((lw_hi, xwa_hi), (lw_hi, xwa_lo), (lw_lo, xwa_hi)):
                                    ins = nc.tensor.matmul(
                                        small[j % 2][:, :], lw[:, 2 * kind + x, bass.ds(i * P, P)], xt[:, tok],
                                        start=(lw is lw_hi and xt is xwa_hi), stop=lw is lw_lo)
                                ins.then_inc(sm_done, 1)

                    for m, name in enumerate(TILES):
                        pe.wait_ge(hi_ready, ONE + T_LOOP + m + nt * i + 1)
                        pe.wait_ge(lo_ready, ONE + T_LOOP + m + nt * i + 1)
                        for b in range(NB):
                            if name == "h":
                                lora(b)
                            ring_free(NB * m + b)
                            big_block(pe, (T_LOOP + m) % 2, NB * m + b, b)
                        if name == "v":
                            pe.wait_ge(sq_ready, ONE + i + 1)
                            for b in range(NB):
                                small_free(b)
                                nc.tensor.matmul(small[b % 2][:, :], ones[:, :], tmp[:, 1 + 512 * b:513 + 512 * b],
                                                 start=True, stop=True).then_inc(sm_done, 1)
                        if name == "b":
                            for b in range(NB):
                                j = 20 + b
                                small_free(j)
                                pe.wait_ge(q_ready, ONE + NB * i + b + 1)
                                nc.tensor.matmul(small[j % 2][:, :], ones[:, :], Q[:, 1 + 512 * b:513 + 512 * b],
                                                 start=True, stop=True).then_inc(sm_done, 1)


def phase_scan(nc, d, y):
    with ExitStack() as stack:
        sc = Scope(nc, stack, "scan")
        NA, UN = 6, HP
        A_R, A_KK, A_V, A_CUM, A_KD, A_B = range(NA)
        LV = 6
        win = [sc.sb(f"win{w}", [P, NA, 2, UN, 2 * C]) for w in range(2)]

        def pair(name, shape, dt=F32):
            return [sc.sb(f"{name}{x}", shape, dt) for x in range(2)]

        def quad(name, shape, dt=F32):
            return [pair(f"{name}{q}_", shape, dt) for q in range(2)]

        E = pair("E", [P, UN, C + 1])
        Ei = pair("Ei", [P, UN, C])
        bs, ks = pair("bs", [P, UN, C]), pair("ks", [P, UN, C])
        bh, kh = pair("bh", [P, UN, C]), pair("kh", [P, UN, C])
        bbd, kbd = pair("bbd", [P, UN, P]), pair("kbd", [P, UN, P])
        Nh, Nl = pair("Nh", [P, UN, P], F16), pair("Nl", [P, UN, P], F16)
        X, Xbd = pair("X", [P, UN, C], F16), pair("Xbd", [P, UN, P], F16)
        GV, Vbd = pair("GV", [P, 2, UN, C], F16), pair("Vbd", [P, UN, P], F16)
        SL, Xs, Us = pair("SL", [P, UN, C]), pair("Xs", [P, UN, C]), pair("Us", [P, UN, C])
        kkr = quad("kkr", [P, UN, 2, C])
        Bt, Kt, Vt = quad("Bt", [P, UN, C]), quad("Kt", [P, UN, C]), quad("Vt", [P, UN, C])
        AB, AK = quad("AB", [P, UN, 2, C]), quad("AK", [P, UN, 2, C])
        TI = quad("TI", [P, UN, C])
        St = quad("St", [P, UN, C])
        lam = quad("lam", [P, UN, 1])
        idn = sc.sb("ident", [P, P])
        idh = sc.sb("identh", [P, P], F16)
        ids = sc.sb("idents", [P, C], F16)
        mA = sc.sb("maskA", [P, 2, 2, C])
        mL = sc.sb("maskL", [P, 2, LV, C])
        ring = [sc.ps(f"ring{n}") for n in range(2)]
        px = [sc.ps(f"px{x}", (P, UN, C)) for x in range(2)]
        pg = [sc.ps(f"pg{x}", (P, 2, UN, C)) for x in range(2)]
        pq = [sc.ps(f"pq{x}", (P, UN, C)) for x in range(2)]

        const_in, zeroed, dve_own = sc.sem("const_in"), sc.sem("zeroed"), sc.sem("dve_own")
        win_in = [sc.sem(f"win_in{w}") for w in range(2)]
        exps, prods, bds = sc.sem("exps"), sc.sem("prods"), sc.sem("bds")
        turned, t_left = sc.sem("turned"), sc.sem("t_left")
        a_done, a_left = sc.sem("a_done"), sc.sem("a_left")
        nh_done, nl_done = sc.sem("nh_done"), sc.sem("nl_done")
        x_done, x_left, xbd_done = sc.sem("x_done"), sc.sem("x_left"), sc.sem("xbd_done")
        gv_done, gv_left, vbd_done = sc.sem("gv_done"), sc.sem("gv_left"), sc.sem("vbd_done")
        res_done, res_left, rbd_done = sc.sem("res_done"), sc.sem("res_left"), sc.sem("rbd_done")
        dv_done, inv_done = sc.sem("dv_done"), sc.sem("inv_done")
        sx_done, sx_left = sc.sem("sx_done"), sc.sem("sx_left")
        su_done, su_left = sc.sem("su_done"), sc.sem("su_left")
        ss_done, ss_left = sc.sem("ss_done"), sc.sem("ss_left")
        sy_done, sy_left = sc.sem("sy_done"), sc.sem("sy_left")
        N_CONST, N_ZERO = 5, 30
        heads = (slice(0, C), slice(C, P))
        block = stack.enter_context(nc.Block())

        def steps(eng, step, last_run):
            with eng.Fori(0, NCH // 4) as i:
                for s in range(4):
                    step(4 * i + s, s, i)
            last_run(NCH)

        def cols(s, x):
            q = s % 2
            return slice(C * q, C * q + C) if x == 0 else slice(C * (1 - q), C * (1 - q) + C)

        @block.sync
        def _(sp):
            sc.start_at_one(sp)
            for dst, src in ((idn, "ident"), (idh, "identh"), (ids, "idents"), (mA, "maskA"), (mL, "maskL")):
                sp.dma_start(dst[tuple(slice(None) for _ in dst.shape)], d[src]).then_inc(const_in, 16)

            def load(w, it):
                for x, tok in ((0, it * (2 * C)), (1, S - 2 * C - it * (2 * C))):
                    at = bass.ds(tok, 2 * C)
                    for a, src in ((A_R, d["s_r"]), (A_KK, d["s_kk"]), (A_V, d["s_v"]), (A_CUM, d["s_cum"][x]),
                                   (A_KD, d["s_kd"][x]), (A_B, d["s_b"][x])):
                        sp.dma_start(win[w][:, a, x, :, :],
                                     src.rearrange("h p t -> p h t")[:, :, at]).then_inc(win_in[w], 16)

            for w in range(2):
                load(w, w)
            with sp.Fori(1, NCH // 4) as i:
                for w in range(2):
                    done = 4 * i + 2 * w - 2
                    alone(sp, exps, 4 * done)
                    alone(sp, prods, 14 * done)
                    alone(sp, turned, 6 * done)
                    load(w, 2 * i + w)

        @block.gpsimd
        def _(pool):
            n = 0
            for t in (bbd[0], bbd[1], kbd[0], kbd[1], Nh[0], Nh[1], Nl[0], Nl[1], Xbd[0], Xbd[1], Vbd[0], Vbd[1],
                      kkr[1][0], kkr[1][1], Bt[1][0], Bt[1][1], Kt[1][0], Kt[1][1], Vt[1][0], Vt[1][1],
                      TI[1][0], TI[1][1], St[1][0], St[1][1], lam[1][0], lam[1][1],
                      AB[1][0], AB[1][1], AK[1][0], AK[1][1]):
                nc.gpsimd.memset(t[tuple(slice(None) for _ in t.shape)], 0.0).then_inc(zeroed, 1)
                n += 1
            assert n == N_ZERO
            for x in range(2):
                one = 0 if x == 0 else C
                nc.gpsimd.memset(E[x][:, :, one:one + 1], 1.0).then_inc(zeroed, 1)
            for u in range(UN):
                nc.gpsimd.memset(y[:, u, :], 0.0).then_inc(zeroed, 1)

        @block.scalar
        def _(act):
            act.wait_ge(zeroed, ONE + N_ZERO + 2 + UN)

            def run_x(cs):
                for x in range(2):
                    act.wait_ge(sx_done, ONE + 2 * cs + x + 1)
                    nc.scalar.activation(Xs[x][:, :, :], pq[x][:, :, :], ACT.Copy, scale=-1.0).then_inc(sx_left, 1)

            def run_u(cs):
                for x in range(2):
                    act.wait_ge(su_done, ONE + 2 * cs + x + 1)
                    nc.scalar.activation(Us[x][:, :, :], pq[x][:, :, :], ACT.Copy).then_inc(su_left, 1)

            def step(cs, s, i):
                w, par = s // 2, s % 2
                if s % 2 == 0:
                    act.wait_ge(win_in[w], ONE + 16 * 2 * NA * (i + 1))
                act.wait_ge(prods, ONE + 14 * cs)
                for x in range(2):
                    at = slice(1, C + 1) if x == 0 else slice(0, C)
                    src = win[w][:, A_CUM, x, :, cols(s, x)]
                    nc.scalar.activation(E[x][:, :, at], src, ACT.Exp, scale=-DECAY).then_inc(exps, 1)
                    nc.scalar.activation(Ei[x][:, :, :], src, ACT.Exp, scale=DECAY).then_inc(exps, 1)
                act.wait_ge(a_done, ONE + 4 * cs)
                for x in range(2):
                    for m, (dst, src) in enumerate(((bbd[x], bs[x]), (kbd[x], ks[x]))):
                        act.wait_ge(prods, ONE + 14 * cs + 7 * x + 3 + m)
                        for h, hs in enumerate(heads):
                            nc.scalar.activation(dst[hs, :, C * h:C * h + C], src[hs, :, :], ACT.Copy).then_inc(bds, 1)
                run_x(cs)
                act.wait_ge(sy_done, ONE + 2 * cs)
                for x in range(2):
                    for m, dst in enumerate((Bt[par][x], Kt[par][x], Vt[par][x])):
                        act.wait_ge(turned, ONE + 6 * cs + 3 * x + m + 1)
                        src = ring[(5 * x + m) % 2][0:C, :].rearrange("p (u k) -> p u k", u=UN)
                        for h, hs in enumerate(heads):
                            ins = nc.scalar.activation(dst[hs, :, :], src[:, :, C * h:C * h + C], ACT.Copy)
                            ins.then_inc(t_left, 1)
                act.wait_ge(res_done, ONE + 2 * cs)
                for x in range(2):
                    act.wait_ge(a_left, ONE + 4 + 4 * cs + 2 * x + 1)
                    for h, hs in enumerate(heads):
                        nc.scalar.activation(Nh[x][hs, :, C * h:C * h + C], AB[par][x][hs, :, 0, :],
                                             ACT.Copy).then_inc(nh_done, 1)
                run_u(cs)
                for l in range(LV):
                    for x in range(2):
                        act.wait_ge(gv_done, ONE + 12 * cs + 2 * l + x + 1)
                        nc.scalar.activation(GV[x][:, :, :, :], pg[x][:, :, :, :], ACT.Copy).then_inc(gv_left, 1)

            def last_run(cs):
                run_x(cs)
                run_u(cs)

            steps(act, step, last_run)

        @block.vector
        def _(dve):
            dve.sem_inc(a_left, 4)
            dve.wait_ge(zeroed, ONE + N_ZERO + 2 + UN)
            dve.wait_ge(const_in, ONE + 16 * N_CONST)

            def run_s(cs, par, own):
                for x in range(2):
                    own.link(nc.vector.tensor_tensor(SL[x][:, :, :], St[1 - par][x][:, :, :],
                                                     lam[1 - par][x][:, :, :].broadcast_to((P, UN, C)), ALU.mult))
                    dve.wait_ge(ss_done, ONE + 2 * cs + x + 1)
                    nc.vector.tensor_tensor(St[par][x][:, :, :], SL[x][:, :, :], pq[x][:, :, :], ALU.add).then_inc(ss_left, 1)

            def run_y(cs, x):
                at = bass.ds(cs * C, C) if x == 0 else bass.ds((NCH + 1) * C - cs * C, C)
                alone(dve, sy_done, 2 * cs + x + 1)
                alone(dve, sy_left, 2 * cs + x)
                nc.vector.tensor_tensor(y[:, :, at], y[:, :, at], pq[x][:, :, :], ALU.add).then_inc(sy_left, 1)

            def step(cs, s, i):
                w, par = s // 2, s % 2
                own = Chain(dve, dve_own, 2 * cs)
                alone(dve, sy_done, 2 * cs)
                alone(dve, bds, 8 * cs)
                alone(dve, turned, 6 * cs)
                if s % 2 == 0:
                    dve.wait_ge(win_in[w], ONE + 16 * 2 * NA * (i + 1))
                for x in range(2):
                    c = cols(s, x)
                    now, past, end = ((slice(1, C + 1), slice(0, C), C) if x == 0 else
                                      (slice(0, C), slice(1, C + 1), 0))
                    g = win[w]
                    dve.wait_ge(exps, ONE + 4 * cs + 2 * x + 2)
                    nc.vector.tensor_tensor(kkr[par][x][:, :, 0, :], g[:, A_KK, x, :, c], E[x][:, :, past],
                                            ALU.mult).then_inc(prods, 1)
                    nc.vector.tensor_tensor(kkr[par][x][:, :, 1, :], g[:, A_R, x, :, c], E[x][:, :, now],
                                            ALU.mult).then_inc(prods, 1)
                    nc.vector.tensor_tensor(bs[x][:, :, :], g[:, A_B, x, :, c], Ei[x][:, :, :], ALU.mult).then_inc(prods, 1)
                    nc.vector.tensor_tensor(ks[x][:, :, :], g[:, A_KD, x, :, c], Ei[x][:, :, :], ALU.mult).then_inc(prods, 1)
                    nc.vector.tensor_copy(lam[par][x][:, :, :], E[x][:, :, end:end + 1]).then_inc(prods, 1)
                    dve.wait_ge(prods, ONE + 14 * cs + 7 * x + 5)
                    lb = lam[par][x][:, :, :].broadcast_to((P, UN, C))
                    nc.vector.tensor_tensor(bh[x][:, :, :], bs[x][:, :, :], lb, ALU.mult).then_inc(prods, 1)
                    nc.vector.tensor_tensor(kh[x][:, :, :], ks[x][:, :, :], lb, ALU.mult).then_inc(prods, 1)
                for x in range(2):
                    mask = mA[:, x:x + 1, :, :].rearrange("p o a b -> p o (a b)").broadcast_to((P, UN, 2 * C))
                    for m, dst in enumerate((AB[par][x], AK[par][x])):
                        dve.wait_ge(a_done, ONE + 4 * cs + 2 * x + m + 1)
                        nc.vector.tensor_tensor(dst[:, :, :, :].rearrange("p u a b -> p u (a b)"),
                                                ring[(5 * x + 3 + m) % 2][:, :].rearrange("p (u k) -> p u k", u=UN),
                                                mask, ALU.mult).then_inc(a_left, 1)

                def spread(dst, src, sem):
                    for h, hs in enumerate(heads):
                        nc.vector.tensor_copy(dst[hs, :, C * h:C * h + C], src[hs]).then_inc(sem, 1)

                def level(l):
                    for x in range(2):
                        if l:
                            dve.wait_ge(gv_left, ONE + 12 * cs + 2 * (l - 1) + x + 1)
                            spread(Vbd[x], GV[x][:, 1, :, :], vbd_done)
                    for x in range(2):
                        dve.wait_ge(x_done, ONE + 12 * cs + 2 * l + x + 1)
                        nc.vector.tensor_tensor(X[x][:, :, :], px[x][:, :, :],
                                                mL[:, x, l:l + 1, :].broadcast_to((P, UN, C)), ALU.mult).then_inc(x_left, 1)
                    for x in range(2):
                        dve.wait_ge(x_left, ONE + 12 * cs + 2 * l + x + 1)
                        spread(Xbd[x], X[x], xbd_done)

                level(0)
                for x in range(2):
                    for h, hs in enumerate(heads):
                        dve.wait_ge(nh_done, ONE + 4 * cs + 2 * x + h + 1)
                        nc.vector.tensor_tensor(Nl[x][hs, :, C * h:C * h + C], AB[par][x][hs, :, 0, :],
                                                Nh[x][hs, :, C * h:C * h + C], ALU.subtract).then_inc(nl_done, 1)
                run_s(cs, par, own)
                level(1)
                run_y(cs, 0)
                level(2)
                run_y(cs, 1)
                for l in range(3, LV):
                    level(l)
                for x in range(2):
                    dve.wait_ge(res_done, ONE + 2 * cs + x + 1)
                    nc.vector.tensor_tensor(X[x][:, :, :], ids[:, :].unsqueeze(1).broadcast_to((P, UN, C)),
                                            px[x][:, :, :], ALU.subtract).then_inc(res_left, 1)
                for x in range(2):
                    dve.wait_ge(res_left, ONE + 2 * cs + x + 1)
                    spread(Xbd[x], X[x], rbd_done)
                for x in range(2):
                    dve.wait_ge(dv_done, ONE + 2 * cs + x + 1)
                    nc.vector.tensor_tensor(TI[par][x][:, :, :], GV[x][:, 1, :, :], pg[x][:, 0, :, :],
                                            ALU.add).then_inc(inv_done, 1)

            def last_run(cs):
                run_s(cs, 0, Chain(dve, dve_own, 2 * cs))
                run_y(cs, 0)
                run_y(cs, 1)

            steps(dve, step, last_run)
            dve.wait_ge(sy_left, ONE + 2 * NCH + 2)

        @block.tensor
        def _(pe):
            pe.wait_ge(zeroed, ONE + N_ZERO + 2 + UN)
            pe.wait_ge(const_in, ONE + 16 * N_CONST)

            def by_head(out, terms, sem):
                for u in range(UN):
                    for hs in heads:
                        for n, (l, r) in enumerate(terms):
                            ins = nc.tensor.matmul(out[hs, u, :], l(hs, u), r(hs, u), start=n == 0,
                                                   stop=n == len(terms) - 1)
                ins.then_inc(sem, 1)

            def run_x(cs, par):
                o = 1 - par
                alone(pe, ss_left, 2 * cs)
                alone(pe, prods, 14 * cs)
                alone(pe, a_left, 4 + 4 * cs)
                alone(pe, t_left, 12 * cs)
                alone(pe, sy_left, 2 * cs)
                for x in range(2):
                    by_head(pq[x], ((lambda hs, u: kkr[o][x][hs, u, 0, :], lambda hs, u: St[o][x][hs, u, :]),
                                    (lambda hs, u: AK[o][x][hs, u, 0, :], lambda hs, u: Vt[o][x][hs, u, :])), sx_done)

            def run_u(cs, par):
                o = 1 - par
                alone(pe, inv_done, 2 * cs)
                for x in range(2):
                    alone(pe, sx_left, 2 * cs + x + 1)
                    by_head(pq[x], ((lambda hs, u: TI[o][x][hs, u, :], lambda hs, u: Xs[x][hs, u, :]),), su_done)

            def run_s(cs, par):
                o = 1 - par
                for x in range(2):
                    alone(pe, su_left, 2 * cs + x + 1)
                    by_head(pq[x], ((lambda hs, u: Bt[o][x][hs, u, :], lambda hs, u: Us[x][hs, u, :]),
                                    (lambda hs, u: Kt[o][x][hs, u, :], lambda hs, u: Vt[o][x][hs, u, :])), ss_done)

            def run_y(cs, par, x):
                o = 1 - par
                alone(pe, ss_left, 2 * cs + x + 1)
                by_head(pq[x], ((lambda hs, u: St[o][x][hs, u, :], lambda hs, u: kkr[o][x][hs, u, 1, :]),
                                (lambda hs, u: Us[x][hs, u, :], lambda hs, u: AB[o][x][hs, u, 1, :]),
                                (lambda hs, u: Vt[o][x][hs, u, :], lambda hs, u: AK[o][x][hs, u, 1, :])), sy_done)

            def step(cs, s, i):
                w, par = s // 2, s % 2
                run_x(cs, par)
                frees = ((a_left, 4 * cs + 3), (a_left, 4 * cs + 4), (t_left, 12 * cs + 2), (t_left, 12 * cs + 4),
                         (t_left, 12 * cs + 6), (a_left, 4 * cs + 5), (a_left, 4 * cs + 6), (t_left, 12 * cs + 8),
                         (t_left, 12 * cs + 10), (t_left, 12 * cs + 12))
                for x in range(2):
                    alone(pe, prods, 14 * cs + 7 * x + 7)
                    for m in range(3):
                        alone(pe, *frees[5 * x + m])
                        for u in range(UN):
                            src = (bh[x][:, u, :], kh[x][:, u, :], win[w][:, A_V, x, u, cols(s, x)])[m]
                            ins = nc.tensor.transpose(ring[(5 * x + m) % 2][0:C, P * u:P * u + P], src, idn[:, :])
                        ins.then_inc(turned, 1)
                    for m, lhs in enumerate((bbd[x], kbd[x])):
                        alone(pe, bds, 8 * cs + 4 * x + 2 * m + 2)
                        alone(pe, *frees[5 * x + 3 + m])
                        for u in range(UN):
                            ins = nc.tensor.matmul(ring[(5 * x + 3 + m) % 2][:, P * u:P * u + P], lhs[:, u, :],
                                                   kkr[par][x][:, u, :, :], start=True, stop=True)
                        ins.then_inc(a_done, 1)
                run_u(cs, par)
                alone(pe, inv_done, 2 * cs)

                def level(l):
                    for x in range(2):
                        if l == 0:
                            alone(pe, nh_done, 4 * cs + 2 * x + 2)
                        else:
                            alone(pe, gv_left, 12 * cs + 2 * (l - 1) + x + 1)
                        for u in range(UN):
                            g = GV[x][:, 0, u, :] if l else ids[:, :]
                            ins = nc.tensor.matmul(px[x][:, u, :], Nh[x][:, u, :], g, start=True, stop=True)
                        ins.then_inc(x_done, 1)
                    if l == 0:
                        run_s(cs, par)
                    if l in (1, 2):
                        run_y(cs, par, l - 1)
                    for x in range(2):
                        alone(pe, xbd_done, 24 * cs + 4 * l + 2 * x + 2)
                        if l:
                            alone(pe, vbd_done, 20 * cs + 4 * (l - 1) + 2 * x + 2)
                        for u in range(UN):
                            for q in range(2):
                                old = GV[x][:, q, u, :] if l else ids[:, :]
                                vb = Vbd[x][:, u, :] if l else idh[:, :]
                                nc.tensor.matmul(pg[x][:, q, u, :], idh[:, :], old, start=True, stop=False)
                                ins = nc.tensor.matmul(pg[x][:, q, u, :], *((vb, X[x][:, u, :]) if q == 0 else
                                                                            (Xbd[x][:, u, :], old)),
                                                       start=False, stop=True)
                        ins.then_inc(gv_done, 1)

                for l in range(LV):
                    level(l)
                for x in range(2):
                    alone(pe, gv_left, 12 * cs + 2 * (LV - 1) + x + 1)
                    alone(pe, nl_done, 4 * cs + 2 * x + 2)
                    for u in range(UN):
                        for n, lhs in enumerate((Nh[x][:, u, :], Nl[x][:, u, :], idh[:, :])):
                            ins = nc.tensor.matmul(px[x][:, u, :], lhs, GV[x][:, 0, u, :], start=n == 0, stop=n == 2)
                    ins.then_inc(res_done, 1)
                for x in range(2):
                    alone(pe, rbd_done, 4 * cs + 2 * x + 2)
                    for u in range(UN):
                        ins = nc.tensor.matmul(pg[x][:, 0, u, :], Xbd[x][:, u, :], GV[x][:, 1, u, :], start=True, stop=True)
                    ins.then_inc(dv_done, 1)

            def last_run(cs):
                run_x(cs, 0)
                run_u(cs, 0)
                run_s(cs, 0)
                run_y(cs, 0, 0)
                run_y(cs, 0, 1)

            steps(pe, step, last_run)


def phase_groupnorm(nc, d, y, or_hi, or_lo):
    with ExitStack() as stack:
        sc = Scope(nc, stack, "gn")
        chan, ones = sc.sb("chan", [P, NCOL]), sc.sb("ones", [P, P])
        bon = [sc.sb(f"bon{n}", [P, 512]) for n in range(2)]
        gate = [sc.sb(f"gate{n}", [P, 512]) for n in range(2)]
        dev = [sc.sb(f"dev{n}", [P, 512]) for n in range(2)]
        sq = [sc.sb(f"sq{n}", [P, 512]) for n in range(2)]
        pm = [sc.ps(f"mean{n}") for n in range(2)]
        pv = [sc.ps(f"var{n}") for n in range(2)]
        const_in, ld = sc.sem("const_in"), [sc.sem(f"ld{n}") for n in range(2)]
        mean_done, dev_done, sq_done, var_done = (sc.sem(n) for n in ("mean_done", "dev_done", "sq_done", "var_done"))
        vs_done, rooted, o_done, hi_done, lo_done = (sc.sem(n) for n in ("vs_done", "rooted", "o_done", "hi_done", "lo_done"))
        dve_own = sc.sem("dve_own")
        block = stack.enter_context(nc.Block())

        def tok(i):
            return bass.ds(i * 512, 512)

        @block.sync
        def _(sp):
            sc.start_at_one(sp)
            sp.dma_start(chan[:, :], d["chan"]).then_inc(const_in, 16)
            sp.dma_start(ones[:, :], d["ones"]).then_inc(const_in, 16)
            for h in range(2):
                sp.dma_start(bon[h][:, :], d["s_bonus"][h, :, 0:512]).then_inc(ld[h], 16)
                sp.dma_start(gate[h][:, :], d["s_g"][h, :, 0:512]).then_inc(ld[h], 16)
            with sp.Fori(0, NB - 1) as i:
                for h in range(HP):
                    sp.wait_ge(o_done, ONE + HP * i + h + 1)
                    g, t = (h + 2, tok(i)) if h < 2 else (h - 2, tok(i + 1))
                    sp.dma_start(bon[h % 2][:, :], d["s_bonus"][g][:, t]).then_inc(ld[h % 2], 16)
                    sp.dma_start(gate[h % 2][:, :], d["s_g"][g][:, t]).then_inc(ld[h % 2], 16)
            for h in range(2):
                sp.wait_ge(o_done, ONE + HP * (NB - 1) + h + 1)
                sp.dma_start(bon[h][:, :], d["s_bonus"][h + 2, :, S - 512:S]).then_inc(ld[h], 16)
                sp.dma_start(gate[h][:, :], d["s_g"][h + 2, :, S - 512:S]).then_inc(ld[h], 16)

        @block.tensor
        def _(pe):
            pe.wait_ge(const_in, ONE + 32)
            with pe.Fori(0, NB) as i:
                for h in range(HP):
                    n = h % 2
                    pe.wait_ge(dev_done, ONE + (HP * i if h < 2 else HP * i + h - 1))
                    nc.tensor.matmul(pm[n][:, :], ones[:, :], y[:, h, bass.ds(i * 512 + C, 512)],
                                     start=True, stop=True).then_inc(mean_done, 1)
                    pe.wait_ge(vs_done, ONE + (HP * i if h < 2 else HP * i + h - 1))
                    pe.wait_ge(sq_done, ONE + HP * i + h + 1)
                    nc.tensor.matmul(pv[n][:, :], ones[:, :], sq[n][:, :], start=True, stop=True).then_inc(var_done, 1)

        @block.scalar
        def _(act):
            with act.Fori(0, NB) as i:
                for h in range(HP):
                    n = h % 2
                    act.wait_ge(dev_done, ONE + HP * i + h + 1)
                    nc.scalar.activation(sq[n][:, :], dev[n][:, :], ACT.Square).then_inc(sq_done, 1)
                    act.wait_ge(vs_done, ONE + HP * i + h + 1)
                    nc.scalar.activation(sq[n][:, :], sq[n][:, :], ACT.Sqrt).then_inc(rooted, 1)
                    act.wait_ge(o_done, ONE + HP * i + h + 1)
                    nc.scalar.activation(or_hi[:, h, tok(i)], dev[n][:, :], ACT.Copy).then_inc(hi_done, 1)

        @block.vector
        def _(dve):
            dve.wait_ge(const_in, ONE + 32)
            with dve.Fori(0, NB) as i:
                own = Chain(dve, dve_own, 6 * HP * i)
                for h in range(HP):
                    n = h % 2
                    dve.wait_ge(mean_done, ONE + HP * i + h + 1)
                    dve.wait_ge(lo_done, ONE + (HP * i if h < 2 else HP * i + h - 1))
                    nc.vector.scalar_tensor_tensor(out=dev[n][:, :], in0=pm[n][:, :], scalar=-1.0 / C,
                                                   in1=y[:, h, bass.ds(i * 512 + C, 512)], op0=ALU.mult,
                                                   op1=ALU.add).then_inc(dev_done, 1)
                    dve.wait_ge(var_done, ONE + HP * i + h + 1)
                    nc.vector.tensor_scalar(sq[n][:, :], pv[n][:, :], 1.0 / C, GN_EPS, ALU.mult, ALU.add).then_inc(vs_done, 1)
                    dve.wait_ge(rooted, ONE + HP * i + h + 1)
                    own.link(nc.vector.reciprocal(sq[n][:, :], sq[n][:, :]))
                    own.link(nc.vector.tensor_tensor(dev[n][:, :], dev[n][:, :], sq[n][:, :], ALU.mult))
                    own.link(nc.vector.tensor_scalar(dev[n][:, :], dev[n][:, :], chan[:, h * NPC + GN_W:h * NPC + GN_W + 1],
                                                     chan[:, h * NPC + GN_B:h * NPC + GN_B + 1], ALU.mult, ALU.add))
                    dve.wait_ge(ld[n], ONE + (64 * i + (32 if h < 2 else 64)))
                    own.link(nc.vector.tensor_tensor(dev[n][:, :], dev[n][:, :], bon[n][:, :], ALU.add))
                    own.link(nc.vector.tensor_tensor(dev[n][:, :], dev[n][:, :], gate[n][:, :], ALU.mult))
                    nc.vector.sem_inc(o_done, 1)
                    dve.wait_ge(hi_done, ONE + HP * i + h + 1)
                    own.link(nc.vector.tensor_tensor(or_lo[:, h, tok(i)], dev[n][:, :], or_hi[:, h, tok(i)], ALU.subtract))
                    nc.vector.sem_inc(lo_done, 1)


def phase_outproj(nc, d, hi, lo, x1, spare):
    with ExitStack() as stack:
        sc = Scope(nc, stack, "op")
        w_hi, w_lo = sc.sb("w_hi", [P, KT, D], F16), sc.sb("w_lo", [P, KT, D], F16)
        rows = [spare[:, n * D:n * D + D] for n in range(7)]
        wst, xt, xn, wrow = rows[0:2], rows[2:4], rows[4:6], rows[6]
        idn = sc.sb("ident", [P, P])
        ss = [sc.sb(f"ss{s}", [P, 4]) for s in range(2)]
        pp = [[sc.ps(f"p{s}{g}") for g in range(2)] for s in range(2)]
        pt = [[sc.ps(f"t{s}{g}", (P, 4, P)) for g in range(2)] for s in range(2)]
        const_in = sc.sem("const_in")
        w_in, x_in = ([sc.sem(f"{n}{s}") for s in range(2)] for n in ("w_in", "x_in"))
        w_hi_done, w_lo_done = sc.sem("w_hi_done"), sc.sem("w_lo_done")
        proj, added, squared, rooted, scaled = (sc.sem(n) for n in ("proj", "added", "squared", "rooted", "scaled"))
        var_done, turned, hi_done, lo_done, dve_own = (sc.sem(n) for n in ("var_done", "turned", "hi_done", "lo_done", "dve_own"))
        block = stack.enter_context(nc.Block())

        def at(i, s):
            return bass.ds((2 * i + s) * P, P)

        @block.sync
        def _(sp):
            sc.start_at_one(sp)
            for k in range(2):
                sp.dma_start(wst[k][:, :], d["w_out"][k * P:(k + 1) * P, :]).then_inc(w_in[k], 16)
            sp.dma_start(idn[:, :], d["ident"]).then_inc(const_in, 16)
            sp.dma_start(wrow[:, :], d["norm2_w"].partition_broadcast(P)).then_inc(const_in, 16)
            for s in range(2):
                sp.dma_start(xt[s][:, :], d["x"][s * P:(s + 1) * P, :]).then_inc(x_in[s], 16)
            for k in range(2, KT):
                sp.wait_ge(w_lo_done, ONE + k - 1)
                sp.dma_start(wst[k % 2][:, :], d["w_out"][k * P:(k + 1) * P, :]).then_inc(w_in[k % 2], 16)
            with sp.Fori(1, TT // 2) as i:
                for s in range(2):
                    sp.wait_ge(added, ONE + 4 * i + 2 * s - 2)
                    sp.dma_start(xt[s][:, :], d["x"][at(i, s), :]).then_inc(x_in[s], 16)

        @block.scalar
        def _(act):
            for k in range(KT):
                act.wait_ge(w_in[k % 2], ONE + 16 * (k // 2 + 1))
                nc.scalar.activation(w_hi[:, k, :], wst[k % 2][:, :], ACT.Copy, scale=WS).then_inc(w_hi_done, 1)
            with act.Fori(0, TT // 2) as i:
                for s in range(2):
                    act.wait_ge(added, ONE + 4 * i + 2 * s + 2)
                    act.wait_ge(turned, ONE + 4 * i)
                    nc.scalar.activation(xn[s][:, :], x1[:, 2 * i + s, :], ACT.Square,
                                         accum_out=ss[s][:, 0:1]).then_inc(squared, 1)
                    act.wait_ge(var_done, ONE + 2 * i + s + 1)
                    nc.scalar.activation(ss[s][:, 2:3], ss[s][:, 1:2], ACT.Sqrt).then_inc(rooted, 1)
                for s in range(2):
                    for g in range(2):
                        act.wait_ge(turned, ONE + 4 * i + 2 * s + g + 1)
                        nc.scalar.activation(hi[g][:, :, at(i, s)], pt[s][g][:, :, :], ACT.Copy).then_inc(hi_done, 1)

        @block.vector
        def _(dve):
            for k in range(KT):
                dve.wait_ge(w_hi_done, ONE + k + 1)
                nc.vector.scalar_tensor_tensor(out=w_lo[:, k, :], in0=wst[k % 2][:, :], scalar=WS, in1=w_hi[:, k, :],
                                               op0=ALU.mult, op1=ALU.subtract).then_inc(w_lo_done, 1)
            dve.wait_ge(const_in, ONE + 32)
            with dve.Fori(0, TT // 2) as i:
                own = Chain(dve, dve_own, 2 * i)
                for s in range(2):
                    dve.wait_ge(x_in[s], ONE + 16 * i + 16)
                    for g in range(2):
                        dve.wait_ge(proj, ONE + 4 * i + 2 * s + g + 1)
                        nc.vector.scalar_tensor_tensor(
                            out=x1[:, 2 * i + s, 512 * g:512 * g + 512], in0=pp[s][g][:, :], scalar=1 / WS,
                            in1=xt[s][:, 512 * g:512 * g + 512], op0=ALU.mult, op1=ALU.add).then_inc(added, 1)
                    dve.wait_ge(squared, ONE + 2 * i + s + 1)
                    nc.vector.tensor_scalar(ss[s][:, 1:2], ss[s][:, 0:1], 1.0 / D, RMS_EPS,
                                            ALU.mult, ALU.add).then_inc(var_done, 1)
                    dve.wait_ge(rooted, ONE + 2 * i + s + 1)
                    own.link(nc.vector.reciprocal(ss[s][:, 3:4], ss[s][:, 2:3]))
                    nc.vector.scalar_tensor_tensor(out=xn[s][:, :], in0=x1[:, 2 * i + s, :], scalar=ss[s][:, 3:4],
                                                   in1=wrow[:, :], op0=ALU.mult, op1=ALU.mult).then_inc(scaled, 1)
                for s in range(2):
                    for g in range(2):
                        dve.wait_ge(hi_done, ONE + 4 * i + 2 * s + g + 1)
                        nc.vector.tensor_tensor(lo[g][:, :, at(i, s)], pt[s][g][:, :, :], hi[g][:, :, at(i, s)],
                                                ALU.subtract).then_inc(lo_done, 1)

        @block.tensor
        def _(pe):
            pe.wait_ge(w_lo_done, ONE + KT)
            pe.wait_ge(const_in, ONE + 32)
            with pe.Fori(0, TT // 2) as i:
                for s in range(2):
                    pe.wait_ge(added, ONE + 4 * i)
                    for g in range(2):
                        for k in range(KT):
                            for w, o in ((w_hi, hi), (w_lo, hi), (w_hi, lo)):
                                ins = nc.tensor.matmul(pp[s][g][:, :], o[k // 4][:, k % 4, at(i, s)],
                                                       w[:, k, 512 * g:512 * g + 512],
                                                       start=(k == 0 and w is w_hi and o is hi),
                                                       stop=(k == KT - 1 and o is lo))
                        ins.then_inc(proj, 1)
                pe.wait_ge(lo_done, ONE + 4 * i)
                for s in range(2):
                    pe.wait_ge(scaled, ONE + 2 * i + s + 1)
                    for g in range(2):
                        for k in range(4):
                            kt = 4 * g + k
                            ins = nc.tensor.transpose(pt[s][g][:, k, :], xn[s][:, kt * P:(kt + 1) * P], idn[:, :])
                        ins.then_inc(turned, 1)


def phase_ffn(nc, d, hi, lo, x1, spare):
    G = 2
    NG = FT // G
    with ExitStack() as stack:
        sc = Scope(nc, stack, "ff")
        st_g, st_u, st_d = (spare[:, n * 2 * D:n * 2 * D + 2 * D] for n in range(3))
        st_g, st_u = (t.rearrange("p (k n) -> p k n", k=KT) for t in (st_g, st_u))
        g_hi, g_lo = sc.sb("g_hi", [P, KT, G * P], F16), sc.sb("g_lo", [P, KT, G * P], F16)
        u_hi, u_lo = sc.sb("u_hi", [P, KT, G * P], F16), sc.sb("u_lo", [P, KT, G * P], F16)
        d_hi, d_lo = sc.sb("d_hi", [P, G, D], F16), sc.sb("d_lo", [P, G, D], F16)
        st_d = st_d.rearrange("p (g n) -> p g n", g=G)
        a_hi, a_lo = sc.sb("a_hi", [P, G, S], F16), sc.sb("a_lo", [P, G, S], F16)
        sig = [sc.sb(f"sig{n}", [P, 512]) for n in range(2)]
        pg, pu = [sc.ps(f"g{n}") for n in range(2)], [sc.ps(f"u{n}") for n in range(2)]
        pd = [sc.ps(f"d{n}") for n in range(4)]
        gu_in, dn_in = sc.sem("gu_in"), sc.sem("dn_in")
        gu_hi, gu_lo, dn_hi, dn_lo = (sc.sem(n) for n in ("gu_hi", "gu_lo", "dn_hi", "dn_lo"))
        gate_done, up_done, down_done = (sc.sem(n) for n in ("gate_done", "up_done", "down_done"))
        sig_done, prod_done, a_hi_done, a_lo_done = (sc.sem(n) for n in ("sig_done", "prod_done", "a_hi_done", "a_lo_done"))
        added, dve_own = sc.sem("added"), sc.sem("dve_own")
        NGU = NB * G
        ND = TT * 2
        block = stack.enter_context(nc.Block())

        @block.sync
        def _(sp):
            sc.start_at_one(sp)
            with sp.Fori(0, NG) as i:
                sp.wait_ge(gu_lo, ONE + 2 * i)
                sp.dma_start(st_g[:, :, :], d["w_gate"][i]).then_inc(gu_in, 16)
                sp.dma_start(st_u[:, :, :], d["w_up"][i]).then_inc(gu_in, 16)
                sp.wait_ge(dn_lo, ONE + i)
                sp.dma_start(st_d[:, :, :], d["w_down"][i].rearrange("g p n -> p g n")).then_inc(dn_in, 16)

        @block.scalar
        def _(act):
            with act.Fori(0, NG) as i:
                act.wait_ge(gu_in, ONE + 32 * i + 32)
                act.wait_ge(up_done, ONE + NGU * i)
                nc.scalar.activation(g_hi[:, :, :], st_g[:, :, :], ACT.Copy, scale=WS).then_inc(gu_hi, 1)
                nc.scalar.activation(u_hi[:, :, :], st_u[:, :, :], ACT.Copy, scale=WS).then_inc(gu_hi, 1)
                act.wait_ge(dn_in, ONE + 16 * i + 16)
                act.wait_ge(down_done, ONE + ND * i)
                nc.scalar.activation(d_hi[:, :, :], st_d[:, :, :], ACT.Copy, scale=WS).then_inc(dn_hi, 1)
                for n in range(NGU):
                    b, f = n // G, n % G
                    act.wait_ge(gate_done, ONE + NGU * i + n + 1)
                    act.wait_ge(a_lo_done, ONE + (NGU * i if n < 2 else NGU * i + n - 1))
                    nc.scalar.activation(sig[n % 2][:, :], pg[n % 2][:, :], ACT.Sigmoid, scale=1 / WS).then_inc(sig_done, 1)
                    act.wait_ge(prod_done, ONE + NGU * i + n + 1)
                    nc.scalar.activation(a_hi[:, f, 512 * b:512 * b + 512], sig[n % 2][:, :], ACT.Copy).then_inc(a_hi_done, 1)

        @block.vector
        def _(dve):
            with dve.Fori(0, NG) as i:
                own = Chain(dve, dve_own, NGU * i)

                def add(t, g):
                    m = 2 * t + g
                    dve.wait_ge(down_done, ONE + ND * i + m + 1)
                    nc.vector.scalar_tensor_tensor(
                        out=x1[:, t, 512 * g:512 * g + 512], in0=pd[m % 4][:, :], scalar=1 / WS,
                        in1=x1[:, t, 512 * g:512 * g + 512], op0=ALU.mult, op1=ALU.add).then_inc(added, 1)

                for n, (lo_, st, hi_) in enumerate(((g_lo, st_g, g_hi), (u_lo, st_u, u_hi))):
                    dve.wait_ge(gu_hi, ONE + 2 * i + n + 1)
                    nc.vector.scalar_tensor_tensor(out=lo_[:, :, :], in0=st[:, :, :], scalar=WS, in1=hi_[:, :, :],
                                                   op0=ALU.mult, op1=ALU.subtract).then_inc(gu_lo, 1)
                dve.wait_ge(dn_hi, ONE + i + 1)
                nc.vector.scalar_tensor_tensor(out=d_lo[:, :, :], in0=st_d[:, :, :], scalar=WS, in1=d_hi[:, :, :],
                                               op0=ALU.mult, op1=ALU.subtract).then_inc(dn_lo, 1)
                for n in range(NGU):
                    b, f = n // G, n % G
                    dve.wait_ge(sig_done, ONE + NGU * i + n + 1)
                    own.link(nc.vector.scalar_tensor_tensor(out=sig[n % 2][:, :], in0=pg[n % 2][:, :], scalar=1 / WS,
                                                            in1=sig[n % 2][:, :], op0=ALU.mult, op1=ALU.mult))
                    dve.wait_ge(up_done, ONE + NGU * i + n + 1)
                    nc.vector.scalar_tensor_tensor(out=sig[n % 2][:, :], in0=pu[n % 2][:, :], scalar=1 / WS,
                                                   in1=sig[n % 2][:, :], op0=ALU.mult, op1=ALU.mult).then_inc(prod_done, 1)
                    dve.wait_ge(a_hi_done, ONE + NGU * i + n + 1)
                    nc.vector.tensor_tensor(a_lo[:, f, 512 * b:512 * b + 512], sig[n % 2][:, :],
                                            a_hi[:, f, 512 * b:512 * b + 512], ALU.subtract).then_inc(a_lo_done, 1)
                dve.wait_ge(added, ONE + ND * i)
                for t in range(TT):
                    for g in range(2):
                        add(t, g)

        @block.tensor
        def _(pe):
            with pe.Fori(0, NG) as i:
                pe.wait_ge(gu_lo, ONE + 2 * i + 2)
                for n in range(NGU):
                    b, f = n // G, n % G
                    tok = slice(512 * b, 512 * b + 512)
                    pe.wait_ge(prod_done, ONE + (NGU * i if n < 2 else NGU * i + n - 1))
                    for w_hi, w_lo, bank, sem in ((g_hi, g_lo, pg, gate_done), (u_hi, u_lo, pu, up_done)):
                        for k in range(KT):
                            for w, h in ((w_hi, hi), (w_hi, lo), (w_lo, hi)):
                                ins = nc.tensor.matmul(bank[n % 2][:, :], w[:, k, f * P:f * P + P],
                                                       h[k // 4][:, k % 4, tok],
                                                       start=(k == 0 and w is w_hi and h is hi),
                                                       stop=(k == KT - 1 and w is w_lo))
                        ins.then_inc(sem, 1)
                pe.wait_ge(dn_lo, ONE + i + 1)
                for t in range(TT):
                    if t % (TT // NB) == 0:
                        pe.wait_ge(a_lo_done, ONE + NGU * i + G * (t // (TT // NB)) + G)
                    for g in range(2):
                        m = 2 * t + g
                        pe.wait_ge(added, ONE + (ND * i if m < 4 else ND * i + m - 3))
                        for f in range(G):
                            for a, w in ((a_hi, d_hi), (a_hi, d_lo), (a_lo, d_hi)):
                                ins = nc.tensor.matmul(pd[m % 4][:, :], a[:, f, t * P:t * P + P],
                                                       w[:, f, 512 * g:512 * g + 512],
                                                       start=(f == 0 and a is a_hi and w is d_hi),
                                                       stop=(f == G - 1 and a is a_lo))
                        ins.then_inc(down_done, 1)


def phase_final(nc, d, x1, out):
    with ExitStack() as stack:
        sc = Scope(nc, stack, "fin")
        wrow = sc.sb("wrow", [P, D])
        o = [sc.sb(f"o{s}", [P, D]) for s in range(2)]
        ss = [sc.sb(f"ss{s}", [P, 4]) for s in range(2)]
        const_in, squared, var_done, rooted, o_done, dve_own = (
            sc.sem(n) for n in ("const_in", "squared", "var_done", "rooted", "o_done", "dve_own"))
        out_done = [sc.sem(f"out{s}") for s in range(2)]
        block = stack.enter_context(nc.Block())

        @block.sync
        def _(sp):
            sc.start_at_one(sp)
            sp.dma_start(wrow[:, :], d["norm_f_w"].partition_broadcast(P)).then_inc(const_in, 16)
            with sp.Fori(0, TT // 2) as i:
                for s in range(2):
                    sp.wait_ge(o_done, ONE + 2 * i + s + 1)
                    sp.dma_start(out[bass.ds((2 * i + s) * P, P), :], o[s][:, :]).then_inc(out_done[s], 16)
            for s in range(2):
                sp.wait_ge(out_done[s], ONE + 16 * (TT // 2))

        @block.scalar
        def _(act):
            with act.Fori(0, TT // 2) as i:
                for s in range(2):
                    act.wait_ge(out_done[s], ONE + 16 * i)
                    nc.scalar.activation(o[s][:, :], x1[:, 2 * i + s, :], ACT.Square,
                                         accum_out=ss[s][:, 0:1]).then_inc(squared, 1)
                for s in range(2):
                    act.wait_ge(var_done, ONE + 2 * i + s + 1)
                    nc.scalar.activation(ss[s][:, 2:3], ss[s][:, 1:2], ACT.Sqrt).then_inc(rooted, 1)

        @block.vector
        def _(dve):
            dve.wait_ge(const_in, ONE + 16)
            with dve.Fori(0, TT // 2) as i:
                own = Chain(dve, dve_own, 2 * i)
                for s in range(2):
                    dve.wait_ge(squared, ONE + 2 * i + s + 1)
                    nc.vector.tensor_scalar(ss[s][:, 1:2], ss[s][:, 0:1], 1.0 / D, RMS_EPS,
                                            ALU.mult, ALU.add).then_inc(var_done, 1)
                for s in range(2):
                    dve.wait_ge(rooted, ONE + 2 * i + s + 1)
                    own.link(nc.vector.reciprocal(ss[s][:, 3:4], ss[s][:, 2:3]))
                    nc.vector.scalar_tensor_tensor(out=o[s][:, :], in0=x1[:, 2 * i + s, :], scalar=ss[s][:, 3:4],
                                                   in1=wrow[:, :], op0=ALU.mult, op1=ALU.mult).then_inc(o_done, 1)


def build(nc, d, out):
    for n, dirs in (("s_r", ()), ("s_kk", ()), ("s_v", ()), ("s_g", ()), ("s_bonus", ()),
                    ("s_cum", (2,)), ("s_kd", (2,)), ("s_b", (2,))):
        d[n] = nc.dram_tensor(n, (*dirs, HP, P, S), F32, kind="Internal").ap()
    with ExitStack() as whole:
        sc = Scope(nc, whole, "all")
        PASSED.append(sc.sem("passed"))
        oc_hi, oc_lo = sc.sb("oc_hi", [P, HP, S], F16), sc.sb("oc_lo", [P, HP, S], F16)
        with ExitStack() as st:
            s1 = Scope(nc, st, "h")
            hT_hi, hT_lo = s1.sb("hT_hi", [P, KT, S], F16), s1.sb("hT_lo", [P, KT, S], F16)
            phase_norm1(nc, d["x"], d["norm1_w"], d["ident"], hT_hi, hT_lo)
            phase_inproj(nc, d, hT_hi, hT_lo, oc_hi, oc_lo)
        y = sc.sb("y", [P, HP, S + 2 * C])
        phase_scan(nc, d, y)
        or_hi, or_lo = sc.sb("or_hi", [P, HP, S], F16), sc.sb("or_lo", [P, HP, S], F16)
        phase_groupnorm(nc, d, y, or_hi, or_lo)
        x1 = sc.sb("x1", [P, TT, D])
        spare = y[:, :, :].rearrange("p h t -> p (h t)")
        phase_outproj(nc, d, (or_hi, oc_hi), (or_lo, oc_lo), x1, spare)
        phase_ffn(nc, d, (or_hi, oc_hi), (or_lo, oc_lo), x1, spare)
        phase_final(nc, d, x1, out)


def layout(inputs):
    f = lambda n: np.asarray(inputs[n])
    L = {}
    L["x"] = f("x").reshape(S, D)
    L["norm1_w"] = f("norm1_w").reshape(1, D)
    w = f("w_in")[0]
    R5, LO, G1 = 512, 3 * 512, 3 * 512 + 256
    cut = lambda a, n: w[:, a:a + n]
    tiles = [cut(LO, P), cut(LO + P, P), np.concatenate([cut(G1, 32), np.zeros((D, P - 32), w.dtype)], 1)]
    CV = G1 + 32
    for h in range(HP):
        for base in (0, R5, 2 * R5, CV + R5, CV + 2 * R5, CV):
            tiles.append(cut(base + P * h, P))
    tiles.append(np.zeros((D, P), w.dtype))
    L["w_in"] = np.ascontiguousarray(np.stack(tiles).reshape(len(tiles), KT, P, P).transpose(0, 2, 1, 3))
    mu = f("mu_shift")[0]
    cols = []
    for h in range(HP):
        c = slice(P * h, P * h + P)
        row = [mu[0:512][c], mu[512:1024][c], mu[1024:1536][c]]
        row += [f(n).reshape(-1)[c] for n in ("k_k", "w0_f", "w0_b", "a0_f", "a0_b", "k_a_f", "k_a_b", "r_k_f", "r_k_b", "gn_w", "gn_b")]
        row += [f("conv_w")[0, t][c] for t in range(3)]
        cols += row
    cols += [mu[LO:LO + P], mu[LO + P:LO + 2 * P], np.concatenate([mu[G1:G1 + 32], np.zeros(P - 32, mu.dtype)])]
    L["chan"] = np.ascontiguousarray(np.stack(cols, 1))
    for n in ("w_up_f", "w_up_b", "a_up_f", "a_up_b", "g_up"):
        L[n] = f(n)[0]
    L["ident"] = np.eye(P, dtype=np.float32)
    L["ones"] = np.kron(np.eye(2, dtype=np.float32), np.ones((C, C), np.float32))
    L["norm2_w"], L["norm_f_w"] = f("norm2_w").reshape(1, D), f("norm_f_w").reshape(1, D)
    L["w_out"] = f("w_out")[0]
    for n in ("w_gate", "w_up"):
        L[n] = np.ascontiguousarray(f(n)[0].reshape(KT, P, FT // 2, 2 * P).transpose(2, 1, 0, 3))
    L["w_down"] = f("w_down")[0].reshape(FT // 2, 2, P, D)
    L["identh"] = np.eye(P, dtype=np.float16)
    L["idents"] = np.tile(np.eye(C, dtype=np.float16), (2, 1))
    row, cl = np.arange(P)[:, None] % C, np.arange(C)[None]
    L["maskA"] = np.stack([np.stack([cl > row, cl >= row], 1), np.stack([cl < row, cl <= row], 1)], 1).astype(np.float32)
    lv = []
    for way in range(2):
        for l in range(6):
            m = 2 ** l
            late_t, late_s = row // m % 2, cl // m % 2
            lv.append((row // (2 * m) == cl // (2 * m)) & (late_t == 1 - way) & (late_s == way))
    L["maskL"] = -np.stack(lv, 1).reshape(P, 2, 6, C).astype(np.float32)
    L["keep"] = np.ascontiguousarray(np.broadcast_to((np.arange(512) % C != 0).astype(np.float16), (P, 512)))
    return L


def kernel(**inputs):
    import concourse.bacc as bacc
    from concourse.bass_utils import run_bass_kernel_spmd

    nc = bacc.Bacc("TRN2", target_bir_lowering=False, num_devices=1)
    arrays = layout(inputs)
    d = {n: nc.dram_tensor(n, a.shape, mybir.dt.from_np(a.dtype), kind="ExternalInput").ap() for n, a in arrays.items()}
    out = nc.dram_tensor("out", (S, D), F32, kind="ExternalOutput").ap()
    build(nc, d, out)
    r = run_bass_kernel_spmd(nc, [arrays], core_ids=[0])
    return r.results[0]["out"].reshape(1, S, D)
```

```python
from contextlib import ExitStack

import numpy as np

import concourse.bass as bass
from concourse import mybir

F32 = mybir.dt.float32
F16 = mybir.dt.float16
ALU = mybir.AluOpType
ACT = mybir.ActivationFunctionType

P = 128
D = 1024
S = 2048
KT = D // P
TT = S // P
NB = S // 512
HP = 4
C = 64
NCH = S // C
F = 2816
FT = F // P
DECAY = 0.606531
RMS_EPS = 1e-6
GN_EPS = 64e-5
NORM_EPS = 1e-12
ONE = 1
WS = 64.0

(MU_R, MU_K, MU_V, K_K, W0_F, W0_B, A0_F, A0_B, KA_F, KA_B, RK_F, RK_B, GN_W, GN_B, CW0, CW1, CW2) = range(17)
NPC = 17
MU_WA, MU_G0, MU_G1 = HP * NPC, HP * NPC + 1, HP * NPC + 2
NCOL = HP * NPC + 3
T_WA, T_G0, T_G1, T_LOOP = 0, 1, 2, 3
TILES = ("r", "k", "v", "c", "h", "b")


class Chain:

    def __init__(self, eng, sem, base=0):
        self.eng, self.sem, self.base, self.n = eng, sem, base, 0

    def inc(self, ins):
        ins.then_inc(self.sem, 1)
        self.n += 1
        return self.n

    def wait(self, n):
        self.eng.wait_ge(self.sem, ONE + self.base + n)

    def link(self, ins):
        self.wait(self.inc(ins))


PASSED = []


def alone(eng, sem, value):
    eng.wait_ge(sem, ONE + value)
    eng.sem_inc(PASSED[-1], 1)


class Scope:

    def __init__(self, nc, stack, prefix):
        self.nc, self.stack, self.prefix, self.sems = nc, stack, prefix, []

    def sb(self, name, shape, dt=F32):
        return self.stack.enter_context(self.nc.sbuf_tensor(f"{self.prefix}_{name}", shape, dt))

    def ps(self, name, shape=(P, 512), dt=F32):
        return self.stack.enter_context(self.nc.psum_tensor(f"{self.prefix}_{name}", list(shape), dt))

    def sem(self, name):
        self.sems.append(self.stack.enter_context(self.nc.semaphore(f"{self.prefix}_{name}")))
        return self.sems[-1]

    def start_at_one(self, eng):
        for sem in self.sems:
            eng.sem_inc(sem, ONE)


def phase_norm1(nc, x, norm_w, ident, hT_hi, hT_lo):
    with ExitStack() as stack:
        sc = Scope(nc, stack, "n1")
        xt = [sc.sb(f"x{s}", [P, D]) for s in range(2)]
        xn = [sc.sb(f"xn{s}", [P, D]) for s in range(2)]
        wrow = sc.sb("wrow", [P, D])
        idn = sc.sb("ident", [P, P])
        ss = [sc.sb(f"ss{s}", [P, 4]) for s in range(2)]
        ps = [[sc.ps(f"t{s}{g}", (P, 4, P)) for g in range(2)] for s in range(2)]
        const_in = sc.sem("const_in")
        x_in = [sc.sem(f"x_in{s}") for s in range(2)]
        squared, rooted, scaled = sc.sem("squared"), sc.sem("rooted"), sc.sem("scaled")
        turned, hi_done, lo_done = sc.sem("turned"), sc.sem("hi_done"), sc.sem("lo_done")
        var_done, dve_own = sc.sem("var_done"), sc.sem("dve_own")
        block = stack.enter_context(nc.Block())

        @block.sync
        def _(sp):
            sc.start_at_one(sp)
            sp.dma_start(idn[:, :], ident).then_inc(const_in, 16)
            sp.dma_start(wrow[:, :], norm_w.partition_broadcast(P)).then_inc(const_in, 16)
            for s in range(2):
                sp.dma_start(xt[s][:, :], x[s * P:(s + 1) * P, :]).then_inc(x_in[s], 16)
            with sp.Fori(1, TT // 2) as i:
                for s in range(2):
                    sp.wait_ge(scaled, ONE + 2 * i + s - 1)
                    sp.dma_start(xt[s][:, :], x[bass.ds((2 * i + s) * P, P), :]).then_inc(x_in[s], 16)

        @block.scalar
        def _(act):
            with act.Fori(0, TT // 2) as i:
                for s in range(2):
                    act.wait_ge(x_in[s], ONE + 16 * i + 16)
                    act.wait_ge(turned, ONE + 4 * i)
                    nc.scalar.activation(xn[s][:, :], xt[s][:, :], ACT.Square,
                                         accum_out=ss[s][:, 0:1]).then_inc(squared, 1)
                for s in range(2):
                    act.wait_ge(var_done, ONE + 2 * i + s + 1)
                    nc.scalar.activation(ss[s][:, 2:3], ss[s][:, 1:2], ACT.Sqrt).then_inc(rooted, 1)
                for s in range(2):
                    for g in range(2):
                        act.wait_ge(turned, ONE + 4 * i + 2 * s + g + 1)
                        nc.scalar.activation(hT_hi[:, 4 * g:4 * g + 4, bass.ds((2 * i + s) * P, P)],
                                             ps[s][g][:, :, :], ACT.Copy).then_inc(hi_done, 1)

        @block.vector
        def _(dve):
            dve.wait_ge(const_in, ONE + 32)
            with dve.Fori(0, TT // 2) as i:
                own = Chain(dve, dve_own, 2 * i)
                for s in range(2):
                    dve.wait_ge(squared, ONE + 2 * i + s + 1)
                    nc.vector.tensor_scalar(ss[s][:, 1:2], ss[s][:, 0:1], 1.0 / D, RMS_EPS,
                                            ALU.mult, ALU.add).then_inc(var_done, 1)
                for s in range(2):
                    dve.wait_ge(rooted, ONE + 2 * i + s + 1)
                    own.link(nc.vector.reciprocal(ss[s][:, 3:4], ss[s][:, 2:3]))
                    nc.vector.scalar_tensor_tensor(out=xn[s][:, :], in0=xt[s][:, :], scalar=ss[s][:, 3:4],
                                                   in1=wrow[:, :], op0=ALU.mult, op1=ALU.mult).then_inc(scaled, 1)
                for s in range(2):
                    for g in range(2):
                        dve.wait_ge(hi_done, ONE + 4 * i + 2 * s + g + 1)
                        tok = bass.ds((2 * i + s) * P, P)
                        nc.vector.tensor_tensor(hT_lo[:, 4 * g:4 * g + 4, tok], ps[s][g][:, :, :],
                                                hT_hi[:, 4 * g:4 * g + 4, tok], ALU.subtract).then_inc(lo_done, 1)

        @block.tensor
        def _(pe):
            pe.wait_ge(const_in, ONE + 32)
            with pe.Fori(0, TT // 2) as i:
                for s in range(2):
                    pe.wait_ge(scaled, ONE + 2 * i + s + 1)
                    for g in range(2):
                        pe.wait_ge(lo_done, ONE + 4 * i)
                        for k in range(4):
                            kt = 4 * g + k
                            ins = nc.tensor.transpose(ps[s][g][:, k, :], xn[s][:, kt * P:(kt + 1) * P], idn[:, :])
                        ins.then_inc(turned, 1)


def phase_inproj(nc, d, hT_hi, hT_lo, oc_hi, oc_lo):
    with ExitStack() as stack:
        sc = Scope(nc, stack, "ip")
        chan = sc.sb("chan", [P, NCOL])
        half = sc.sb("half", [P, NCOL])
        rest = sc.sb("rest", [P, NCOL])
        ones = sc.sb("ones", [P, P])
        wst = [sc.sb(f"wst{s}", [P, KT, P]) for s in range(2)]
        w_hi = [sc.sb(f"whi{s}", [P, KT, P], F16) for s in range(2)]
        w_lo = [sc.sb(f"wlo{s}", [P, KT, P], F16) for s in range(2)]
        xwa_hi, xwa_lo = sc.sb("xwa_hi", [P, S], F16), sc.sb("xwa_lo", [P, S], F16)
        lw_hi, lw_lo = sc.sb("lw_hi", [P, 4, 512], F16), sc.sb("lw_lo", [P, 4, 512], F16)
        raw = sc.sb("raw", [P, S + 2])
        tmp = sc.sb("tmp", [P, S + 2])
        Cb = sc.sb("Cb", [P, S])
        Q = raw
        ring = [sc.ps(f"ring{n}") for n in range(6)]
        small = [sc.ps(f"small{n}") for n in range(2)]

        const_in = sc.sem("const_in")
        prep = sc.sem("prep")
        w_in = [sc.sem(f"w_in{s}") for s in range(2)]
        hi_ready, lo_ready = sc.sem("hi_ready"), sc.sem("lo_ready")
        tile_done = sc.sem("tile_done")
        blk_done = sc.sem("blk_done")
        act_left, dve_left = sc.sem("act_left"), sc.sem("dve_left")
        sm_done = sc.sem("sm_done")
        sm_act, sm_dve = sc.sem("sm_act"), sc.sem("sm_dve")
        raw_full, raw_free = sc.sem("raw_full"), sc.sem("raw_free")
        dve_own, act_own = sc.sem("dve_own"), sc.sem("act_own")

        def big_block(pe, slot, n, b):
            tok = slice(512 * b, 512 * b + 512)
            for k in range(KT):
                for wt, ht in ((w_hi, hT_hi), (w_hi, hT_lo), (w_lo, hT_hi)):
                    ins = nc.tensor.matmul(ring[n % 6][:, :], wt[slot][:, k, :], ht[:, k, tok],
                                           start=(k == 0 and wt is w_hi and ht is hT_hi),
                                           stop=(k == KT - 1 and wt is w_lo))
            ins.then_inc(blk_done, 1)

        with ExitStack() as st2:
            s2 = Scope(nc, st2, "ip0")
            lst = s2.sb("lst", [P, 4, 512])
            gst = s2.sb("gst", [P, 2, 512])
            lg_hi, lg_lo = s2.sb("lg_hi", [P, 2, 512], F16), s2.sb("lg_lo", [P, 2, 512], F16)
            sg_hi, sg_lo = s2.sb("sg_hi", [P, 2, S], F16), s2.sb("sg_lo", [P, 2, S], F16)
            act_t = s2.sb("act_t", [P, S])
            gout = [s2.sb(f"gout{n}", [P, 512]) for n in range(2)]
            lw_in, g_out = s2.sem("lw_in"), [s2.sem(f"g_out{n}") for n in range(2)]
            lsplit_hi, lsplit_lo = s2.sem("lsplit_hi"), s2.sem("lsplit_lo")
            shifted, bent, bent_lo = s2.sem("shifted"), s2.sem("bent"), s2.sem("bent_lo")
            zeroed = s2.sem("zeroed")
            block = st2.enter_context(nc.Block())
            GR = 32

            @block.sync
            def _(sp):
                sc.start_at_one(sp)
                s2.start_at_one(sp)
                sp.dma_start(chan[:, :], d["chan"]).then_inc(const_in, 16)
                sp.dma_start(ones[:, :], d["ones"]).then_inc(const_in, 16)
                for s in range(2):
                    sp.dma_start(wst[s][:, :, :], d["w_in"][s]).then_inc(w_in[s], 16)
                sp.wait_ge(zeroed, ONE + 1)
                for n, name in enumerate(("w_up_f", "w_up_b")):
                    sp.dma_start(lst[0:64, n, :], d[name]).then_inc(lw_in, 16)
                for n, name in enumerate(("a_up_f", "a_up_b")):
                    sp.dma_start(lst[64:128, 2 + n, :], d[name]).then_inc(lw_in, 16)
                sp.dma_start(gst[:, 0, :], d["g_up"][0:P, :]).then_inc(lw_in, 16)
                sp.dma_start(gst[0:GR, 1, :], d["g_up"][P:P + GR, :]).then_inc(lw_in, 16)
                for T in (2, 3):
                    sp.wait_ge(hi_ready, ONE + T - 1)
                    sp.wait_ge(lo_ready, ONE + T - 1)
                    sp.dma_start(wst[T % 2][:, :, :], d["w_in"][T]).then_inc(w_in[T % 2], 16)
                for n in range(4 * HP):
                    sp.wait_ge(sm_act, ONE + n + 1)
                    sp.dma_start(d["s_g"][n // 4, :, 512 * (n % 4):512 * (n % 4) + 512],
                                 gout[n % 2][:, :]).then_inc(g_out[n % 2], 16)
                for n in range(2):
                    sp.wait_ge(g_out[n], ONE + 16 * 2 * HP)

            @block.gpsimd
            def _(pool):
                nc.gpsimd.memset(lst[:, :, :], 0.0).then_inc(zeroed, 1)
                nc.gpsimd.memset(raw[:, 0:1], 0.0).then_inc(prep, 1)
                nc.gpsimd.memset(raw[:, S + 1:S + 2], 0.0).then_inc(prep, 1)
                nc.gpsimd.memset(tmp[:, 0:1], 0.0).then_inc(prep, 1)
                nc.gpsimd.memset(tmp[:, S + 1:S + 2], 0.0).then_inc(prep, 1)

            @block.scalar
            def _(act):
                def split_hi(T):
                    act.wait_ge(w_in[T % 2], ONE + 16 * (T // 2 + 1))
                    if T >= 2:
                        act.wait_ge(blk_done, ONE + NB * (T - 1))
                    nc.scalar.activation(w_hi[T % 2][:, :, :], wst[T % 2][:, :, :], ACT.Copy,
                                         scale=WS).then_inc(hi_ready, 1)

                split_hi(0)
                act.wait_ge(lw_in, ONE + 16 * 6)
                nc.scalar.activation(lw_hi[:, :, :], lst[:, :, :], ACT.Copy, scale=WS).then_inc(lsplit_hi, 1)
                nc.scalar.activation(lg_hi[:, 0, :], gst[:, 0, :], ACT.Copy, scale=WS).then_inc(lsplit_hi, 1)
                nc.scalar.activation(lg_hi[0:GR, 1, :], gst[0:GR, 1, :], ACT.Copy, scale=WS).then_inc(lsplit_hi, 1)
                for T in range(3):
                    split_hi(T + 1)
                    rows = P if T < T_G1 else GR
                    act.wait_ge(raw_free, ONE + T)
                    for b in range(NB):
                        act.wait_ge(blk_done, ONE + NB * T + b + 1)
                        nc.scalar.activation(raw[0:rows, 1 + 512 * b:513 + 512 * b],
                                             ring[(NB * T + b) % 6][0:rows, :], ACT.Copy,
                                             scale=1 / WS).then_inc(act_left, 1)
                    act.wait_ge(shifted, ONE + T + 1)
                    if T == T_WA:
                        nc.scalar.activation(act_t[0:64, :], tmp[0:64, 1:S + 1], ACT.Tanh).then_inc(act_own, 1)
                        nc.scalar.activation(act_t[64:128, :], tmp[64:128, 1:S + 1], ACT.Copy).then_inc(act_own, 1)
                        act.wait_ge(act_own, ONE + 2)
                        nc.scalar.activation(xwa_hi[:, :], act_t[:, :], ACT.Copy).then_inc(bent, 1)
                    else:
                        act.wait_ge(bent_lo, ONE + T)
                        nc.scalar.activation(act_t[0:rows, :], tmp[0:rows, 1:S + 1],
                                             ACT.Sigmoid).then_inc(act_own, 1)
                        act.wait_ge(act_own, ONE + T + 2)
                        nc.scalar.activation(sg_hi[0:rows, T - 1, :], act_t[0:rows, :], ACT.Copy).then_inc(bent, 1)
                for n in range(4 * HP):
                    act.wait_ge(sm_done, ONE + n + 1)
                    if n >= 2:
                        act.wait_ge(g_out[n % 2], ONE + 16 * (n // 2))
                    nc.scalar.activation(gout[n % 2][:, :], small[n % 2][:, :], ACT.Copy,
                                         scale=1 / WS).then_inc(sm_act, 1)

            @block.vector
            def _(dve):
                own = Chain(dve, dve_own)

                def split_lo(T):
                    dve.wait_ge(hi_ready, ONE + T + 1)
                    nc.vector.scalar_tensor_tensor(out=w_lo[T % 2][:, :, :], in0=wst[T % 2][:, :, :], scalar=WS,
                                                   in1=w_hi[T % 2][:, :, :], op0=ALU.mult,
                                                   op1=ALU.subtract).then_inc(lo_ready, 1)

                dve.wait_ge(const_in, ONE + 32)
                nc.vector.tensor_scalar(half[:, :], chan[:, :], 0.5, None, ALU.mult).then_inc(prep, 1)
                nc.vector.tensor_scalar(rest[:, :], chan[:, :], -1.0, 1.0, ALU.mult, ALU.add).then_inc(prep, 1)
                split_lo(0)
                for n, (lo, st, hi) in enumerate(((lw_lo[:, :, :], lst[:, :, :], lw_hi[:, :, :]),
                                                  (lg_lo[:, 0, :], gst[:, 0, :], lg_hi[:, 0, :]),
                                                  (lg_lo[0:GR, 1, :], gst[0:GR, 1, :], lg_hi[0:GR, 1, :]))):
                    dve.wait_ge(lsplit_hi, ONE + n + 1)
                    nc.vector.scalar_tensor_tensor(out=lo, in0=st, scalar=WS, in1=hi, op0=ALU.mult,
                                                   op1=ALU.subtract).then_inc(lsplit_lo, 1)
                dve.wait_ge(prep, ONE + 6)
                for T in range(3):
                    split_lo(T + 1)
                    rows = P if T < T_G1 else GR
                    mu = MU_WA + T
                    dve.wait_ge(act_left, ONE + NB * (T + 1))
                    if T >= 1:
                        dve.wait_ge(act_own, ONE + T + 1)
                    own.link(nc.vector.tensor_tensor(tmp[0:rows, 1:S + 1], raw[0:rows, 0:S], raw[0:rows, 2:S + 2], ALU.add))
                    own.link(nc.vector.tensor_scalar(tmp[0:rows, 1:S + 1], tmp[0:rows, 1:S + 1],
                                                     half[0:rows, mu:mu + 1], None, ALU.mult))
                    own.link(nc.vector.scalar_tensor_tensor(
                        out=tmp[0:rows, 1:S + 1], in0=raw[0:rows, 1:S + 1], scalar=rest[0:rows, mu:mu + 1],
                        in1=tmp[0:rows, 1:S + 1], op0=ALU.mult, op1=ALU.add))
                    nc.vector.sem_inc(raw_free, 1)
                    nc.vector.sem_inc(shifted, 1)
                    dve.wait_ge(bent, ONE + T + 1)
                    lo, hi = (xwa_lo[:, :], xwa_hi[:, :]) if T == T_WA else (sg_lo[0:rows, T - 1, :], sg_hi[0:rows, T - 1, :])
                    nc.vector.tensor_tensor(lo, act_t[0:rows, :], hi, ALU.subtract).then_inc(bent_lo, 1)

            @block.tensor
            def _(pe):
                def free_wait(n):
                    if n >= 6:
                        pe.wait_ge(act_left, ONE + n - 5)

                for T in range(3):
                    pe.wait_ge(hi_ready, ONE + T + 1)
                    pe.wait_ge(lo_ready, ONE + T + 1)
                    for b in range(NB):
                        free_wait(NB * T + b)
                        big_block(pe, T % 2, NB * T + b, b)
                pe.wait_ge(bent_lo, ONE + 3)
                pe.wait_ge(lsplit_lo, ONE + 3)
                for hp in range(HP):
                    ch = slice(P * hp, P * hp + P)
                    for b in range(NB):
                        n = NB * hp + b
                        tok = slice(512 * b, 512 * b + 512)
                        if n >= 2:
                            pe.wait_ge(sm_act, ONE + n - 1)
                        for g, rows in ((0, P), (1, GR)):
                            for lw, sgt in ((lg_hi, sg_hi), (lg_hi, sg_lo), (lg_lo, sg_hi)):
                                ins = nc.tensor.matmul(small[n % 2][:, :], lw[0:rows, g, ch], sgt[0:rows, g, tok],
                                                       start=(g == 0 and lw is lg_hi and sgt is sg_hi),
                                                       stop=(g == 1 and lw is lg_lo))
                        ins.then_inc(sm_done, 1)

        with ExitStack() as st2:
            s2 = Scope(nc, st2, "ip1")
            R, K, V, KK = (s2.sb(n, [P, S]) for n in ("R", "K", "V", "KK"))
            sg = [s2.sb(f"s{x}", [P, 512]) for x in range(2)]
            cum = [s2.sb(f"cum{x}", [P, 512]) for x in range(2)]
            rate = [s2.sb(f"rate{x}", [P, 512]) for x in range(2)]
            kd = [s2.sb(f"kd{x}", [P, 512]) for x in range(2)]
            bb = [s2.sb(f"bb{x}", [P, 512]) for x in range(2)]
            keep = s2.sb("keep", [P, 512], F16)
            r_st, kk_st, v_st = s2.sem("r_st"), s2.sem("kk_st"), s2.sem("v_st")
            r_ready, v_ready, kk_ready = s2.sem("r_ready"), s2.sem("v_ready"), s2.sem("kk_ready")
            kraw_ready, sq_ready = s2.sem("kraw_ready"), s2.sem("sq_ready")
            cum_ready, kd_ready, bb_ready = s2.sem("cum_ready"), s2.sem("kd_ready"), s2.sem("bb_ready")
            cum_st, kd_st, bb_st = ([s2.sem(f"{n}_st{x}") for x in range(2)] for n in ("cum", "kd", "bb"))
            sg_read, rate_read = s2.sem("sg_read"), s2.sem("rate_read")
            q_ready, bonus_ready = s2.sem("q_ready"), s2.sem("bonus_ready")
            bonus_st = s2.sem("bonus_st")
            conv_free = s2.sem("conv_free")
            o_ready, o_hi = s2.sem("o_ready"), s2.sem("o_hi")
            tmp_read = s2.sem("tmp_read")
            keep_in = s2.sem("keep_in")
            block = st2.enter_context(nc.Block())
            nt = len(TILES)
            DVE_STEPS = 76

            @block.sync
            def _(sp):
                s2.start_at_one(sp)
                sp.dma_start(keep[:, :], d["keep"]).then_inc(keep_in, 16)
                with sp.Fori(0, HP) as i:
                    def load(m):
                        T = T_LOOP + 1 + m + nt * i
                        s = (T_LOOP + 1 + m) % 2
                        sp.wait_ge(hi_ready, ONE + T - 1)
                        sp.wait_ge(lo_ready, ONE + T - 1)
                        sp.dma_start(wst[s][:, :, :], d["w_in"][T]).then_inc(w_in[s], 16)

                    load(0)
                    load(1)
                    load(2)
                    sp.wait_ge(r_ready, ONE + i + 1)
                    sp.dma_start(d["s_r"][i], R[:, :]).then_inc(r_st, 16)
                    load(3)
                    load(4)
                    sp.wait_ge(kk_ready, ONE + i + 1)
                    sp.dma_start(d["s_kk"][i], KK[:, :]).then_inc(kk_st, 16)
                    sp.wait_ge(v_ready, ONE + i + 1)
                    sp.dma_start(d["s_v"][i], V[:, :]).then_inc(v_st, 16)
                    load(5)
                    for b in range(NB):
                        tok = slice(512 * b, 512 * b + 512)
                        for x in range(2):
                            n = 2 * NB * i + 2 * b + x + 1
                            sp.wait_ge(cum_ready, ONE + n)
                            sp.dma_start(d["s_cum"][x, i][:, tok], cum[x][:, :]).then_inc(cum_st[x], 16)
                            sp.wait_ge(kd_ready, ONE + n)
                            sp.dma_start(d["s_kd"][x, i][:, tok], kd[x][:, :]).then_inc(kd_st[x], 16)
                            sp.wait_ge(bb_ready, ONE + n)
                            sp.dma_start(d["s_b"][x, i][:, tok], bb[x][:, :]).then_inc(bb_st[x], 16)
                    sp.wait_ge(bonus_ready, ONE + i + 1)
                    sp.dma_start(d["s_bonus"][i], V[:, :]).then_inc(bonus_st, 16)
                for sem in (r_st, v_st, kk_st, bonus_st):
                    sp.wait_ge(sem, ONE + 16 * HP)
                for sem in (*cum_st, *kd_st, *bb_st):
                    sp.wait_ge(sem, ONE + 16 * HP * NB)

            @block.scalar
            def _(act):
                with act.Fori(0, HP) as i:
                    def split_hi(m):
                        s = (T_LOOP + 1 + m) % 2
                        act.wait_ge(w_in[s], ONE + 16 * ((T_LOOP + 1 + m) // 2 + 1) + 16 * (nt // 2) * i)
                        act.wait_ge(blk_done, ONE + NB * (T_LOOP + m + nt * i))
                        nc.scalar.activation(w_hi[s][:, :, :], wst[s][:, :, :], ACT.Copy,
                                             scale=WS).then_inc(hi_ready, 1)

                    for m, name in enumerate(TILES):
                        T = T_LOOP + 1 + m + nt * i
                        if name != "h":
                            split_hi(m)
                        if name in "rkv":
                            if name == "r":
                                act.wait_ge(sm_dve, ONE + NB * i + NB)
                            act.wait_ge(raw_free, ONE + 3 + 3 * i + m)
                        if name == "c":
                            act.wait_ge(conv_free, ONE + i)
                        if name in "rkvc":
                            for b in range(NB):
                                dst = Cb[:, 512 * b:512 * b + 512] if name == "c" else raw[:, 1 + 512 * b:513 + 512 * b]
                                act.wait_ge(blk_done, ONE + NB * (T - 1) + b + 1)
                                nc.scalar.activation(dst, ring[(NB * m + b) % 6][:, :], ACT.Copy,
                                                     scale=1 / WS).then_inc(act_left, 1)
                        if name == "k":
                            act.wait_ge(kraw_ready, ONE + i + 1)
                            nc.scalar.activation(tmp[:, 1:S + 1], KK[:, :], ACT.Square).then_inc(sq_ready, 1)
                        if name == "v":
                            for b in range(NB):
                                act.wait_ge(sm_done, ONE + 4 * HP + 24 * i + b + 1)
                                nc.scalar.activation(tmp[:, 1 + 512 * b:513 + 512 * b], small[b % 2][:, :],
                                                     ACT.Sqrt).then_inc(sm_act, 1)
                        if name == "c":
                            split_hi(m + 1)
                            for b in range(NB):
                                for x in range(2):
                                    n = 2 * NB * i + 2 * b + x
                                    j = NB + 4 * b + 2 * x
                                    act.wait_ge(sg_read, ONE + n + 1)
                                    alone(act, sm_done, 4 * HP + 24 * i + j + 1)
                                    nc.scalar.activation(sg[x][:, :], small[j % 2][:, :], ACT.Sigmoid, scale=1 / WS,
                                                         bias=chan[:, bass.ds(i * NPC + W0_F + x, 1)]).then_inc(sm_act, 1)
                                    act.wait_ge(rate_read, ONE + n + 1)
                                    alone(act, sm_done, 4 * HP + 24 * i + j + 2)
                                    nc.scalar.activation(rate[x][:, :], small[(j + 1) % 2][:, :], ACT.Sigmoid, scale=1 / WS,
                                                         bias=chan[:, bass.ds(i * NPC + A0_F + x, 1)]).then_inc(sm_act, 1)
                        if name == "b":
                            for b in range(NB):
                                act.wait_ge(o_ready, ONE + NB * i + b + 1)
                                nc.scalar.activation(oc_hi[:, i, 512 * b:512 * b + 512], Cb[:, 512 * b:512 * b + 512],
                                                     ACT.Copy).then_inc(o_hi, 1)

            @block.vector
            def _(dve):
                dve.sem_inc(dve_left, 2 * NB)
                dve.sem_inc(sm_dve, NB)
                dve.sem_inc(sg_read, 2)
                dve.sem_inc(rate_read, 2)
                dve.wait_ge(keep_in, ONE + 16)
                with dve.Fori(0, HP) as i:
                    own = Chain(dve, dve_own, 9 + DVE_STEPS * i)

                    def col(arr, c):
                        return arr[:, bass.ds(i * NPC + c, 1)]

                    def split_lo(m):
                        s = (T_LOOP + 1 + m) % 2
                        dve.wait_ge(hi_ready, ONE + T_LOOP + 2 + m + nt * i)
                        nc.vector.scalar_tensor_tensor(out=w_lo[s][:, :, :], in0=wst[s][:, :, :], scalar=WS,
                                                       in1=w_hi[s][:, :, :], op0=ALU.mult,
                                                       op1=ALU.subtract).then_inc(lo_ready, 1)

                    def shift(m, dst, mu):
                        dve.wait_ge(act_left, ONE + 3 * NB + 4 * NB * i + NB * (m + 1))
                        own.link(nc.vector.tensor_tensor(tmp[:, 1:S + 1], raw[:, 0:S], raw[:, 2:S + 2], ALU.add))
                        own.link(nc.vector.tensor_scalar(dst[:, :], raw[:, 1:S + 1], col(rest, mu), None, ALU.mult))
                        nc.vector.sem_inc(raw_free, 1)
                        own.link(nc.vector.scalar_tensor_tensor(out=dst[:, :], in0=tmp[:, 1:S + 1], scalar=col(half, mu),
                                                                in1=dst[:, :], op0=ALU.mult, op1=ALU.add))

                    split_lo(0)
                    dve.wait_ge(r_st, ONE + 16 * i)
                    shift(0, R, MU_R)
                    nc.vector.sem_inc(r_ready, 1)
                    split_lo(1)
                    shift(1, K, MU_K)
                    dve.wait_ge(kk_st, ONE + 16 * i)
                    own.link(nc.vector.tensor_scalar(KK[:, :], K[:, :], col(chan, K_K), None, ALU.mult))
                    nc.vector.sem_inc(kraw_ready, 1)
                    split_lo(2)
                    dve.wait_ge(bonus_st, ONE + 16 * i)
                    dve.wait_ge(sm_act, ONE + 4 * HP + 20 * i + NB)
                    own.link(nc.vector.tensor_scalar(tmp[:, 1:S + 1], tmp[:, 1:S + 1], NORM_EPS, None, ALU.max))
                    own.link(nc.vector.reciprocal(tmp[:, 1:S + 1], tmp[:, 1:S + 1]))
                    own.link(nc.vector.tensor_tensor(KK[:, :], KK[:, :], tmp[:, 1:S + 1], ALU.mult))
                    nc.vector.sem_inc(kk_ready, 1)
                    shift(2, V, MU_V)
                    nc.vector.sem_inc(v_ready, 1)
                    split_lo(3)
                    split_lo(4)
                    for b in range(NB):
                        tok = slice(512 * b, 512 * b + 512)
                        ptok = slice(1 + 512 * b, 513 + 512 * b)
                        for x in range(2):
                            n = 2 * NB * i + 2 * b + x
                            j = NB + 4 * b + 2 * x
                            dve.wait_ge(cum_st[x], ONE + 16 * (NB * i + b))
                            dve.wait_ge(sm_act, ONE + 4 * HP + 20 * i + j + 1)
                            way = slice(None, None, -1) if x else slice(None)
                            own.link(nc.vector.tensor_tensor_scan(
                                out=cum[x][:, way], data0=keep[:, :], data1=sg[x][:, way],
                                initial=0.0, op0=ALU.mult, op1=ALU.add))
                            nc.vector.sem_inc(cum_ready, 1)
                            nc.vector.sem_inc(sg_read, 1)
                            dve.wait_ge(sm_act, ONE + 4 * HP + 20 * i + j + 2)
                            dve.wait_ge(kd_st[x], ONE + 16 * (NB * i + b))
                            own.link(nc.vector.tensor_scalar(kd[x][:, :], rate[x][:, :], col(chan, KA_F + x),
                                                             col(rest, KA_F + x), ALU.mult, ALU.add))
                            own.link(nc.vector.tensor_tensor(kd[x][:, :], kd[x][:, :], K[:, tok], ALU.mult))
                            nc.vector.sem_inc(kd_ready, 1)
                            dve.wait_ge(bb_st[x], ONE + 16 * (NB * i + b))
                            own.link(nc.vector.tensor_tensor(bb[x][:, :], KK[:, tok], rate[x][:, :], ALU.mult))
                            nc.vector.sem_inc(bb_ready, 1)
                            nc.vector.sem_inc(rate_read, 1)
                            if x == 0:
                                own.link(nc.vector.tensor_scalar(Q[:, ptok], kd[x][:, :], col(chan, RK_F), None, ALU.mult))
                            else:
                                own.link(nc.vector.scalar_tensor_tensor(
                                    out=Q[:, ptok], in0=kd[x][:, :], scalar=col(chan, RK_B), in1=Q[:, ptok],
                                    op0=ALU.mult, op1=ALU.add))
                        own.link(nc.vector.tensor_tensor(Q[:, ptok], Q[:, ptok], R[:, tok], ALU.mult))
                        nc.vector.sem_inc(q_ready, 1)
                        dve.wait_ge(blk_done, ONE + NB * (T_LOOP + nt * i + 4) + b + 1)
                        dve.wait_ge(act_left, ONE + 3 * NB + 4 * NB * i + 3 * NB + b + 1)
                        own.link(nc.vector.scalar_tensor_tensor(
                            out=tmp[:, ptok], in0=ring[(NB * 4 + b) % 6][:, :], scalar=1 / WS, in1=Cb[:, tok],
                            op0=ALU.mult, op1=ALU.mult))
                        nc.vector.sem_inc(dve_left, 1)
                    split_lo(5)
                    own.link(nc.vector.tensor_scalar(Cb[:, :], tmp[:, 0:S], col(chan, CW0), None, ALU.mult))
                    for t in (1, 2):
                        own.link(nc.vector.scalar_tensor_tensor(out=Cb[:, :], in0=tmp[:, t:S + t], scalar=col(chan, CW0 + t),
                                                                in1=Cb[:, :], op0=ALU.mult, op1=ALU.add))
                    for b in range(NB):
                        tok = slice(512 * b, 512 * b + 512)
                        dve.wait_ge(blk_done, ONE + NB * (T_LOOP + nt * i + 5) + b + 1)
                        own.link(nc.vector.scalar_tensor_tensor(
                            out=Cb[:, tok], in0=ring[(NB * 5 + b) % 6][:, :], scalar=1 / WS, in1=Cb[:, tok],
                            op0=ALU.mult, op1=ALU.mult))
                        nc.vector.sem_inc(dve_left, 1)
                        nc.vector.sem_inc(o_ready, 1)
                    for b in range(NB):
                        tok = slice(512 * b, 512 * b + 512)
                        dve.wait_ge(o_hi, ONE + NB * i + b + 1)
                        own.link(nc.vector.tensor_tensor(oc_lo[:, i, tok], Cb[:, tok], oc_hi[:, i, tok], ALU.subtract))
                    nc.vector.sem_inc(conv_free, 1)
                    dve.wait_ge(v_st, ONE + 16 * i + 16)
                    for b in range(NB):
                        tok = slice(512 * b, 512 * b + 512)
                        dve.wait_ge(sm_done, ONE + 4 * HP + 24 * i + 20 + b + 1)
                        own.link(nc.vector.tensor_tensor(V[:, tok], V[:, tok], small[b % 2][:, :], ALU.mult))
                        nc.vector.sem_inc(sm_dve, 1)
                    nc.vector.sem_inc(bonus_ready, 1)
                    assert own.n == DVE_STEPS

            @block.tensor
            def _(pe):
                pe.wait_ge(act_left, ONE + 3 * NB)
                pe.wait_ge(sm_act, ONE + 4 * HP)
                with pe.Fori(0, HP) as i:
                    def ring_free(n):
                        q = n - 6
                        if q < 0:
                            pe.wait_ge(dve_left, ONE + 2 * NB * i + 2 * NB + q + 1)
                        elif q < 4 * NB:
                            pe.wait_ge(act_left, ONE + 3 * NB + 4 * NB * i + q + 1)
                        else:
                            pe.wait_ge(dve_left, ONE + 2 * NB * i + 2 * NB + q - 4 * NB + 1)

                    def small_free(j):
                        q = j - 2
                        if q < 0:
                            pe.wait_ge(sm_dve, ONE + NB * i + NB + q + 1)
                        elif q < 20:
                            pe.wait_ge(sm_act, ONE + 4 * HP + 20 * i + q + 1)
                        else:
                            pe.wait_ge(sm_dve, ONE + NB * i + NB + q - 20 + 1)

                    def lora(b):
                        tok = slice(512 * b, 512 * b + 512)
                        for x in range(2):
                            for kind in range(2):
                                j = NB + 4 * b + 2 * x + kind
                                small_free(j)
                                for lw, xt in ((lw_hi, xwa_hi), (lw_hi, xwa_lo), (lw_lo, xwa_hi)):
                                    ins = nc.tensor.matmul(
                                        small[j % 2][:, :], lw[:, 2 * kind + x, bass.ds(i * P, P)], xt[:, tok],
                                        start=(lw is lw_hi and xt is xwa_hi), stop=lw is lw_lo)
                                ins.then_inc(sm_done, 1)

                    for m, name in enumerate(TILES):
                        pe.wait_ge(hi_ready, ONE + T_LOOP + m + nt * i + 1)
                        pe.wait_ge(lo_ready, ONE + T_LOOP + m + nt * i + 1)
                        for b in range(NB):
                            if name == "h":
                                lora(b)
                            ring_free(NB * m + b)
                            big_block(pe, (T_LOOP + m) % 2, NB * m + b, b)
                        if name == "v":
                            pe.wait_ge(sq_ready, ONE + i + 1)
                            for b in range(NB):
                                small_free(b)
                                nc.tensor.matmul(small[b % 2][:, :], ones[:, :], tmp[:, 1 + 512 * b:513 + 512 * b],
                                                 start=True, stop=True).then_inc(sm_done, 1)
                        if name == "b":
                            for b in range(NB):
                                j = 20 + b
                                small_free(j)
                                pe.wait_ge(q_ready, ONE + NB * i + b + 1)
                                nc.tensor.matmul(small[j % 2][:, :], ones[:, :], Q[:, 1 + 512 * b:513 + 512 * b],
                                                 start=True, stop=True).then_inc(sm_done, 1)


def phase_scan(nc, d, y):
    with ExitStack() as stack:
        sc = Scope(nc, stack, "scan")
        NA, UN = 6, HP
        A_R, A_KK, A_V, A_CUM, A_KD, A_B = range(NA)
        LV = 6
        win = [sc.sb(f"win{w}", [P, NA, 2, UN, 2 * C]) for w in range(2)]

        def pair(name, shape, dt=F32):
            return [sc.sb(f"{name}{x}", shape, dt) for x in range(2)]

        def quad(name, shape, dt=F32):
            return [pair(f"{name}{q}_", shape, dt) for q in range(2)]

        E = pair("E", [P, UN, C + 1])
        Ei = pair("Ei", [P, UN, C])
        kkr = pair("kkr", [P, UN, 2, C])
        bk = pair("bk", [P, 2, UN, 2, C])
        Nh, Nl = pair("Nh", [P, UN, P], F16), pair("Nl", [P, UN, P], F16)
        X, Xbd = pair("X", [P, UN, C], F16), pair("Xbd", [P, UN, P], F16)
        GV, Vbd = pair("GV", [P, 2, UN, C], F16), pair("Vbd", [P, UN, P], F16)
        Sx, Xs = pair("Sx", [P, UN, C]), pair("Xs", [P, UN, C])
        Q = quad("Q", [P, 2, UN, 2, C])
        Rz = quad("Rz", [P, 2, UN, C])
        BT = quad("BT", [P, 2, UN, C])
        Z = quad("Z", [P, 2, UN, C])
        TI = quad("TI", [P, UN, P])
        St = quad("St", [P, UN, C])
        lam = quad("lam", [P, UN, 1])
        idn = sc.sb("ident", [P, P])
        idh = sc.sb("identh", [P, P], F16)
        ids = sc.sb("idents", [P, C], F16)
        mA = sc.sb("maskA", [P, 2, 2, C])
        mL = sc.sb("maskL", [P, 2, LV, C])
        ring = [[sc.ps(f"ring{x}{n}") for n in range(2)] for x in range(2)]
        pg = [sc.ps(f"pg{x}", (P, 2, UN, C)) for x in range(2)]
        px = [t[:, 0] for t in pg]
        py = [ring[x][0][:, 0:UN * C].rearrange("p (u k) -> p u k", u=UN) for x in range(2)]
        pq = [sc.ps(f"pq{x}", (P, UN, C)) for x in range(2)]

        const_in, zeroed, dve_own = sc.sem("const_in"), sc.sem("zeroed"), sc.sem("dve_own")
        win_in = [sc.sem(f"win_in{w}") for w in range(2)]
        exps, decayed_done, raised_done = (sc.sem(n) for n in ("exps", "decayed", "raised"))
        r_placed, kk_placed = sc.sem("r_placed"), sc.sem("kk_placed")
        turned, halfway, t_left = sc.sem("turned"), sc.sem("halfway"), sc.sem("t_left")
        a_done, a_left = sc.sem("a_done"), sc.sem("a_left")
        nh_done, nl_done = sc.sem("nh_done"), sc.sem("nl_done")
        x_done, x_left, xbd_done = sc.sem("x_done"), sc.sem("x_left"), sc.sem("xbd_done")
        gv_done, gv_left, vbd_done = sc.sem("gv_done"), sc.sem("gv_left"), [sc.sem(f"vbd_done{x}") for x in range(2)]
        res_done, res_left, rbd_done = sc.sem("res_done"), sc.sem("res_left"), sc.sem("rbd_done")
        dv_done, inv_done = sc.sem("dv_done"), sc.sem("inv_done")
        sx_done, sx_left = sc.sem("sx_done"), sc.sem("sx_left")
        su_done, su_left = sc.sem("su_done"), sc.sem("su_left")
        ss_done, s_placed = sc.sem("ss_done"), sc.sem("s_placed")
        sy_done, sy_left = sc.sem("sy_done"), sc.sem("sy_left")
        N_CONST = 5
        heads = (slice(0, C), slice(C, P))
        zero = (*bk, *Nh, *Nl, *Xbd, *Vbd, *Q[0], *Q[1], *Rz[0], *Rz[1], *TI[0], *TI[1], *St[1], *Z[1], *BT[1], *lam[1])
        N_ZERO = len(zero) + 2 + UN
        block = stack.enter_context(nc.Block())

        def steps(eng, prep, step, last_run):
            prep(0, 0, 0)
            with eng.Fori(0, NCH // 4) as i:
                for s in range(4):
                    step(4 * i + s, s, prep(4 * i + s + 1, (s + 1) % 4, i + (s + 1) // 4, now=False))
            last_run(NCH)

        def cols(s, x):
            q = s % 2
            return slice(C * q, C * q + C) if x == 0 else slice(C * (1 - q), C * (1 - q) + C)

        @block.sync
        def _(sp):
            sc.start_at_one(sp)
            for dst, src in ((idn, "ident"), (idh, "identh"), (ids, "idents"), (mA, "maskA"), (mL, "maskL")):
                sp.dma_start(dst[tuple(slice(None) for _ in dst.shape)], d[src]).then_inc(const_in, 16)

            def load(w, it):
                for x, tok in ((0, it * (2 * C)), (1, S - 2 * C - it * (2 * C))):
                    at = bass.ds(tok, 2 * C)
                    for a, src in ((A_R, d["s_r"]), (A_KK, d["s_kk"]), (A_V, d["s_v"]), (A_CUM, d["s_cum"][x]),
                                   (A_KD, d["s_kd"][x]), (A_B, d["s_b"][x])):
                        sp.dma_start(win[w][:, a, x, :, :],
                                     src.rearrange("h p t -> p h t")[:, :, at]).then_inc(win_in[w], 16)

            for w in range(2):
                load(w, w)
            with sp.Fori(1, NCH // 4) as i:
                for w in range(2):
                    done = 4 * i + 2 * w - 2
                    alone(sp, exps, 4 * done)
                    alone(sp, raised_done, 8 * done)
                    alone(sp, decayed_done, 6 * done)
                    alone(sp, turned, 4 * done)
                    load(w, 2 * i + w)
            sp.wait_ge(exps, ONE + 4 * (NCH - 2))
            sp.wait_ge(raised_done, ONE + 8 * (NCH - 2))
            sp.wait_ge(decayed_done, ONE + 6 * (NCH - 2))
            sp.wait_ge(turned, ONE + 4 * (NCH - 2))
            load(0, 0)

        @block.gpsimd
        def _(pool):
            for t in zero:
                nc.gpsimd.memset(t[tuple(slice(None) for _ in t.shape)], 0.0).then_inc(zeroed, 1)
            for x in range(2):
                one = 0 if x == 0 else C
                nc.gpsimd.memset(E[x][:, :, one:one + 1], 1.0).then_inc(zeroed, 1)
            for u in range(UN):
                nc.gpsimd.memset(y[:, u, :], 0.0).then_inc(zeroed, 1)
            pool.wait_ge(zeroed, ONE + N_ZERO)

            def prep(cs, s, i, now=True):
                def place_r():
                    for x in range(2):
                        if not now:
                            alone(pool, sy_done, 2 * cs - 1 + x)
                        alone(pool, decayed_done, 6 * cs + 3 * x + 2)
                        for e, hs in enumerate(heads):
                            nc.gpsimd.tensor_copy(Rz[s % 2][x][hs, e, :, :], kkr[x][hs, :, 1, :]).then_inc(r_placed, 1)

                if now:
                    place_r()
                return place_r

            steps(pool, prep, lambda cs, s, place_r: place_r(), lambda cs: None)

        @block.scalar
        def _(act):
            act.wait_ge(zeroed, ONE + N_ZERO)

            def copy(dst, src, sem, scale=1.0):
                nc.scalar.activation(dst, src, ACT.Copy, scale=scale).then_inc(sem, 1)

            def run_x(cs):
                for x in range(2):
                    act.wait_ge(sx_done, ONE + 2 * cs + x + 1)
                    copy(Xs[x][:, :, :], pq[x][:, :, :], sx_left, -1.0)

            def run_u(cs, par):
                for x in range(2):
                    act.wait_ge(su_done, ONE + 2 * cs + x + 1)
                    for e, hs in enumerate(heads):
                        copy(Z[1 - par][x][hs, e, :, :], pq[x][hs, :, :], su_left)

            def prep(cs, s, i, now=True):
                w, par = s // 2, s % 2

                def decays():
                    if s % 2 == 0:
                        act.wait_ge(win_in[w], ONE + 16 * 2 * NA * (i + 1))
                    act.wait_ge(decayed_done, ONE + 6 * cs)
                    act.wait_ge(raised_done, ONE + 8 * cs)
                    for x in range(2):
                        at = slice(1, C + 1) if x == 0 else slice(0, C)
                        src = win[w][:, A_CUM, x, :, cols(s, x)]
                        nc.scalar.activation(E[x][:, :, at], src, ACT.Exp, scale=-DECAY).then_inc(exps, 1)
                        nc.scalar.activation(Ei[x][:, :, :], src, ACT.Exp, scale=DECAY).then_inc(exps, 1)

                def turn(x):
                    if not now:
                        act.wait_ge(sy_done, ONE + 2 * cs - 1 + x)
                    act.wait_ge(turned, ONE + 4 * cs + 2 * x + 1)
                    for e in range(2):
                        copy(Z[par][x][heads[1 - e], e, :, :],
                             ring[x][0][0:C, :].rearrange("p (u k) -> p u k", u=UN)[:, :, C * e:C * e + C], t_left)
                    act.wait_ge(turned, ONE + 4 * cs + 2 * x + 2)
                    copy(BT[par][x][:, :, :, :].rearrange("p e u k -> p (e u k)"), ring[x][1][:, :], t_left)

                if now:
                    decays()
                    for x in range(2):
                        turn(x)
                return decays, turn

            def step(cs, s, nxt):
                par = s % 2
                decays, turn = nxt

                def level(l):
                    for x in range(2):
                        act.wait_ge(gv_done, ONE + 12 * cs + 2 * l + x + 1)
                        copy(GV[x][:, :, :, :], pg[x][:, :, :, :], gv_left)

                decays()
                act.wait_ge(res_done, ONE + 2 * cs)
                for x in range(2):
                    for e, hs in enumerate(heads):
                        act.wait_ge(a_left, ONE + 4 + 4 * cs + 2 * x + e + 1)
                        copy(Nh[x][hs, :, C * e:C * e + C], Q[par][x][hs, e, :, 0, :], nh_done)
                run_x(cs)
                level(0)
                run_u(cs, par)
                for x in range(2):
                    for e, hs in enumerate(heads):
                        act.wait_ge(nl_done, ONE + 4 * cs + 2 * x + e + 1)
                        copy(Q[par][x][hs, e, :, 0, :], kkr[x][hs, :, 0, :], kk_placed)
                level(1)
                level(2)
                level(3)
                turn(0)
                level(4)
                turn(1)
                level(5)

            def last_run(cs):
                run_x(cs)
                run_u(cs, 0)

            steps(act, prep, step, last_run)

        @block.vector
        def _(dve):
            dve.sem_inc(a_left, 4)
            dve.wait_ge(zeroed, ONE + N_ZERO)
            dve.wait_ge(const_in, ONE + 16 * N_CONST)

            def run_s(cs, par, own, x):
                alone(dve, ss_done, 2 * cs + x + 1)
                own.link(nc.vector.tensor_tensor(Sx[x][:, :, :], St[1 - par][x][:, :, :], pq[x][:, :, :], ALU.add))
                own.link(nc.vector.tensor_tensor(St[par][x][:, :, :], Sx[x][:, :, :],
                                                 lam[1 - par][x][:, :, :].broadcast_to((P, UN, C)), ALU.mult))
                for e, hs in enumerate(heads):
                    nc.vector.tensor_copy(Z[par][x][hs, e, :, :], St[par][x][hs, :, :]).then_inc(s_placed, 1)

            def run_y(cs, x):
                at = bass.ds(cs * C, C) if x == 0 else bass.ds((NCH + 1) * C - cs * C, C)
                alone(dve, sy_done, 2 * cs + x + 1)
                alone(dve, sy_left, 2 * cs + x)
                nc.vector.tensor_tensor(y[:, :, at], y[:, :, at], py[x][:, :, :], ALU.add).then_inc(sy_left, 1)

            def prep(cs, s, i, now=True):
                w, par = s // 2, s % 2

                def decayed(x):
                    if not now:
                        alone(dve, a_done, 4 * cs - 2 + 2 * x)
                        alone(dve, r_placed, 4 * cs - 2 + 2 * x)
                        alone(dve, kk_placed, 4 * cs - 2 + 2 * x)
                    if s % 2 == 0:
                        dve.wait_ge(win_in[w], ONE + 16 * 2 * NA * (i + 1))
                    c, end = cols(s, x), (1 - x) * C
                    upto, past = ((slice(1, C + 1), slice(0, C)) if x == 0 else
                                  (slice(0, C), slice(1, C + 1)))
                    g = win[w]
                    dve.wait_ge(exps, ONE + 4 * cs + 2 * x + 2)
                    nc.vector.tensor_tensor(kkr[x][:, :, 0, :], g[:, A_KK, x, :, c], E[x][:, :, past],
                                            ALU.mult).then_inc(decayed_done, 1)
                    nc.vector.tensor_tensor(kkr[x][:, :, 1, :], g[:, A_R, x, :, c], E[x][:, :, upto],
                                            ALU.mult).then_inc(decayed_done, 1)

                    nc.vector.tensor_copy(lam[par][x][:, :, :], E[x][:, :, end:end + 1]).then_inc(decayed_done, 1)

                def raised(x):
                    if not now:
                        alone(dve, turned, 4 * cs - 2 + 2 * x)
                    c, g = cols(s, x), win[w]
                    dve.wait_ge(exps, ONE + 4 * cs + 2 * x + 2)
                    for e, hs in enumerate(heads):
                        nc.vector.tensor_tensor(bk[x][hs, e, :, e, :], g[hs, A_B, x, :, c], Ei[x][hs, :, :],
                                                ALU.mult).then_inc(raised_done, 1)
                        nc.vector.tensor_tensor(bk[x][hs, e, :, 1 - e, :], g[hs, A_KD, x, :, c], Ei[x][hs, :, :],
                                                ALU.mult).then_inc(raised_done, 1)

                def scores(x):
                    if not now:
                        alone(dve, sy_done, 2 * cs - 1 + x)
                    mask = mA[:, x:x + 1, :, :].rearrange("p o a b -> p o (a b)").broadcast_to((P, UN, 2 * C))
                    for e in range(2):
                        dve.wait_ge(a_done, ONE + 4 * cs + 2 * x + e + 1)
                        nc.vector.tensor_tensor(Q[par][x][:, e, :, :, :].rearrange("p u a b -> p u (a b)"),
                                                ring[x][e][:, :].rearrange("p (u k) -> p u k", u=UN),
                                                mask, ALU.mult).then_inc(a_left, 1)

                if now:
                    for part in (decayed, raised, scores):
                        part(0)
                        part(1)
                return decayed, raised, scores

            def step(cs, s, nxt):
                par = s % 2
                decayed, raised, scores = nxt
                own = Chain(dve, dve_own, 4 * cs)

                def spread(dst, src, sem):
                    for h, hs in enumerate(heads):
                        nc.vector.tensor_copy(dst[hs, :, C * h:C * h + C], src[hs]).then_inc(sem, 1)

                def level(l):
                    for x in range(2):
                        dve.wait_ge(x_done, ONE + 12 * cs + 2 * l + x + 1)
                        nc.vector.tensor_tensor(X[x][:, :, :], px[x][:, :, :],
                                                mL[:, x, l:l + 1, :].broadcast_to((P, UN, C)), ALU.mult).then_inc(x_left, 1)
                        if l:
                            dve.wait_ge(gv_left, ONE + 12 * cs + 2 * (l - 1) + x + 1)
                            spread(Vbd[x], GV[x][:, 1, :, :], vbd_done[x])
                        dve.wait_ge(x_left, ONE + 12 * cs + 2 * l + x + 1)
                        spread(Xbd[x], X[x], xbd_done)

                def split_n(x):
                    for h, hs in enumerate(heads):
                        dve.wait_ge(nh_done, ONE + 4 * cs + 2 * x + h + 1)
                        nc.vector.tensor_tensor(Nl[x][hs, :, C * h:C * h + C], Q[par][x][hs, h, :, 0, :],
                                                Nh[x][hs, :, C * h:C * h + C], ALU.subtract).then_inc(nl_done, 1)

                raised(0)
                level(0)
                split_n(0)
                split_n(1)
                level(1)
                run_s(cs, par, own, 0)
                level(2)
                run_s(cs, par, own, 1)
                run_y(cs, 0)
                level(3)
                run_y(cs, 1)
                decayed(0)
                level(4)
                raised(1)
                decayed(1)
                level(5)
                scores(0)
                for x in range(2):
                    dve.wait_ge(res_done, ONE + 2 * cs + x + 1)
                    nc.vector.tensor_tensor(X[x][:, :, :], ids[:, :].unsqueeze(1).broadcast_to((P, UN, C)),
                                            px[x][:, :, :], ALU.subtract).then_inc(res_left, 1)
                    dve.wait_ge(res_left, ONE + 2 * cs + x + 1)
                    spread(Xbd[x], X[x], rbd_done)
                scores(1)
                for x in range(2):
                    dve.wait_ge(dv_done, ONE + 2 * cs + x + 1)
                    for e, hs in enumerate(heads):
                        nc.vector.tensor_tensor(TI[par][x][hs, :, C * e:C * e + C], GV[x][hs, 1, :, :],
                                                pg[x][hs, 0, :, :], ALU.add).then_inc(inv_done, 1)

            def last_run(cs):
                own = Chain(dve, dve_own, 4 * cs)
                run_s(cs, 0, own, 0)
                run_s(cs, 0, own, 1)
                run_y(cs, 0)
                run_y(cs, 1)

            steps(dve, prep, step, last_run)
            dve.wait_ge(sy_left, ONE + 2 * NCH + 2)
            dve.wait_ge(s_placed, ONE + 4 * NCH + 4)

        @block.tensor
        def _(pe):
            pe.wait_ge(zeroed, ONE + N_ZERO)
            pe.wait_ge(const_in, ONE + 16 * N_CONST)

            def by_head(out, *terms):
                for e, hs in enumerate(heads):
                    for u in range(UN):
                        for n, (lhs, rhs) in enumerate(terms):
                            ins = nc.tensor.matmul(out[hs, u, :], lhs(e, u), rhs(e, u), start=n == 0,
                                                   stop=n == len(terms) - 1)
                return ins

            def run_x(cs, par, x):
                o = 1 - par
                if x == 0:
                    alone(pe, s_placed, 4 * cs)
                    alone(pe, kk_placed, 4 * cs)
                    alone(pe, t_left, 6 * cs)
                    alone(pe, sy_left, 2 * cs)
                by_head(pq[x], (lambda e, u: Q[o][x][:, e, u, 0, :], lambda e, u: Z[o][x][:, e, u, :])).then_inc(sx_done, 1)

            def run_u(cs, par, x):
                o = 1 - par
                alone(pe, sx_left, 2 * cs + x + 1)
                by_head(pq[x], (lambda e, u: TI[o][x][:, u, C * e:C * e + C], lambda e, u: Xs[x][:, u, :])).then_inc(su_done, 1)

            def run_s(cs, par, x):
                o = 1 - par
                alone(pe, su_left, 4 * cs + 2 * x + 2)
                by_head(pq[x], (lambda e, u: BT[o][x][:, e, u, :], lambda e, u: Z[o][x][:, e, u, :])).then_inc(ss_done, 1)

            def run_y(cs, par, x):
                o = 1 - par
                alone(pe, r_placed, 4 * cs)
                alone(pe, a_left, 4 * cs + 2 * x + 5)
                by_head(py[x], (lambda e, u: St[o][x][:, u, :], lambda e, u: Rz[o][x][:, e, u, :]),
                        (lambda e, u: Z[o][x][:, e, u, :], lambda e, u: Q[o][x][:, e, u, 1, :])).then_inc(sy_done, 1)

            def prep(cs, s, i, now=True):
                w, par = s // 2, s % 2

                def turn(x):
                    alone(pe, raised_done, 8 * cs + 4 * x + 4)
                    alone(pe, a_left, 4 * cs + 2 * x + 1)
                    if not now:
                        alone(pe, sy_left, 2 * cs - 1 + x)
                    for u in range(UN):
                        ins = nc.tensor.transpose(ring[x][0][0:C, P * u:P * u + P], win[w][:, A_V, x, u, cols(s, x)], idn[:, :])
                    ins.then_inc(turned, 1)
                    alone(pe, a_left, 4 * cs + 2 * x + 2)
                    for e, hs in enumerate(heads):
                        for u in range(UN):
                            at = C * (UN * e + u)
                            ins = nc.tensor.transpose(ring[x][1][:, at:at + C], bk[x][hs, e, u, :, :].rearrange("p a b -> p (a b)"),
                                                      idn[hs, hs])
                        if e == 0:
                            ins.then_inc(halfway, 1)
                            alone(pe, halfway, 2 * cs + x + 1)
                    ins.then_inc(turned, 1)

                def scores(x):
                    alone(pe, decayed_done, 6 * cs + 3 * x + 2)
                    for e in range(2):
                        alone(pe, t_left, 6 * cs + 3 * x + 2 + e)
                        for u in range(UN):
                            ins = nc.tensor.matmul(ring[x][e][:, P * u:P * u + P],
                                                   bk[x][:, e, u, :, :].rearrange("p a b -> p (a b)"),
                                                   kkr[x][:, u, :, :].rearrange("p a b -> p (a b)"), start=True, stop=True)
                        ins.then_inc(a_done, 1)

                if now:
                    for x in range(2):
                        turn(x)
                        scores(x)
                return turn, scores

            def step(cs, s, nxt):
                par = s % 2
                turn, scores = nxt

                def level_x(l):
                    for x in range(2):
                        if l == 0:
                            alone(pe, nh_done, 4 * cs + 2 * x + 2)
                        else:
                            alone(pe, gv_left, 12 * cs + 2 * (l - 1) + x + 1)
                        for u in range(UN):
                            g = GV[x][:, 0, u, :] if l else ids[:, :]
                            nc.tensor.matmul(px[x][:, u, :], idh[:, :], ids[:, :], start=True, stop=False)
                            ins = nc.tensor.matmul(px[x][:, u, :], Nh[x][:, u, :], g, start=False, stop=True)
                        ins.then_inc(x_done, 1)

                def level_g(l):
                    for x in range(2):
                        alone(pe, xbd_done, 24 * cs + 4 * l + 2 * x + 2)
                        if l:
                            alone(pe, vbd_done[x], 10 * cs + 2 * l)
                        for u in range(UN):
                            nc.tensor.matmul(pg[x][:, 0, u, :], Vbd[x][:, u, :] if l else idh[:, :], X[x][:, u, :],
                                             start=True, stop=True)
                            ins = nc.tensor.matmul(pg[x][:, 1, u, :], Xbd[x][:, u, :], GV[x][:, 1, u, :] if l else ids[:, :],
                                                   start=True, stop=True)
                        ins.then_inc(gv_done, 1)

                run_x(cs, par, 0)
                run_x(cs, par, 1)
                alone(pe, inv_done, 4 * cs)
                level_x(0)
                run_u(cs, par, 0)
                level_g(0)
                run_u(cs, par, 1)
                level_x(1)
                run_s(cs, par, 0)
                level_g(1)
                run_s(cs, par, 1)
                level_x(2)
                run_y(cs, par, 0)
                level_g(2)
                run_y(cs, par, 1)
                level_x(3)
                turn(0)
                level_g(3)
                level_x(4)
                scores(0)
                level_g(4)
                turn(1)
                level_x(5)
                scores(1)
                level_g(5)
                for x in range(2):
                    alone(pe, gv_left, 12 * cs + 2 * (LV - 1) + x + 1)
                    alone(pe, nl_done, 4 * cs + 2 * x + 2)
                    for u in range(UN):
                        for n, lhs in enumerate((Nh[x][:, u, :], Nl[x][:, u, :], idh[:, :])):
                            ins = nc.tensor.matmul(px[x][:, u, :], lhs, GV[x][:, 0, u, :], start=n == 0, stop=n == 2)
                    ins.then_inc(res_done, 1)
                for x in range(2):
                    alone(pe, rbd_done, 4 * cs + 2 * x + 2)
                    for u in range(UN):
                        ins = nc.tensor.matmul(pg[x][:, 0, u, :], Xbd[x][:, u, :], GV[x][:, 1, u, :], start=True, stop=True)
                    ins.then_inc(dv_done, 1)

            def last_run(cs):
                alone(pe, inv_done, 4 * cs)
                for run in (run_x, run_u, run_s, run_y):
                    for x in range(2):
                        run(cs, 0, x)

            steps(pe, prep, step, last_run)


def phase_groupnorm(nc, d, y, or_hi, or_lo):
    with ExitStack() as stack:
        sc = Scope(nc, stack, "gn")
        chan, ones = sc.sb("chan", [P, NCOL]), sc.sb("ones", [P, P])
        bon = [sc.sb(f"bon{n}", [P, 512]) for n in range(2)]
        gate = [sc.sb(f"gate{n}", [P, 512]) for n in range(2)]
        dev = [sc.sb(f"dev{n}", [P, 512]) for n in range(2)]
        sq = [sc.sb(f"sq{n}", [P, 512]) for n in range(2)]
        pm = [sc.ps(f"mean{n}") for n in range(2)]
        pv = [sc.ps(f"var{n}") for n in range(2)]
        const_in, ld = sc.sem("const_in"), [sc.sem(f"ld{n}") for n in range(2)]
        mean_done, dev_done, sq_done, var_done = (sc.sem(n) for n in ("mean_done", "dev_done", "sq_done", "var_done"))
        vs_done, rooted, o_done, hi_done, lo_done = (sc.sem(n) for n in ("vs_done", "rooted", "o_done", "hi_done", "lo_done"))
        dve_own = sc.sem("dve_own")
        block = stack.enter_context(nc.Block())

        def tok(i):
            return bass.ds(i * 512, 512)

        @block.sync
        def _(sp):
            sc.start_at_one(sp)
            sp.dma_start(chan[:, :], d["chan"]).then_inc(const_in, 16)
            sp.dma_start(ones[:, :], d["ones"]).then_inc(const_in, 16)
            for h in range(2):
                sp.dma_start(bon[h][:, :], d["s_bonus"][h, :, 0:512]).then_inc(ld[h], 16)
                sp.dma_start(gate[h][:, :], d["s_g"][h, :, 0:512]).then_inc(ld[h], 16)
            with sp.Fori(0, NB - 1) as i:
                for h in range(HP):
                    sp.wait_ge(o_done, ONE + HP * i + h + 1)
                    g, t = (h + 2, tok(i)) if h < 2 else (h - 2, tok(i + 1))
                    sp.dma_start(bon[h % 2][:, :], d["s_bonus"][g][:, t]).then_inc(ld[h % 2], 16)
                    sp.dma_start(gate[h % 2][:, :], d["s_g"][g][:, t]).then_inc(ld[h % 2], 16)
            for h in range(2):
                sp.wait_ge(o_done, ONE + HP * (NB - 1) + h + 1)
                sp.dma_start(bon[h][:, :], d["s_bonus"][h + 2, :, S - 512:S]).then_inc(ld[h], 16)
                sp.dma_start(gate[h][:, :], d["s_g"][h + 2, :, S - 512:S]).then_inc(ld[h], 16)

        @block.tensor
        def _(pe):
            pe.wait_ge(const_in, ONE + 32)
            with pe.Fori(0, NB) as i:
                for h in range(HP):
                    n = h % 2
                    pe.wait_ge(dev_done, ONE + (HP * i if h < 2 else HP * i + h - 1))
                    nc.tensor.matmul(pm[n][:, :], ones[:, :], y[:, h, bass.ds(i * 512 + C, 512)],
                                     start=True, stop=True).then_inc(mean_done, 1)
                    pe.wait_ge(vs_done, ONE + (HP * i if h < 2 else HP * i + h - 1))
                    pe.wait_ge(sq_done, ONE + HP * i + h + 1)
                    nc.tensor.matmul(pv[n][:, :], ones[:, :], sq[n][:, :], start=True, stop=True).then_inc(var_done, 1)

        @block.scalar
        def _(act):
            with act.Fori(0, NB) as i:
                for h in range(HP):
                    n = h % 2
                    act.wait_ge(dev_done, ONE + HP * i + h + 1)
                    nc.scalar.activation(sq[n][:, :], dev[n][:, :], ACT.Square).then_inc(sq_done, 1)
                    act.wait_ge(vs_done, ONE + HP * i + h + 1)
                    nc.scalar.activation(sq[n][:, :], sq[n][:, :], ACT.Sqrt).then_inc(rooted, 1)
                    act.wait_ge(o_done, ONE + HP * i + h + 1)
                    nc.scalar.activation(or_hi[:, h, tok(i)], dev[n][:, :], ACT.Copy).then_inc(hi_done, 1)

        @block.vector
        def _(dve):
            dve.wait_ge(const_in, ONE + 32)
            with dve.Fori(0, NB) as i:
                own = Chain(dve, dve_own, 6 * HP * i)
                for h in range(HP):
                    n = h % 2
                    dve.wait_ge(mean_done, ONE + HP * i + h + 1)
                    dve.wait_ge(lo_done, ONE + (HP * i if h < 2 else HP * i + h - 1))
                    nc.vector.scalar_tensor_tensor(out=dev[n][:, :], in0=pm[n][:, :], scalar=-1.0 / C,
                                                   in1=y[:, h, bass.ds(i * 512 + C, 512)], op0=ALU.mult,
                                                   op1=ALU.add).then_inc(dev_done, 1)
                    dve.wait_ge(var_done, ONE + HP * i + h + 1)
                    nc.vector.tensor_scalar(sq[n][:, :], pv[n][:, :], 1.0 / C, GN_EPS, ALU.mult, ALU.add).then_inc(vs_done, 1)
                    dve.wait_ge(rooted, ONE + HP * i + h + 1)
                    own.link(nc.vector.reciprocal(sq[n][:, :], sq[n][:, :]))
                    own.link(nc.vector.tensor_tensor(dev[n][:, :], dev[n][:, :], sq[n][:, :], ALU.mult))
                    own.link(nc.vector.tensor_scalar(dev[n][:, :], dev[n][:, :], chan[:, h * NPC + GN_W:h * NPC + GN_W + 1],
                                                     chan[:, h * NPC + GN_B:h * NPC + GN_B + 1], ALU.mult, ALU.add))
                    dve.wait_ge(ld[n], ONE + (64 * i + (32 if h < 2 else 64)))
                    own.link(nc.vector.tensor_tensor(dev[n][:, :], dev[n][:, :], bon[n][:, :], ALU.add))
                    own.link(nc.vector.tensor_tensor(dev[n][:, :], dev[n][:, :], gate[n][:, :], ALU.mult))
                    nc.vector.sem_inc(o_done, 1)
                    dve.wait_ge(hi_done, ONE + HP * i + h + 1)
                    own.link(nc.vector.tensor_tensor(or_lo[:, h, tok(i)], dev[n][:, :], or_hi[:, h, tok(i)], ALU.subtract))
                    nc.vector.sem_inc(lo_done, 1)


def phase_outproj(nc, d, hi, lo, x1, spare):
    with ExitStack() as stack:
        sc = Scope(nc, stack, "op")
        w_hi, w_lo = sc.sb("w_hi", [P, KT, D], F16), sc.sb("w_lo", [P, KT, D], F16)
        rows = [spare[:, n * D:n * D + D] for n in range(7)]
        wst, xt, xn, wrow = rows[0:2], rows[2:4], rows[4:6], rows[6]
        idn = sc.sb("ident", [P, P])
        ss = [sc.sb(f"ss{s}", [P, 4]) for s in range(2)]
        pp = [[sc.ps(f"p{s}{g}") for g in range(2)] for s in range(2)]
        pt = [[sc.ps(f"t{s}{g}", (P, 4, P)) for g in range(2)] for s in range(2)]
        const_in = sc.sem("const_in")
        w_in, x_in = ([sc.sem(f"{n}{s}") for s in range(2)] for n in ("w_in", "x_in"))
        w_hi_done, w_lo_done = sc.sem("w_hi_done"), sc.sem("w_lo_done")
        proj, added, squared, rooted, scaled = (sc.sem(n) for n in ("proj", "added", "squared", "rooted", "scaled"))
        var_done, turned, hi_done, lo_done, dve_own = (sc.sem(n) for n in ("var_done", "turned", "hi_done", "lo_done", "dve_own"))
        block = stack.enter_context(nc.Block())

        def at(i, s):
            return bass.ds((2 * i + s) * P, P)

        @block.sync
        def _(sp):
            sc.start_at_one(sp)
            for k in range(2):
                sp.dma_start(wst[k][:, :], d["w_out"][k * P:(k + 1) * P, :]).then_inc(w_in[k], 16)
            sp.dma_start(idn[:, :], d["ident"]).then_inc(const_in, 16)
            sp.dma_start(wrow[:, :], d["norm2_w"].partition_broadcast(P)).then_inc(const_in, 16)
            for s in range(2):
                sp.dma_start(xt[s][:, :], d["x"][s * P:(s + 1) * P, :]).then_inc(x_in[s], 16)
            for k in range(2, KT):
                sp.wait_ge(w_lo_done, ONE + k - 1)
                sp.dma_start(wst[k % 2][:, :], d["w_out"][k * P:(k + 1) * P, :]).then_inc(w_in[k % 2], 16)
            with sp.Fori(1, TT // 2) as i:
                for s in range(2):
                    sp.wait_ge(added, ONE + 4 * i + 2 * s - 2)
                    sp.dma_start(xt[s][:, :], d["x"][at(i, s), :]).then_inc(x_in[s], 16)

        @block.scalar
        def _(act):
            for k in range(KT):
                act.wait_ge(w_in[k % 2], ONE + 16 * (k // 2 + 1))
                nc.scalar.activation(w_hi[:, k, :], wst[k % 2][:, :], ACT.Copy, scale=WS).then_inc(w_hi_done, 1)
            with act.Fori(0, TT // 2) as i:
                for s in range(2):
                    act.wait_ge(added, ONE + 4 * i + 2 * s + 2)
                    act.wait_ge(turned, ONE + 4 * i)
                    nc.scalar.activation(xn[s][:, :], x1[:, 2 * i + s, :], ACT.Square,
                                         accum_out=ss[s][:, 0:1]).then_inc(squared, 1)
                    act.wait_ge(var_done, ONE + 2 * i + s + 1)
                    nc.scalar.activation(ss[s][:, 2:3], ss[s][:, 1:2], ACT.Sqrt).then_inc(rooted, 1)
                for s in range(2):
                    for g in range(2):
                        act.wait_ge(turned, ONE + 4 * i + 2 * s + g + 1)
                        nc.scalar.activation(hi[g][:, :, at(i, s)], pt[s][g][:, :, :], ACT.Copy).then_inc(hi_done, 1)

        @block.vector
        def _(dve):
            for k in range(KT):
                dve.wait_ge(w_hi_done, ONE + k + 1)
                nc.vector.scalar_tensor_tensor(out=w_lo[:, k, :], in0=wst[k % 2][:, :], scalar=WS, in1=w_hi[:, k, :],
                                               op0=ALU.mult, op1=ALU.subtract).then_inc(w_lo_done, 1)
            dve.wait_ge(const_in, ONE + 32)
            with dve.Fori(0, TT // 2) as i:
                own = Chain(dve, dve_own, 2 * i)
                for s in range(2):
                    dve.wait_ge(x_in[s], ONE + 16 * i + 16)
                    for g in range(2):
                        dve.wait_ge(proj, ONE + 4 * i + 2 * s + g + 1)
                        nc.vector.scalar_tensor_tensor(
                            out=x1[:, 2 * i + s, 512 * g:512 * g + 512], in0=pp[s][g][:, :], scalar=1 / WS,
                            in1=xt[s][:, 512 * g:512 * g + 512], op0=ALU.mult, op1=ALU.add).then_inc(added, 1)
                    dve.wait_ge(squared, ONE + 2 * i + s + 1)
                    nc.vector.tensor_scalar(ss[s][:, 1:2], ss[s][:, 0:1], 1.0 / D, RMS_EPS,
                                            ALU.mult, ALU.add).then_inc(var_done, 1)
                    dve.wait_ge(rooted, ONE + 2 * i + s + 1)
                    own.link(nc.vector.reciprocal(ss[s][:, 3:4], ss[s][:, 2:3]))
                    nc.vector.scalar_tensor_tensor(out=xn[s][:, :], in0=x1[:, 2 * i + s, :], scalar=ss[s][:, 3:4],
                                                   in1=wrow[:, :], op0=ALU.mult, op1=ALU.mult).then_inc(scaled, 1)
                for s in range(2):
                    for g in range(2):
                        dve.wait_ge(hi_done, ONE + 4 * i + 2 * s + g + 1)
                        nc.vector.tensor_tensor(lo[g][:, :, at(i, s)], pt[s][g][:, :, :], hi[g][:, :, at(i, s)],
                                                ALU.subtract).then_inc(lo_done, 1)

        @block.tensor
        def _(pe):
            pe.wait_ge(w_lo_done, ONE + KT)
            pe.wait_ge(const_in, ONE + 32)
            with pe.Fori(0, TT // 2) as i:
                for s in range(2):
                    pe.wait_ge(added, ONE + 4 * i)
                    for g in range(2):
                        for k in range(KT):
                            for w, o in ((w_hi, hi), (w_lo, hi), (w_hi, lo)):
                                ins = nc.tensor.matmul(pp[s][g][:, :], o[k // 4][:, k % 4, at(i, s)],
                                                       w[:, k, 512 * g:512 * g + 512],
                                                       start=(k == 0 and w is w_hi and o is hi),
                                                       stop=(k == KT - 1 and o is lo))
                        ins.then_inc(proj, 1)
                pe.wait_ge(lo_done, ONE + 4 * i)
                for s in range(2):
                    pe.wait_ge(scaled, ONE + 2 * i + s + 1)
                    for g in range(2):
                        for k in range(4):
                            kt = 4 * g + k
                            ins = nc.tensor.transpose(pt[s][g][:, k, :], xn[s][:, kt * P:(kt + 1) * P], idn[:, :])
                        ins.then_inc(turned, 1)


def phase_ffn(nc, d, hi, lo, x1, spare):
    G = 2
    NG = FT // G
    with ExitStack() as stack:
        sc = Scope(nc, stack, "ff")
        st_g, st_u, st_d = (spare[:, n * 2 * D:n * 2 * D + 2 * D] for n in range(3))
        st_g, st_u = (t.rearrange("p (k n) -> p k n", k=KT) for t in (st_g, st_u))
        g_hi, g_lo = sc.sb("g_hi", [P, KT, G * P], F16), sc.sb("g_lo", [P, KT, G * P], F16)
        u_hi, u_lo = sc.sb("u_hi", [P, KT, G * P], F16), sc.sb("u_lo", [P, KT, G * P], F16)
        d_hi, d_lo = sc.sb("d_hi", [P, G, D], F16), sc.sb("d_lo", [P, G, D], F16)
        st_d = st_d.rearrange("p (g n) -> p g n", g=G)
        a_hi, a_lo = sc.sb("a_hi", [P, G, S], F16), sc.sb("a_lo", [P, G, S], F16)
        sig = [sc.sb(f"sig{n}", [P, 512]) for n in range(2)]
        pg, pu = [sc.ps(f"g{n}") for n in range(2)], [sc.ps(f"u{n}") for n in range(2)]
        pd = [sc.ps(f"d{n}") for n in range(4)]
        gu_in, dn_in = sc.sem("gu_in"), sc.sem("dn_in")
        gu_hi, gu_lo, dn_hi, dn_lo = (sc.sem(n) for n in ("gu_hi", "gu_lo", "dn_hi", "dn_lo"))
        gate_done, up_done, down_done = (sc.sem(n) for n in ("gate_done", "up_done", "down_done"))
        sig_done, prod_done, a_hi_done, a_lo_done = (sc.sem(n) for n in ("sig_done", "prod_done", "a_hi_done", "a_lo_done"))
        added, dve_own = sc.sem("added"), sc.sem("dve_own")
        NGU = NB * G
        ND = TT * 2
        block = stack.enter_context(nc.Block())

        @block.sync
        def _(sp):
            sc.start_at_one(sp)
            with sp.Fori(0, NG) as i:
                sp.wait_ge(gu_lo, ONE + 2 * i)
                sp.dma_start(st_g[:, :, :], d["w_gate"][i]).then_inc(gu_in, 16)
                sp.dma_start(st_u[:, :, :], d["w_up"][i]).then_inc(gu_in, 16)
                sp.wait_ge(dn_lo, ONE + i)
                sp.dma_start(st_d[:, :, :], d["w_down"][i].rearrange("g p n -> p g n")).then_inc(dn_in, 16)

        @block.scalar
        def _(act):
            with act.Fori(0, NG) as i:
                act.wait_ge(gu_in, ONE + 32 * i + 32)
                act.wait_ge(up_done, ONE + NGU * i)
                nc.scalar.activation(g_hi[:, :, :], st_g[:, :, :], ACT.Copy, scale=WS).then_inc(gu_hi, 1)
                nc.scalar.activation(u_hi[:, :, :], st_u[:, :, :], ACT.Copy, scale=WS).then_inc(gu_hi, 1)
                act.wait_ge(dn_in, ONE + 16 * i + 16)
                act.wait_ge(down_done, ONE + ND * i)
                nc.scalar.activation(d_hi[:, :, :], st_d[:, :, :], ACT.Copy, scale=WS).then_inc(dn_hi, 1)
                for n in range(NGU):
                    b, f = n // G, n % G
                    act.wait_ge(gate_done, ONE + NGU * i + n + 1)
                    act.wait_ge(a_lo_done, ONE + (NGU * i if n < 2 else NGU * i + n - 1))
                    nc.scalar.activation(sig[n % 2][:, :], pg[n % 2][:, :], ACT.Sigmoid, scale=1 / WS).then_inc(sig_done, 1)
                    act.wait_ge(prod_done, ONE + NGU * i + n + 1)
                    nc.scalar.activation(a_hi[:, f, 512 * b:512 * b + 512], sig[n % 2][:, :], ACT.Copy).then_inc(a_hi_done, 1)

        @block.vector
        def _(dve):
            with dve.Fori(0, NG) as i:
                own = Chain(dve, dve_own, NGU * i)

                def add(t, g):
                    m = 2 * t + g
                    dve.wait_ge(down_done, ONE + ND * i + m + 1)
                    nc.vector.scalar_tensor_tensor(
                        out=x1[:, t, 512 * g:512 * g + 512], in0=pd[m % 4][:, :], scalar=1 / WS,
                        in1=x1[:, t, 512 * g:512 * g + 512], op0=ALU.mult, op1=ALU.add).then_inc(added, 1)

                for n, (lo_, st, hi_) in enumerate(((g_lo, st_g, g_hi), (u_lo, st_u, u_hi))):
                    dve.wait_ge(gu_hi, ONE + 2 * i + n + 1)
                    nc.vector.scalar_tensor_tensor(out=lo_[:, :, :], in0=st[:, :, :], scalar=WS, in1=hi_[:, :, :],
                                                   op0=ALU.mult, op1=ALU.subtract).then_inc(gu_lo, 1)
                dve.wait_ge(dn_hi, ONE + i + 1)
                nc.vector.scalar_tensor_tensor(out=d_lo[:, :, :], in0=st_d[:, :, :], scalar=WS, in1=d_hi[:, :, :],
                                               op0=ALU.mult, op1=ALU.subtract).then_inc(dn_lo, 1)
                for n in range(NGU):
                    b, f = n // G, n % G
                    dve.wait_ge(sig_done, ONE + NGU * i + n + 1)
                    own.link(nc.vector.scalar_tensor_tensor(out=sig[n % 2][:, :], in0=pg[n % 2][:, :], scalar=1 / WS,
                                                            in1=sig[n % 2][:, :], op0=ALU.mult, op1=ALU.mult))
                    dve.wait_ge(up_done, ONE + NGU * i + n + 1)
                    nc.vector.scalar_tensor_tensor(out=sig[n % 2][:, :], in0=pu[n % 2][:, :], scalar=1 / WS,
                                                   in1=sig[n % 2][:, :], op0=ALU.mult, op1=ALU.mult).then_inc(prod_done, 1)
                    dve.wait_ge(a_hi_done, ONE + NGU * i + n + 1)
                    nc.vector.tensor_tensor(a_lo[:, f, 512 * b:512 * b + 512], sig[n % 2][:, :],
                                            a_hi[:, f, 512 * b:512 * b + 512], ALU.subtract).then_inc(a_lo_done, 1)
                dve.wait_ge(added, ONE + ND * i)
                for t in range(TT):
                    for g in range(2):
                        add(t, g)

        @block.tensor
        def _(pe):
            with pe.Fori(0, NG) as i:
                pe.wait_ge(gu_lo, ONE + 2 * i + 2)
                for n in range(NGU):
                    b, f = n // G, n % G
                    tok = slice(512 * b, 512 * b + 512)
                    pe.wait_ge(prod_done, ONE + (NGU * i if n < 2 else NGU * i + n - 1))
                    for w_hi, w_lo, bank, sem in ((g_hi, g_lo, pg, gate_done), (u_hi, u_lo, pu, up_done)):
                        for k in range(KT):
                            for w, h in ((w_hi, hi), (w_hi, lo), (w_lo, hi)):
                                ins = nc.tensor.matmul(bank[n % 2][:, :], w[:, k, f * P:f * P + P],
                                                       h[k // 4][:, k % 4, tok],
                                                       start=(k == 0 and w is w_hi and h is hi),
                                                       stop=(k == KT - 1 and w is w_lo))
                        ins.then_inc(sem, 1)
                pe.wait_ge(dn_lo, ONE + i + 1)
                for t in range(TT):
                    if t % (TT // NB) == 0:
                        pe.wait_ge(a_lo_done, ONE + NGU * i + G * (t // (TT // NB)) + G)
                    for g in range(2):
                        m = 2 * t + g
                        pe.wait_ge(added, ONE + (ND * i if m < 4 else ND * i + m - 3))
                        for f in range(G):
                            for a, w in ((a_hi, d_hi), (a_hi, d_lo), (a_lo, d_hi)):
                                ins = nc.tensor.matmul(pd[m % 4][:, :], a[:, f, t * P:t * P + P],
                                                       w[:, f, 512 * g:512 * g + 512],
                                                       start=(f == 0 and a is a_hi and w is d_hi),
                                                       stop=(f == G - 1 and a is a_lo))
                        ins.then_inc(down_done, 1)


def phase_final(nc, d, x1, out):
    with ExitStack() as stack:
        sc = Scope(nc, stack, "fin")
        wrow = sc.sb("wrow", [P, D])
        o = [sc.sb(f"o{s}", [P, D]) for s in range(2)]
        ss = [sc.sb(f"ss{s}", [P, 4]) for s in range(2)]
        const_in, squared, var_done, rooted, o_done, dve_own = (
            sc.sem(n) for n in ("const_in", "squared", "var_done", "rooted", "o_done", "dve_own"))
        out_done = [sc.sem(f"out{s}") for s in range(2)]
        block = stack.enter_context(nc.Block())

        @block.sync
        def _(sp):
            sc.start_at_one(sp)
            sp.dma_start(wrow[:, :], d["norm_f_w"].partition_broadcast(P)).then_inc(const_in, 16)
            with sp.Fori(0, TT // 2) as i:
                for s in range(2):
                    sp.wait_ge(o_done, ONE + 2 * i + s + 1)
                    sp.dma_start(out[bass.ds((2 * i + s) * P, P), :], o[s][:, :]).then_inc(out_done[s], 16)
            for s in range(2):
                sp.wait_ge(out_done[s], ONE + 16 * (TT // 2))

        @block.scalar
        def _(act):
            with act.Fori(0, TT // 2) as i:
                for s in range(2):
                    act.wait_ge(out_done[s], ONE + 16 * i)
                    nc.scalar.activation(o[s][:, :], x1[:, 2 * i + s, :], ACT.Square,
                                         accum_out=ss[s][:, 0:1]).then_inc(squared, 1)
                for s in range(2):
                    act.wait_ge(var_done, ONE + 2 * i + s + 1)
                    nc.scalar.activation(ss[s][:, 2:3], ss[s][:, 1:2], ACT.Sqrt).then_inc(rooted, 1)

        @block.vector
        def _(dve):
            dve.wait_ge(const_in, ONE + 16)
            with dve.Fori(0, TT // 2) as i:
                own = Chain(dve, dve_own, 2 * i)
                for s in range(2):
                    dve.wait_ge(squared, ONE + 2 * i + s + 1)
                    nc.vector.tensor_scalar(ss[s][:, 1:2], ss[s][:, 0:1], 1.0 / D, RMS_EPS,
                                            ALU.mult, ALU.add).then_inc(var_done, 1)
                for s in range(2):
                    dve.wait_ge(rooted, ONE + 2 * i + s + 1)
                    own.link(nc.vector.reciprocal(ss[s][:, 3:4], ss[s][:, 2:3]))
                    nc.vector.scalar_tensor_tensor(out=o[s][:, :], in0=x1[:, 2 * i + s, :], scalar=ss[s][:, 3:4],
                                                   in1=wrow[:, :], op0=ALU.mult, op1=ALU.mult).then_inc(o_done, 1)


def build(nc, d, out):
    for n, dirs in (("s_r", ()), ("s_kk", ()), ("s_v", ()), ("s_g", ()), ("s_bonus", ()),
                    ("s_cum", (2,)), ("s_kd", (2,)), ("s_b", (2,))):
        d[n] = nc.dram_tensor(n, (*dirs, HP, P, S), F32, kind="Internal").ap()
    with ExitStack() as whole:
        sc = Scope(nc, whole, "all")
        PASSED.append(sc.sem("passed"))
        oc_hi, oc_lo = sc.sb("oc_hi", [P, HP, S], F16), sc.sb("oc_lo", [P, HP, S], F16)
        with ExitStack() as st:
            s1 = Scope(nc, st, "h")
            hT_hi, hT_lo = s1.sb("hT_hi", [P, KT, S], F16), s1.sb("hT_lo", [P, KT, S], F16)
            phase_norm1(nc, d["x"], d["norm1_w"], d["ident"], hT_hi, hT_lo)
            phase_inproj(nc, d, hT_hi, hT_lo, oc_hi, oc_lo)
        y = sc.sb("y", [P, HP, S + 2 * C])
        phase_scan(nc, d, y)
        or_hi, or_lo = sc.sb("or_hi", [P, HP, S], F16), sc.sb("or_lo", [P, HP, S], F16)
        phase_groupnorm(nc, d, y, or_hi, or_lo)
        x1 = sc.sb("x1", [P, TT, D])
        spare = y[:, :, :].rearrange("p h t -> p (h t)")
        phase_outproj(nc, d, (or_hi, oc_hi), (or_lo, oc_lo), x1, spare)
        phase_ffn(nc, d, (or_hi, oc_hi), (or_lo, oc_lo), x1, spare)
        phase_final(nc, d, x1, out)


def layout(inputs):
    f = lambda n: np.asarray(inputs[n])
    L = {}
    L["x"] = f("x").reshape(S, D)
    L["norm1_w"] = f("norm1_w").reshape(1, D)
    w = f("w_in")[0]
    R5, LO, G1 = 512, 3 * 512, 3 * 512 + 256
    cut = lambda a, n: w[:, a:a + n]
    tiles = [cut(LO, P), cut(LO + P, P), np.concatenate([cut(G1, 32), np.zeros((D, P - 32), w.dtype)], 1)]
    CV = G1 + 32
    for h in range(HP):
        for base in (0, R5, 2 * R5, CV + R5, CV + 2 * R5, CV):
            tiles.append(cut(base + P * h, P))
    tiles.append(np.zeros((D, P), w.dtype))
    L["w_in"] = np.ascontiguousarray(np.stack(tiles).reshape(len(tiles), KT, P, P).transpose(0, 2, 1, 3))
    mu = f("mu_shift")[0]
    cols = []
    for h in range(HP):
        c = slice(P * h, P * h + P)
        row = [mu[0:512][c], mu[512:1024][c], mu[1024:1536][c]]
        row += [f(n).reshape(-1)[c] for n in ("k_k", "w0_f", "w0_b", "a0_f", "a0_b", "k_a_f", "k_a_b", "r_k_f", "r_k_b", "gn_w", "gn_b")]
        row += [f("conv_w")[0, t][c] for t in range(3)]
        cols += row
    cols += [mu[LO:LO + P], mu[LO + P:LO + 2 * P], np.concatenate([mu[G1:G1 + 32], np.zeros(P - 32, mu.dtype)])]
    L["chan"] = np.ascontiguousarray(np.stack(cols, 1))
    for n in ("w_up_f", "w_up_b", "a_up_f", "a_up_b", "g_up"):
        L[n] = f(n)[0]
    L["ident"] = np.eye(P, dtype=np.float32)
    L["ones"] = np.kron(np.eye(2, dtype=np.float32), np.ones((C, C), np.float32))
    L["norm2_w"], L["norm_f_w"] = f("norm2_w").reshape(1, D), f("norm_f_w").reshape(1, D)
    L["w_out"] = f("w_out")[0]
    for n in ("w_gate", "w_up"):
        L[n] = np.ascontiguousarray(f(n)[0].reshape(KT, P, FT // 2, 2 * P).transpose(2, 1, 0, 3))
    L["w_down"] = f("w_down")[0].reshape(FT // 2, 2, P, D)
    L["identh"] = np.eye(P, dtype=np.float16)
    L["idents"] = np.tile(np.eye(C, dtype=np.float16), (2, 1))
    row, cl = np.arange(P)[:, None] % C, np.arange(C)[None]
    L["maskA"] = np.stack([np.stack([cl > row, cl >= row], 1), np.stack([cl < row, cl <= row], 1)], 1).astype(np.float32)
    lv = []
    for way in range(2):
        for l in range(6):
            m = 2 ** l
            late_t, late_s = row // m % 2, cl // m % 2
            lv.append((row // (2 * m) == cl // (2 * m)) & (late_t == 1 - way) & (late_s == way))
    L["maskL"] = ((row == cl)[:, None] - np.stack(lv, 1).astype(np.float32)).reshape(P, 2, 6, C).astype(np.float32)
    L["keep"] = np.ascontiguousarray(np.broadcast_to((np.arange(512) % C != 0).astype(np.float16), (P, 512)))
    return L


def kernel(**inputs):
    import concourse.bacc as bacc
    from concourse.bass_utils import run_bass_kernel_spmd

    nc = bacc.Bacc("TRN2", target_bir_lowering=False, num_devices=1)
    arrays = layout(inputs)
    d = {n: nc.dram_tensor(n, a.shape, mybir.dt.from_np(a.dtype), kind="ExternalInput").ap() for n, a in arrays.items()}
    out = nc.dram_tensor("out", (S, D), F32, kind="ExternalOutput").ap()
    build(nc, d, out)
    r = run_bass_kernel_spmd(nc, [arrays], core_ids=[0])
    return r.results[0]["out"].reshape(1, S, D)
```

```python
from contextlib import ExitStack

import numpy as np

import concourse.bass as bass
from concourse import mybir

F32 = mybir.dt.float32
F16 = mybir.dt.float16
ALU = mybir.AluOpType
ACT = mybir.ActivationFunctionType

P = 128
D = 1024
S = 2048
KT = D // P
TT = S // P
NB = S // 512
HP = 4
C = 64
NCH = S // C
F = 2816
FT = F // P
DECAY = 0.606531
RMS_EPS = 1e-6
GN_EPS = 64e-5
NORM_EPS = 1e-12
ONE = 1
WS = 64.0

(MU_R, MU_K, MU_V, K_K, W0_F, W0_B, A0_F, A0_B, KA_F, KA_B, RK_F, RK_B, GN_W, GN_B, CW0, CW1, CW2) = range(17)
NPC = 17
MU_WA, MU_G0, MU_G1 = HP * NPC, HP * NPC + 1, HP * NPC + 2
NCOL = HP * NPC + 3
T_WA, T_G0, T_G1, T_LOOP = 0, 1, 2, 3
TILES = ("r", "k", "v", "c", "h", "b")


class Chain:

    def __init__(self, eng, sem, base=0):
        self.eng, self.sem, self.base, self.n = eng, sem, base, 0

    def inc(self, ins):
        ins.then_inc(self.sem, 1)
        self.n += 1
        return self.n

    def wait(self, n):
        self.eng.wait_ge(self.sem, ONE + self.base + n)

    def link(self, ins):
        self.wait(self.inc(ins))


PASSED = []


def alone(eng, sem, value):
    eng.wait_ge(sem, ONE + value)
    eng.sem_inc(PASSED[-1], 1)


class Scope:

    def __init__(self, nc, stack, prefix):
        self.nc, self.stack, self.prefix, self.sems = nc, stack, prefix, []

    def sb(self, name, shape, dt=F32):
        return self.stack.enter_context(self.nc.sbuf_tensor(f"{self.prefix}_{name}", shape, dt))

    def ps(self, name, shape=(P, 512), dt=F32):
        return self.stack.enter_context(self.nc.psum_tensor(f"{self.prefix}_{name}", list(shape), dt))

    def sem(self, name):
        self.sems.append(self.stack.enter_context(self.nc.semaphore(f"{self.prefix}_{name}")))
        return self.sems[-1]

    def start_at_one(self, eng):
        for sem in self.sems:
            eng.sem_inc(sem, ONE)


def phase_norm1(nc, x, norm_w, ident, hT_hi, hT_lo):
    T = 4
    NG = TT // T
    with ExitStack() as stack:
        sc = Scope(nc, stack, "n1")
        xt = [sc.sb(f"x{s}", [P, D]) for s in range(2 * T)]
        xn = [sc.sb(f"xn{s}", [P, D]) for s in range(2 * T)]
        square = sc.sb("square", [P, D])
        wrow = sc.sb("wrow", [P, D])
        idn = sc.sb("ident", [P, P])
        eps = sc.sb("eps", [P, 1])
        ss = [sc.sb(f"ss{s}", [P, 3, T]) for s in range(2)]
        ps = [[sc.ps(f"t{s}{g}", (P, 4, P)) for g in range(2)] for s in range(T)]
        const_in = sc.sem("const_in")
        x_in = [sc.sem(f"x_in{n}") for n in range(4)]
        eps_set, act_own, rooted, scaled, turned, hi_done, lo_done, dve_own = (
            sc.sem(n) for n in ("eps_set", "act_own", "rooted", "scaled", "turned", "hi_done", "lo_done", "dve_own"))
        block = stack.enter_context(nc.Block())

        def tok(t):
            return slice(t * P, t * P + P)

        @block.sync
        def _(sp):
            sc.start_at_one(sp)
            for t in range(TT):
                if t >= 2 * T:
                    sp.wait_ge(scaled, ONE + t - 2 * T + 1)
                sp.dma_start(xt[t % (2 * T)][:, :], x[tok(t), :]).then_inc(x_in[t // 2 % 4], 16)
                if t == 1:
                    sp.dma_start(idn[:, :], ident).then_inc(const_in, 16)
                    sp.dma_start(wrow[:, :], norm_w.partition_broadcast(P)).then_inc(const_in, 16)

        @block.gpsimd
        def _(pool):
            nc.gpsimd.memset(eps[:, :], RMS_EPS).then_inc(eps_set, 1)

        @block.scalar
        def _(act):
            act.wait_ge(eps_set, ONE + 1)

            def norms(g):
                if g >= 2:
                    act.wait_ge(scaled, ONE + T * (g - 1))
                for s in range(T):
                    t = T * g + s
                    act.wait_ge(x_in[t // 2 % 4], ONE + 32 * (t // 8 + 1))
                    if t:
                        act.wait_ge(act_own, ONE + t)
                    nc.scalar.activation(square[:, :], xt[t % (2 * T)][:, :], ACT.Square,
                                         accum_out=ss[g % 2][:, 0, s:s + 1]).then_inc(act_own, 1)
                act.wait_ge(act_own, ONE + T * g + T)
                nc.scalar.activation(ss[g % 2][:, 1, :], ss[g % 2][:, 0, :], ACT.Sqrt, scale=1.0 / D,
                                     bias=eps[:, 0:1]).then_inc(rooted, 1)

            def split_hi(g):
                for t in range(T * g, T * g + T):
                    for h in range(2):
                        act.wait_ge(turned, ONE + 2 * t + h + 1)
                        nc.scalar.activation(hT_hi[:, 4 * h:4 * h + 4, tok(t)], ps[t % T][h][:, :, :],
                                             ACT.Copy).then_inc(hi_done, 1)

            norms(0)
            for g in range(1, NG):
                norms(g)
                split_hi(g - 1)
            split_hi(NG - 1)

        @block.vector
        def _(dve):
            own = Chain(dve, dve_own)

            def scale(g):
                dve.wait_ge(rooted, ONE + g + 1)
                own.link(nc.vector.reciprocal(ss[g % 2][:, 2, :], ss[g % 2][:, 1, :]))
                for s in range(T):
                    t = T * g + s
                    if g >= 2:
                        dve.wait_ge(turned, ONE + 2 * (t - 2 * T) + 2)
                    nc.vector.scalar_tensor_tensor(out=xn[t % (2 * T)][:, :], in0=xt[t % (2 * T)][:, :],
                                                   scalar=ss[g % 2][:, 2, s:s + 1], in1=wrow[:, :],
                                                   op0=ALU.mult, op1=ALU.mult).then_inc(scaled, 1)

            def split_lo(g):
                for t in range(T * g, T * g + T):
                    for h in range(2):
                        dve.wait_ge(hi_done, ONE + 2 * t + h + 1)
                        nc.vector.tensor_tensor(hT_lo[:, 4 * h:4 * h + 4, tok(t)], ps[t % T][h][:, :, :],
                                                hT_hi[:, 4 * h:4 * h + 4, tok(t)], ALU.subtract).then_inc(lo_done, 1)

            dve.wait_ge(const_in, ONE + 32)
            scale(0)
            for g in range(1, NG):
                scale(g)
                split_lo(g - 1)
            split_lo(NG - 1)

        @block.tensor
        def _(pe):
            pe.wait_ge(const_in, ONE + 32)
            for t in range(TT):
                pe.wait_ge(scaled, ONE + t + 1)
                if t >= T:
                    pe.wait_ge(lo_done, ONE + 2 * (t - T) + 2)
                for h in range(2):
                    for k in range(4):
                        kt = 4 * h + k
                        ins = nc.tensor.transpose(ps[t % T][h][:, k, :], xn[t % (2 * T)][:, kt * P:(kt + 1) * P], idn[:, :])
                    ins.then_inc(turned, 1)


def phase_inproj(nc, d, hT_hi, hT_lo, oc_hi, oc_lo):
    with ExitStack() as stack:
        sc = Scope(nc, stack, "ip")
        chan = sc.sb("chan", [P, NCOL])
        half = sc.sb("half", [P, NCOL])
        rest = sc.sb("rest", [P, NCOL])
        ones = sc.sb("ones", [P, P])
        wst = [sc.sb(f"wst{s}", [P, KT, P]) for s in range(2)]
        w_hi = [sc.sb(f"whi{s}", [P, KT, P], F16) for s in range(2)]
        w_lo = [sc.sb(f"wlo{s}", [P, KT, P], F16) for s in range(2)]
        xwa_hi, xwa_lo = sc.sb("xwa_hi", [P, S], F16), sc.sb("xwa_lo", [P, S], F16)
        lw_hi, lw_lo = sc.sb("lw_hi", [P, 4, 512], F16), sc.sb("lw_lo", [P, 4, 512], F16)
        raw = sc.sb("raw", [P, S + 2])
        tmp = sc.sb("tmp", [P, S + 2])
        Cb = sc.sb("Cb", [P, S])
        Q = raw
        ring = [sc.ps(f"ring{n}") for n in range(6)]
        small = [sc.ps(f"small{n}") for n in range(2)]

        const_in = sc.sem("const_in")
        prep = sc.sem("prep")
        w_in = [sc.sem(f"w_in{s}") for s in range(2)]
        hi_ready, lo_ready = sc.sem("hi_ready"), sc.sem("lo_ready")
        tile_done = sc.sem("tile_done")
        blk_done = sc.sem("blk_done")
        act_left, dve_left = sc.sem("act_left"), sc.sem("dve_left")
        sm_done = sc.sem("sm_done")
        sm_act, sm_dve = sc.sem("sm_act"), sc.sem("sm_dve")
        raw_full, raw_free = sc.sem("raw_full"), sc.sem("raw_free")
        dve_own, act_own = sc.sem("dve_own"), sc.sem("act_own")

        def big_block(pe, slot, n, b):
            tok = slice(512 * b, 512 * b + 512)
            for k in range(KT):
                for wt, ht in ((w_hi, hT_hi), (w_hi, hT_lo), (w_lo, hT_hi)):
                    ins = nc.tensor.matmul(ring[n % 6][:, :], wt[slot][:, k, :], ht[:, k, tok],
                                           start=(k == 0 and wt is w_hi and ht is hT_hi),
                                           stop=(k == KT - 1 and wt is w_lo))
            ins.then_inc(blk_done, 1)

        with ExitStack() as st2:
            s2 = Scope(nc, st2, "ip0")
            lst = s2.sb("lst", [P, 4, 512])
            gst = s2.sb("gst", [P, 2, 512])
            lg_hi, lg_lo = s2.sb("lg_hi", [P, 2, 512], F16), s2.sb("lg_lo", [P, 2, 512], F16)
            sg_hi, sg_lo = s2.sb("sg_hi", [P, 2, S], F16), s2.sb("sg_lo", [P, 2, S], F16)
            act_t = s2.sb("act_t", [P, S])
            gout = [s2.sb(f"gout{n}", [P, 512]) for n in range(2)]
            lw_in, g_out = s2.sem("lw_in"), [s2.sem(f"g_out{n}") for n in range(2)]
            lsplit_hi, lsplit_lo = s2.sem("lsplit_hi"), s2.sem("lsplit_lo")
            shifted, bent, bent_lo = s2.sem("shifted"), s2.sem("bent"), s2.sem("bent_lo")
            zeroed = s2.sem("zeroed")
            block = st2.enter_context(nc.Block())
            GR = 32

            @block.sync
            def _(sp):
                sc.start_at_one(sp)
                s2.start_at_one(sp)
                sp.dma_start(chan[:, :], d["chan"]).then_inc(const_in, 16)
                sp.dma_start(ones[:, :], d["ones"]).then_inc(const_in, 16)
                for s in range(2):
                    sp.dma_start(wst[s][:, :, :], d["w_in"][s]).then_inc(w_in[s], 16)
                sp.wait_ge(zeroed, ONE + 1)
                for n, name in enumerate(("w_up_f", "w_up_b")):
                    sp.dma_start(lst[0:64, n, :], d[name]).then_inc(lw_in, 16)
                for n, name in enumerate(("a_up_f", "a_up_b")):
                    sp.dma_start(lst[64:128, 2 + n, :], d[name]).then_inc(lw_in, 16)
                sp.dma_start(gst[:, 0, :], d["g_up"][0:P, :]).then_inc(lw_in, 16)
                sp.dma_start(gst[0:GR, 1, :], d["g_up"][P:P + GR, :]).then_inc(lw_in, 16)
                for T in (2, 3):
                    sp.wait_ge(hi_ready, ONE + T - 1)
                    sp.wait_ge(lo_ready, ONE + T - 1)
                    sp.dma_start(wst[T % 2][:, :, :], d["w_in"][T]).then_inc(w_in[T % 2], 16)
                for n in range(4 * HP):
                    sp.wait_ge(sm_act, ONE + n + 1)
                    sp.dma_start(d["s_g"][n // 4, :, 512 * (n % 4):512 * (n % 4) + 512],
                                 gout[n % 2][:, :]).then_inc(g_out[n % 2], 16)
                for n in range(2):
                    sp.wait_ge(g_out[n], ONE + 16 * 2 * HP)

            @block.gpsimd
            def _(pool):
                nc.gpsimd.memset(lst[:, :, :], 0.0).then_inc(zeroed, 1)
                nc.gpsimd.memset(raw[:, 0:1], 0.0).then_inc(prep, 1)
                nc.gpsimd.memset(raw[:, S + 1:S + 2], 0.0).then_inc(prep, 1)
                nc.gpsimd.memset(tmp[:, 0:1], 0.0).then_inc(prep, 1)
                nc.gpsimd.memset(tmp[:, S + 1:S + 2], 0.0).then_inc(prep, 1)

            @block.scalar
            def _(act):
                def split_hi(T):
                    act.wait_ge(w_in[T % 2], ONE + 16 * (T // 2 + 1))
                    if T >= 2:
                        act.wait_ge(blk_done, ONE + NB * (T - 1))
                    nc.scalar.activation(w_hi[T % 2][:, :, :], wst[T % 2][:, :, :], ACT.Copy,
                                         scale=WS).then_inc(hi_ready, 1)

                split_hi(0)
                act.wait_ge(lw_in, ONE + 16 * 6)
                nc.scalar.activation(lw_hi[:, :, :], lst[:, :, :], ACT.Copy, scale=WS).then_inc(lsplit_hi, 1)
                nc.scalar.activation(lg_hi[:, 0, :], gst[:, 0, :], ACT.Copy, scale=WS).then_inc(lsplit_hi, 1)
                nc.scalar.activation(lg_hi[0:GR, 1, :], gst[0:GR, 1, :], ACT.Copy, scale=WS).then_inc(lsplit_hi, 1)
                for T in range(3):
                    split_hi(T + 1)
                    rows = P if T < T_G1 else GR
                    act.wait_ge(raw_free, ONE + T)
                    for b in range(NB):
                        act.wait_ge(blk_done, ONE + NB * T + b + 1)
                        nc.scalar.activation(raw[0:rows, 1 + 512 * b:513 + 512 * b],
                                             ring[(NB * T + b) % 6][0:rows, :], ACT.Copy,
                                             scale=1 / WS).then_inc(act_left, 1)
                    act.wait_ge(shifted, ONE + T + 1)
                    if T == T_WA:
                        nc.scalar.activation(act_t[0:64, :], tmp[0:64, 1:S + 1], ACT.Tanh).then_inc(act_own, 1)
                        nc.scalar.activation(act_t[64:128, :], tmp[64:128, 1:S + 1], ACT.Copy).then_inc(act_own, 1)
                        act.wait_ge(act_own, ONE + 2)
                        nc.scalar.activation(xwa_hi[:, :], act_t[:, :], ACT.Copy).then_inc(bent, 1)
                    else:
                        act.wait_ge(bent_lo, ONE + T)
                        nc.scalar.activation(act_t[0:rows, :], tmp[0:rows, 1:S + 1],
                                             ACT.Sigmoid).then_inc(act_own, 1)
                        act.wait_ge(act_own, ONE + T + 2)
                        nc.scalar.activation(sg_hi[0:rows, T - 1, :], act_t[0:rows, :], ACT.Copy).then_inc(bent, 1)
                for n in range(4 * HP):
                    act.wait_ge(sm_done, ONE + n + 1)
                    if n >= 2:
                        act.wait_ge(g_out[n % 2], ONE + 16 * (n // 2))
                    nc.scalar.activation(gout[n % 2][:, :], small[n % 2][:, :], ACT.Copy,
                                         scale=1 / WS).then_inc(sm_act, 1)

            @block.vector
            def _(dve):
                own = Chain(dve, dve_own)

                def split_lo(T):
                    dve.wait_ge(hi_ready, ONE + T + 1)
                    nc.vector.scalar_tensor_tensor(out=w_lo[T % 2][:, :, :], in0=wst[T % 2][:, :, :], scalar=WS,
                                                   in1=w_hi[T % 2][:, :, :], op0=ALU.mult,
                                                   op1=ALU.subtract).then_inc(lo_ready, 1)

                dve.wait_ge(const_in, ONE + 32)
                nc.vector.tensor_scalar(half[:, :], chan[:, :], 0.5, None, ALU.mult).then_inc(prep, 1)
                nc.vector.tensor_scalar(rest[:, :], chan[:, :], -1.0, 1.0, ALU.mult, ALU.add).then_inc(prep, 1)
                split_lo(0)
                for n, (lo, st, hi) in enumerate(((lw_lo[:, :, :], lst[:, :, :], lw_hi[:, :, :]),
                                                  (lg_lo[:, 0, :], gst[:, 0, :], lg_hi[:, 0, :]),
                                                  (lg_lo[0:GR, 1, :], gst[0:GR, 1, :], lg_hi[0:GR, 1, :]))):
                    dve.wait_ge(lsplit_hi, ONE + n + 1)
                    nc.vector.scalar_tensor_tensor(out=lo, in0=st, scalar=WS, in1=hi, op0=ALU.mult,
                                                   op1=ALU.subtract).then_inc(lsplit_lo, 1)
                dve.wait_ge(prep, ONE + 6)
                for T in range(3):
                    split_lo(T + 1)
                    rows = P if T < T_G1 else GR
                    mu = MU_WA + T
                    dve.wait_ge(act_left, ONE + NB * (T + 1))
                    if T >= 1:
                        dve.wait_ge(act_own, ONE + T + 1)
                    own.link(nc.vector.tensor_tensor(tmp[0:rows, 1:S + 1], raw[0:rows, 0:S], raw[0:rows, 2:S + 2], ALU.add))
                    own.link(nc.vector.tensor_scalar(tmp[0:rows, 1:S + 1], tmp[0:rows, 1:S + 1],
                                                     half[0:rows, mu:mu + 1], None, ALU.mult))
                    own.link(nc.vector.scalar_tensor_tensor(
                        out=tmp[0:rows, 1:S + 1], in0=raw[0:rows, 1:S + 1], scalar=rest[0:rows, mu:mu + 1],
                        in1=tmp[0:rows, 1:S + 1], op0=ALU.mult, op1=ALU.add))
                    nc.vector.sem_inc(raw_free, 1)
                    nc.vector.sem_inc(shifted, 1)
                    dve.wait_ge(bent, ONE + T + 1)
                    lo, hi = (xwa_lo[:, :], xwa_hi[:, :]) if T == T_WA else (sg_lo[0:rows, T - 1, :], sg_hi[0:rows, T - 1, :])
                    nc.vector.tensor_tensor(lo, act_t[0:rows, :], hi, ALU.subtract).then_inc(bent_lo, 1)

            @block.tensor
            def _(pe):
                def free_wait(n):
                    if n >= 6:
                        pe.wait_ge(act_left, ONE + n - 5)

                for T in range(3):
                    pe.wait_ge(hi_ready, ONE + T + 1)
                    pe.wait_ge(lo_ready, ONE + T + 1)
                    for b in range(NB):
                        free_wait(NB * T + b)
                        big_block(pe, T % 2, NB * T + b, b)
                pe.wait_ge(bent_lo, ONE + 3)
                pe.wait_ge(lsplit_lo, ONE + 3)
                for hp in range(HP):
                    ch = slice(P * hp, P * hp + P)
                    for b in range(NB):
                        n = NB * hp + b
                        tok = slice(512 * b, 512 * b + 512)
                        if n >= 2:
                            pe.wait_ge(sm_act, ONE + n - 1)
                        for g, rows in ((0, P), (1, GR)):
                            for lw, sgt in ((lg_hi, sg_hi), (lg_hi, sg_lo), (lg_lo, sg_hi)):
                                ins = nc.tensor.matmul(small[n % 2][:, :], lw[0:rows, g, ch], sgt[0:rows, g, tok],
                                                       start=(g == 0 and lw is lg_hi and sgt is sg_hi),
                                                       stop=(g == 1 and lw is lg_lo))
                        ins.then_inc(sm_done, 1)

        with ExitStack() as st2:
            s2 = Scope(nc, st2, "ip1")
            R, K, V, KK = (s2.sb(n, [P, S]) for n in ("R", "K", "V", "KK"))
            sg = [s2.sb(f"s{x}", [P, 512]) for x in range(2)]
            cum = [s2.sb(f"cum{x}", [P, 512]) for x in range(2)]
            rate = [s2.sb(f"rate{x}", [P, 512]) for x in range(2)]
            kd = [s2.sb(f"kd{x}", [P, 512]) for x in range(2)]
            bb = [s2.sb(f"bb{x}", [P, 512]) for x in range(2)]
            keep = s2.sb("keep", [P, 512], F16)
            r_st, kk_st, v_st = s2.sem("r_st"), s2.sem("kk_st"), s2.sem("v_st")
            r_ready, v_ready, kk_ready = s2.sem("r_ready"), s2.sem("v_ready"), s2.sem("kk_ready")
            kraw_ready, sq_ready = s2.sem("kraw_ready"), s2.sem("sq_ready")
            cum_ready, kd_ready, bb_ready = s2.sem("cum_ready"), s2.sem("kd_ready"), s2.sem("bb_ready")
            cum_st, kd_st, bb_st = ([s2.sem(f"{n}_st{x}") for x in range(2)] for n in ("cum", "kd", "bb"))
            sg_read, rate_read = s2.sem("sg_read"), s2.sem("rate_read")
            q_ready, bonus_ready = s2.sem("q_ready"), s2.sem("bonus_ready")
            bonus_st = s2.sem("bonus_st")
            conv_free = s2.sem("conv_free")
            o_ready, o_hi = s2.sem("o_ready"), s2.sem("o_hi")
            tmp_read = s2.sem("tmp_read")
            keep_in = s2.sem("keep_in")
            block = st2.enter_context(nc.Block())
            nt = len(TILES)
            DVE_STEPS = 76

            @block.sync
            def _(sp):
                s2.start_at_one(sp)
                sp.dma_start(keep[:, :], d["keep"]).then_inc(keep_in, 16)
                with sp.Fori(0, HP) as i:
                    def load(m):
                        T = T_LOOP + 1 + m + nt * i
                        s = (T_LOOP + 1 + m) % 2
                        sp.wait_ge(hi_ready, ONE + T - 1)
                        sp.wait_ge(lo_ready, ONE + T - 1)
                        sp.dma_start(wst[s][:, :, :], d["w_in"][T]).then_inc(w_in[s], 16)

                    load(0)
                    load(1)
                    load(2)
                    sp.wait_ge(r_ready, ONE + i + 1)
                    sp.dma_start(d["s_r"][i], R[:, :]).then_inc(r_st, 16)
                    load(3)
                    load(4)
                    sp.wait_ge(kk_ready, ONE + i + 1)
                    sp.dma_start(d["s_kk"][i], KK[:, :]).then_inc(kk_st, 16)
                    sp.wait_ge(v_ready, ONE + i + 1)
                    sp.dma_start(d["s_v"][i], V[:, :]).then_inc(v_st, 16)
                    load(5)
                    for b in range(NB):
                        tok = slice(512 * b, 512 * b + 512)
                        for x in range(2):
                            n = 2 * NB * i + 2 * b + x + 1
                            sp.wait_ge(cum_ready, ONE + n)
                            sp.dma_start(d["s_cum"][x, i][:, tok], cum[x][:, :]).then_inc(cum_st[x], 16)
                            sp.wait_ge(kd_ready, ONE + n)
                            sp.dma_start(d["s_kd"][x, i][:, tok], kd[x][:, :]).then_inc(kd_st[x], 16)
                            sp.wait_ge(bb_ready, ONE + n)
                            sp.dma_start(d["s_b"][x, i][:, tok], bb[x][:, :]).then_inc(bb_st[x], 16)
                    sp.wait_ge(bonus_ready, ONE + i + 1)
                    sp.dma_start(d["s_bonus"][i], V[:, :]).then_inc(bonus_st, 16)
                for sem in (r_st, v_st, kk_st, bonus_st):
                    sp.wait_ge(sem, ONE + 16 * HP)
                for sem in (*cum_st, *kd_st, *bb_st):
                    sp.wait_ge(sem, ONE + 16 * HP * NB)

            @block.scalar
            def _(act):
                with act.Fori(0, HP) as i:
                    def split_hi(m):
                        s = (T_LOOP + 1 + m) % 2
                        act.wait_ge(w_in[s], ONE + 16 * ((T_LOOP + 1 + m) // 2 + 1) + 16 * (nt // 2) * i)
                        act.wait_ge(blk_done, ONE + NB * (T_LOOP + m + nt * i))
                        nc.scalar.activation(w_hi[s][:, :, :], wst[s][:, :, :], ACT.Copy,
                                             scale=WS).then_inc(hi_ready, 1)

                    for m, name in enumerate(TILES):
                        T = T_LOOP + 1 + m + nt * i
                        if name != "h":
                            split_hi(m)
                        if name in "rkv":
                            if name == "r":
                                act.wait_ge(sm_dve, ONE + NB * i + NB)
                            act.wait_ge(raw_free, ONE + 3 + 3 * i + m)
                        if name == "c":
                            act.wait_ge(conv_free, ONE + i)
                        if name in "rkvc":
                            for b in range(NB):
                                dst = Cb[:, 512 * b:512 * b + 512] if name == "c" else raw[:, 1 + 512 * b:513 + 512 * b]
                                act.wait_ge(blk_done, ONE + NB * (T - 1) + b + 1)
                                nc.scalar.activation(dst, ring[(NB * m + b) % 6][:, :], ACT.Copy,
                                                     scale=1 / WS).then_inc(act_left, 1)
                        if name == "k":
                            act.wait_ge(kraw_ready, ONE + i + 1)
                            nc.scalar.activation(tmp[:, 1:S + 1], KK[:, :], ACT.Square).then_inc(sq_ready, 1)
                        if name == "v":
                            for b in range(NB):
                                act.wait_ge(sm_done, ONE + 4 * HP + 24 * i + b + 1)
                                nc.scalar.activation(tmp[:, 1 + 512 * b:513 + 512 * b], small[b % 2][:, :],
                                                     ACT.Sqrt).then_inc(sm_act, 1)
                        if name == "c":
                            split_hi(m + 1)
                            for b in range(NB):
                                for x in range(2):
                                    n = 2 * NB * i + 2 * b + x
                                    j = NB + 4 * b + 2 * x
                                    act.wait_ge(sg_read, ONE + n + 1)
                                    alone(act, sm_done, 4 * HP + 24 * i + j + 1)
                                    nc.scalar.activation(sg[x][:, :], small[j % 2][:, :], ACT.Sigmoid, scale=1 / WS,
                                                         bias=chan[:, bass.ds(i * NPC + W0_F + x, 1)]).then_inc(sm_act, 1)
                                    act.wait_ge(rate_read, ONE + n + 1)
                                    alone(act, sm_done, 4 * HP + 24 * i + j + 2)
                                    nc.scalar.activation(rate[x][:, :], small[(j + 1) % 2][:, :], ACT.Sigmoid, scale=1 / WS,
                                                         bias=chan[:, bass.ds(i * NPC + A0_F + x, 1)]).then_inc(sm_act, 1)
                        if name == "b":
                            for b in range(NB):
                                act.wait_ge(o_ready, ONE + NB * i + b + 1)
                                nc.scalar.activation(oc_hi[:, i, 512 * b:512 * b + 512], Cb[:, 512 * b:512 * b + 512],
                                                     ACT.Copy).then_inc(o_hi, 1)

            @block.vector
            def _(dve):
                dve.sem_inc(dve_left, 2 * NB)
                dve.sem_inc(sm_dve, NB)
                dve.sem_inc(sg_read, 2)
                dve.sem_inc(rate_read, 2)
                dve.wait_ge(keep_in, ONE + 16)
                with dve.Fori(0, HP) as i:
                    own = Chain(dve, dve_own, 9 + DVE_STEPS * i)

                    def col(arr, c):
                        return arr[:, bass.ds(i * NPC + c, 1)]

                    def split_lo(m):
                        s = (T_LOOP + 1 + m) % 2
                        dve.wait_ge(hi_ready, ONE + T_LOOP + 2 + m + nt * i)
                        nc.vector.scalar_tensor_tensor(out=w_lo[s][:, :, :], in0=wst[s][:, :, :], scalar=WS,
                                                       in1=w_hi[s][:, :, :], op0=ALU.mult,
                                                       op1=ALU.subtract).then_inc(lo_ready, 1)

                    def shift(m, dst, mu):
                        dve.wait_ge(act_left, ONE + 3 * NB + 4 * NB * i + NB * (m + 1))
                        own.link(nc.vector.tensor_tensor(tmp[:, 1:S + 1], raw[:, 0:S], raw[:, 2:S + 2], ALU.add))
                        own.link(nc.vector.tensor_scalar(dst[:, :], raw[:, 1:S + 1], col(rest, mu), None, ALU.mult))
                        nc.vector.sem_inc(raw_free, 1)
                        own.link(nc.vector.scalar_tensor_tensor(out=dst[:, :], in0=tmp[:, 1:S + 1], scalar=col(half, mu),
                                                                in1=dst[:, :], op0=ALU.mult, op1=ALU.add))

                    split_lo(0)
                    dve.wait_ge(r_st, ONE + 16 * i)
                    shift(0, R, MU_R)
                    nc.vector.sem_inc(r_ready, 1)
                    split_lo(1)
                    shift(1, K, MU_K)
                    dve.wait_ge(kk_st, ONE + 16 * i)
                    own.link(nc.vector.tensor_scalar(KK[:, :], K[:, :], col(chan, K_K), None, ALU.mult))
                    nc.vector.sem_inc(kraw_ready, 1)
                    split_lo(2)
                    dve.wait_ge(bonus_st, ONE + 16 * i)
                    dve.wait_ge(sm_act, ONE + 4 * HP + 20 * i + NB)
                    own.link(nc.vector.tensor_scalar(tmp[:, 1:S + 1], tmp[:, 1:S + 1], NORM_EPS, None, ALU.max))
                    split_lo(3)
                    own.link(nc.vector.reciprocal(tmp[:, 1:S + 1], tmp[:, 1:S + 1]))
                    own.link(nc.vector.tensor_tensor(KK[:, :], KK[:, :], tmp[:, 1:S + 1], ALU.mult))
                    nc.vector.sem_inc(kk_ready, 1)
                    shift(2, V, MU_V)
                    nc.vector.sem_inc(v_ready, 1)
                    split_lo(4)
                    for b in range(NB):
                        tok = slice(512 * b, 512 * b + 512)
                        ptok = slice(1 + 512 * b, 513 + 512 * b)
                        for x in range(2):
                            n = 2 * NB * i + 2 * b + x
                            j = NB + 4 * b + 2 * x
                            dve.wait_ge(cum_st[x], ONE + 16 * (NB * i + b))
                            dve.wait_ge(sm_act, ONE + 4 * HP + 20 * i + j + 1)
                            way = slice(None, None, -1) if x else slice(None)
                            own.link(nc.vector.tensor_tensor_scan(
                                out=cum[x][:, way], data0=keep[:, :], data1=sg[x][:, way],
                                initial=0.0, op0=ALU.mult, op1=ALU.add))
                            nc.vector.sem_inc(cum_ready, 1)
                            nc.vector.sem_inc(sg_read, 1)
                            dve.wait_ge(sm_act, ONE + 4 * HP + 20 * i + j + 2)
                            dve.wait_ge(kd_st[x], ONE + 16 * (NB * i + b))
                            own.link(nc.vector.tensor_scalar(kd[x][:, :], rate[x][:, :], col(chan, KA_F + x),
                                                             col(rest, KA_F + x), ALU.mult, ALU.add))
                            own.link(nc.vector.tensor_tensor(kd[x][:, :], kd[x][:, :], K[:, tok], ALU.mult))
                            nc.vector.sem_inc(kd_ready, 1)
                            dve.wait_ge(bb_st[x], ONE + 16 * (NB * i + b))
                            own.link(nc.vector.tensor_tensor(bb[x][:, :], KK[:, tok], rate[x][:, :], ALU.mult))
                            nc.vector.sem_inc(bb_ready, 1)
                            nc.vector.sem_inc(rate_read, 1)
                            if x == 0:
                                own.link(nc.vector.tensor_scalar(Q[:, ptok], kd[x][:, :], col(chan, RK_F), None, ALU.mult))
                            else:
                                own.link(nc.vector.scalar_tensor_tensor(
                                    out=Q[:, ptok], in0=kd[x][:, :], scalar=col(chan, RK_B), in1=Q[:, ptok],
                                    op0=ALU.mult, op1=ALU.add))
                        own.link(nc.vector.tensor_tensor(Q[:, ptok], Q[:, ptok], R[:, tok], ALU.mult))
                        nc.vector.sem_inc(q_ready, 1)
                        dve.wait_ge(blk_done, ONE + NB * (T_LOOP + nt * i + 4) + b + 1)
                        dve.wait_ge(act_left, ONE + 3 * NB + 4 * NB * i + 3 * NB + b + 1)
                        own.link(nc.vector.scalar_tensor_tensor(
                            out=tmp[:, ptok], in0=ring[(NB * 4 + b) % 6][:, :], scalar=1 / WS, in1=Cb[:, tok],
                            op0=ALU.mult, op1=ALU.mult))
                        nc.vector.sem_inc(dve_left, 1)
                    split_lo(5)
                    own.link(nc.vector.tensor_scalar(Cb[:, :], tmp[:, 0:S], col(chan, CW0), None, ALU.mult))
                    for t in (1, 2):
                        own.link(nc.vector.scalar_tensor_tensor(out=Cb[:, :], in0=tmp[:, t:S + t], scalar=col(chan, CW0 + t),
                                                                in1=Cb[:, :], op0=ALU.mult, op1=ALU.add))
                    for b in range(NB):
                        tok = slice(512 * b, 512 * b + 512)
                        dve.wait_ge(blk_done, ONE + NB * (T_LOOP + nt * i + 5) + b + 1)
                        own.link(nc.vector.scalar_tensor_tensor(
                            out=Cb[:, tok], in0=ring[(NB * 5 + b) % 6][:, :], scalar=1 / WS, in1=Cb[:, tok],
                            op0=ALU.mult, op1=ALU.mult))
                        nc.vector.sem_inc(dve_left, 1)
                        nc.vector.sem_inc(o_ready, 1)
                        if b == 0:
                            dve.wait_ge(v_st, ONE + 16 * i + 16)
                        dve.wait_ge(sm_done, ONE + 4 * HP + 24 * i + 20 + b + 1)
                        own.link(nc.vector.tensor_tensor(V[:, tok], V[:, tok], small[b % 2][:, :], ALU.mult))
                        nc.vector.sem_inc(sm_dve, 1)
                    nc.vector.sem_inc(bonus_ready, 1)
                    for b in range(NB):
                        tok = slice(512 * b, 512 * b + 512)
                        dve.wait_ge(o_hi, ONE + NB * i + b + 1)
                        own.link(nc.vector.tensor_tensor(oc_lo[:, i, tok], Cb[:, tok], oc_hi[:, i, tok], ALU.subtract))
                    nc.vector.sem_inc(conv_free, 1)
                    assert own.n == DVE_STEPS

            @block.tensor
            def _(pe):
                pe.wait_ge(act_left, ONE + 3 * NB)
                pe.wait_ge(sm_act, ONE + 4 * HP)
                with pe.Fori(0, HP) as i:
                    def ring_free(n):
                        q = n - 6
                        if q < 0:
                            pe.wait_ge(dve_left, ONE + 2 * NB * i + 2 * NB + q + 1)
                        elif q < 4 * NB:
                            pe.wait_ge(act_left, ONE + 3 * NB + 4 * NB * i + q + 1)
                        else:
                            pe.wait_ge(dve_left, ONE + 2 * NB * i + 2 * NB + q - 4 * NB + 1)

                    def small_free(j):
                        q = j - 2
                        if q < 0:
                            pe.wait_ge(sm_dve, ONE + NB * i + NB + q + 1)
                        elif q < 20:
                            pe.wait_ge(sm_act, ONE + 4 * HP + 20 * i + q + 1)
                        else:
                            pe.wait_ge(sm_dve, ONE + NB * i + NB + q - 20 + 1)

                    def lora(b):
                        tok = slice(512 * b, 512 * b + 512)
                        for x in range(2):
                            for kind in range(2):
                                j = NB + 4 * b + 2 * x + kind
                                small_free(j)
                                for lw, xt in ((lw_hi, xwa_hi), (lw_hi, xwa_lo), (lw_lo, xwa_hi)):
                                    ins = nc.tensor.matmul(
                                        small[j % 2][:, :], lw[:, 2 * kind + x, bass.ds(i * P, P)], xt[:, tok],
                                        start=(lw is lw_hi and xt is xwa_hi), stop=lw is lw_lo)
                                ins.then_inc(sm_done, 1)

                    for m, name in enumerate(TILES):
                        pe.wait_ge(hi_ready, ONE + T_LOOP + m + nt * i + 1)
                        pe.wait_ge(lo_ready, ONE + T_LOOP + m + nt * i + 1)
                        for b in range(NB):
                            if name == "h":
                                lora(b)
                            ring_free(NB * m + b)
                            big_block(pe, (T_LOOP + m) % 2, NB * m + b, b)
                            if name == "b":
                                j = 20 + b
                                small_free(j)
                                pe.wait_ge(q_ready, ONE + NB * i + b + 1)
                                nc.tensor.matmul(small[j % 2][:, :], ones[:, :], Q[:, 1 + 512 * b:513 + 512 * b],
                                                 start=True, stop=True).then_inc(sm_done, 1)
                        if name == "v":
                            pe.wait_ge(sq_ready, ONE + i + 1)
                            for b in range(NB):
                                small_free(b)
                                nc.tensor.matmul(small[b % 2][:, :], ones[:, :], tmp[:, 1 + 512 * b:513 + 512 * b],
                                                 start=True, stop=True).then_inc(sm_done, 1)


def phase_scan(nc, d, y):
    with ExitStack() as stack:
        sc = Scope(nc, stack, "scan")
        NA, UN = 6, HP
        A_R, A_KK, A_V, A_CUM, A_KD, A_B = range(NA)
        LV = 6
        win = [sc.sb(f"win{w}", [P, NA, 2, UN, 2 * C]) for w in range(2)]

        def pair(name, shape, dt=F32):
            return [sc.sb(f"{name}{x}", shape, dt) for x in range(2)]

        def quad(name, shape, dt=F32):
            return [pair(f"{name}{q}_", shape, dt) for q in range(2)]

        E = pair("E", [P, UN, C + 1])
        Ei = pair("Ei", [P, UN, C])
        kkr = pair("kkr", [P, UN, 2, C])
        bk = pair("bk", [P, 2, UN, 2, C])
        Nh, Nl = pair("Nh", [P, UN, P], F16), pair("Nl", [P, UN, P], F16)
        X, Xbd = pair("X", [P, UN, C], F16), pair("Xbd", [P, UN, P], F16)
        GV, Vbd = pair("GV", [P, 2, UN, C], F16), pair("Vbd", [P, UN, P], F16)
        Sx, Xs = pair("Sx", [P, UN, C]), pair("Xs", [P, UN, C])
        Q = quad("Q", [P, 2, UN, 2, C])
        Rz = quad("Rz", [P, 2, UN, C])
        BT = quad("BT", [P, 2, UN, C])
        Z = quad("Z", [P, 2, UN, C])
        TI = quad("TI", [P, UN, P])
        St = quad("St", [P, UN, C])
        lam = quad("lam", [P, UN, 1])
        idn = sc.sb("ident", [P, P])
        idh = sc.sb("identh", [P, P], F16)
        ids = sc.sb("idents", [P, C], F16)
        mA = sc.sb("maskA", [P, 2, 2, C])
        mL = sc.sb("maskL", [P, 2, LV, C])
        ring = [[sc.ps(f"ring{x}{n}") for n in range(2)] for x in range(2)]
        pg = [sc.ps(f"pg{x}", (P, 2, UN, C)) for x in range(2)]
        px = [t[:, 0] for t in pg]
        py = [ring[x][0][:, 0:UN * C].rearrange("p (u k) -> p u k", u=UN) for x in range(2)]
        pq = [sc.ps(f"pq{x}", (P, UN, C)) for x in range(2)]

        const_in, zeroed, dve_own = sc.sem("const_in"), sc.sem("zeroed"), sc.sem("dve_own")
        win_in = [sc.sem(f"win_in{w}") for w in range(2)]
        exps, decayed_done, raised_done = (sc.sem(n) for n in ("exps", "decayed", "raised"))
        r_placed, kk_placed = sc.sem("r_placed"), sc.sem("kk_placed")
        turned, halfway, t_left = sc.sem("turned"), sc.sem("halfway"), sc.sem("t_left")
        a_done, a_left = sc.sem("a_done"), sc.sem("a_left")
        nh_done, nl_done = sc.sem("nh_done"), sc.sem("nl_done")
        x_done, x_left, xbd_done = sc.sem("x_done"), sc.sem("x_left"), sc.sem("xbd_done")
        gv_done, gv_left, vbd_done = sc.sem("gv_done"), sc.sem("gv_left"), [sc.sem(f"vbd_done{x}") for x in range(2)]
        res_done, res_left, rbd_done = sc.sem("res_done"), sc.sem("res_left"), sc.sem("rbd_done")
        dv_done, inv_done = sc.sem("dv_done"), sc.sem("inv_done")
        sx_done, sx_left = sc.sem("sx_done"), sc.sem("sx_left")
        su_done, su_left = sc.sem("su_done"), sc.sem("su_left")
        ss_done, s_placed = sc.sem("ss_done"), sc.sem("s_placed")
        sy_done, sy_left = sc.sem("sy_done"), sc.sem("sy_left")
        N_CONST = 5
        heads = (slice(0, C), slice(C, P))
        zero = (*bk, *Nh, *Nl, *Xbd, *Vbd, *Q[0], *Q[1], *Rz[0], *Rz[1], *TI[0], *TI[1], *St[1], *Z[1], *BT[1], *lam[1])
        N_ZERO = len(zero) + 2 + UN
        block = stack.enter_context(nc.Block())

        def steps(eng, prep, step, last_run):
            prep(0, 0, 0)
            with eng.Fori(0, NCH // 4) as i:
                for s in range(4):
                    step(4 * i + s, s, prep(4 * i + s + 1, (s + 1) % 4, i + (s + 1) // 4, now=False))
            last_run(NCH)

        def cols(s, x):
            q = s % 2
            return slice(C * q, C * q + C) if x == 0 else slice(C * (1 - q), C * (1 - q) + C)

        @block.sync
        def _(sp):
            sc.start_at_one(sp)
            for dst, src in ((idn, "ident"), (idh, "identh"), (ids, "idents"), (mA, "maskA"), (mL, "maskL")):
                sp.dma_start(dst[tuple(slice(None) for _ in dst.shape)], d[src]).then_inc(const_in, 16)

            def load(w, it):
                for x, tok in ((0, it * (2 * C)), (1, S - 2 * C - it * (2 * C))):
                    at = bass.ds(tok, 2 * C)
                    for a, src in ((A_R, d["s_r"]), (A_KK, d["s_kk"]), (A_V, d["s_v"]), (A_CUM, d["s_cum"][x]),
                                   (A_KD, d["s_kd"][x]), (A_B, d["s_b"][x])):
                        sp.dma_start(win[w][:, a, x, :, :],
                                     src.rearrange("h p t -> p h t")[:, :, at]).then_inc(win_in[w], 16)

            for w in range(2):
                load(w, w)
            with sp.Fori(1, NCH // 4) as i:
                for w in range(2):
                    done = 4 * i + 2 * w - 2
                    alone(sp, exps, 4 * done)
                    alone(sp, raised_done, 8 * done)
                    alone(sp, decayed_done, 6 * done)
                    alone(sp, turned, 4 * done)
                    load(w, 2 * i + w)
            sp.wait_ge(exps, ONE + 4 * (NCH - 2))
            sp.wait_ge(raised_done, ONE + 8 * (NCH - 2))
            sp.wait_ge(decayed_done, ONE + 6 * (NCH - 2))
            sp.wait_ge(turned, ONE + 4 * (NCH - 2))
            load(0, 0)

        @block.gpsimd
        def _(pool):
            for t in zero[0::2]:
                nc.gpsimd.memset(t[tuple(slice(None) for _ in t.shape)], 0.0).then_inc(zeroed, 1)
            for x in range(2):
                one = 0 if x == 0 else C
                nc.gpsimd.memset(E[x][:, :, one:one + 1], 1.0).then_inc(zeroed, 1)
            pool.wait_ge(zeroed, ONE + N_ZERO)

            def prep(cs, s, i, now=True):
                def place_r():
                    for x in range(2):
                        if not now:
                            alone(pool, sy_done, 2 * cs - 1 + x)
                        alone(pool, decayed_done, 6 * cs + 3 * x + 2)
                        for e, hs in enumerate(heads):
                            nc.gpsimd.tensor_copy(Rz[s % 2][x][hs, e, :, :], kkr[x][hs, :, 1, :]).then_inc(r_placed, 1)

                if now:
                    place_r()
                return place_r

            steps(pool, prep, lambda cs, s, place_r: place_r(), lambda cs: None)

        @block.scalar
        def _(act):
            act.wait_ge(zeroed, ONE + N_ZERO)

            def copy(dst, src, sem, scale=1.0):
                nc.scalar.activation(dst, src, ACT.Copy, scale=scale).then_inc(sem, 1)

            def run_x(cs):
                for x in range(2):
                    act.wait_ge(sx_done, ONE + 2 * cs + x + 1)
                    copy(Xs[x][:, :, :], pq[x][:, :, :], sx_left, -1.0)

            def run_u(cs, par):
                for x in range(2):
                    act.wait_ge(su_done, ONE + 2 * cs + x + 1)
                    for e, hs in enumerate(heads):
                        copy(Z[1 - par][x][hs, e, :, :], pq[x][hs, :, :], su_left)

            def prep(cs, s, i, now=True):
                w, par = s // 2, s % 2

                def decays():
                    if s % 2 == 0:
                        act.wait_ge(win_in[w], ONE + 16 * 2 * NA * (i + 1))
                    act.wait_ge(decayed_done, ONE + 6 * cs)
                    act.wait_ge(raised_done, ONE + 8 * cs)
                    for x in range(2):
                        at = slice(1, C + 1) if x == 0 else slice(0, C)
                        src = win[w][:, A_CUM, x, :, cols(s, x)]
                        nc.scalar.activation(E[x][:, :, at], src, ACT.Exp, scale=-DECAY).then_inc(exps, 1)
                        nc.scalar.activation(Ei[x][:, :, :], src, ACT.Exp, scale=DECAY).then_inc(exps, 1)

                def turn(x):
                    if not now:
                        act.wait_ge(sy_done, ONE + 2 * cs - 1 + x)
                    act.wait_ge(turned, ONE + 4 * cs + 2 * x + 1)
                    for e in range(2):
                        copy(Z[par][x][heads[1 - e], e, :, :],
                             ring[x][0][0:C, :].rearrange("p (u k) -> p u k", u=UN)[:, :, C * e:C * e + C], t_left)
                    act.wait_ge(turned, ONE + 4 * cs + 2 * x + 2)
                    copy(BT[par][x][:, :, :, :].rearrange("p e u k -> p (e u k)"), ring[x][1][:, :], t_left)

                if now:
                    decays()
                    for x in range(2):
                        turn(x)
                return decays, turn

            def step(cs, s, nxt):
                par = s % 2
                decays, turn = nxt

                def level(l):
                    for x in range(2):
                        act.wait_ge(gv_done, ONE + 12 * cs + 2 * l + x + 1)
                        copy(GV[x][:, :, :, :], pg[x][:, :, :, :], gv_left)

                decays()
                act.wait_ge(res_done, ONE + 2 * cs)
                for x in range(2):
                    for e, hs in enumerate(heads):
                        act.wait_ge(a_left, ONE + 4 + 4 * cs + 2 * x + e + 1)
                        copy(Nh[x][hs, :, C * e:C * e + C], Q[par][x][hs, e, :, 0, :], nh_done)
                run_x(cs)
                level(0)
                run_u(cs, par)
                for x in range(2):
                    for e, hs in enumerate(heads):
                        act.wait_ge(nl_done, ONE + 4 * cs + 2 * x + e + 1)
                        copy(Q[par][x][hs, e, :, 0, :], kkr[x][hs, :, 0, :], kk_placed)
                level(1)
                level(2)
                level(3)
                turn(0)
                level(4)
                turn(1)
                level(5)

            def last_run(cs):
                run_x(cs)
                run_u(cs, 0)

            steps(act, prep, step, last_run)

        @block.vector
        def _(dve):
            dve.sem_inc(a_left, 4)
            for t in (*zero[1::2], *(y[:, u, :] for u in range(UN))):
                nc.vector.memset(t[tuple(slice(None) for _ in t.shape)], 0.0).then_inc(zeroed, 1)
            dve.wait_ge(zeroed, ONE + N_ZERO)
            dve.wait_ge(const_in, ONE + 16 * N_CONST)

            def run_s(cs, par, own, x):
                alone(dve, ss_done, 2 * cs + x + 1)
                own.link(nc.vector.tensor_tensor(Sx[x][:, :, :], St[1 - par][x][:, :, :], pq[x][:, :, :], ALU.add))
                own.link(nc.vector.tensor_tensor(St[par][x][:, :, :], Sx[x][:, :, :],
                                                 lam[1 - par][x][:, :, :].broadcast_to((P, UN, C)), ALU.mult))
                for e, hs in enumerate(heads):
                    nc.vector.tensor_copy(Z[par][x][hs, e, :, :], St[par][x][hs, :, :]).then_inc(s_placed, 1)

            def run_y(cs, x):
                at = bass.ds(cs * C, C) if x == 0 else bass.ds((NCH + 1) * C - cs * C, C)
                alone(dve, sy_done, 2 * cs + x + 1)
                alone(dve, sy_left, 2 * cs + x)
                nc.vector.tensor_tensor(y[:, :, at], y[:, :, at], py[x][:, :, :], ALU.add).then_inc(sy_left, 1)

            def prep(cs, s, i, now=True):
                w, par = s // 2, s % 2

                def decayed(x):
                    if not now:
                        alone(dve, a_done, 4 * cs - 2 + 2 * x)
                        alone(dve, r_placed, 4 * cs - 2 + 2 * x)
                        alone(dve, kk_placed, 4 * cs - 2 + 2 * x)
                    if s % 2 == 0:
                        dve.wait_ge(win_in[w], ONE + 16 * 2 * NA * (i + 1))
                    c, end = cols(s, x), (1 - x) * C
                    upto, past = ((slice(1, C + 1), slice(0, C)) if x == 0 else
                                  (slice(0, C), slice(1, C + 1)))
                    g = win[w]
                    dve.wait_ge(exps, ONE + 4 * cs + 2 * x + 2)
                    nc.vector.tensor_tensor(kkr[x][:, :, 0, :], g[:, A_KK, x, :, c], E[x][:, :, past],
                                            ALU.mult).then_inc(decayed_done, 1)
                    nc.vector.tensor_tensor(kkr[x][:, :, 1, :], g[:, A_R, x, :, c], E[x][:, :, upto],
                                            ALU.mult).then_inc(decayed_done, 1)

                    nc.vector.tensor_copy(lam[par][x][:, :, :], E[x][:, :, end:end + 1]).then_inc(decayed_done, 1)

                def raised(x):
                    if not now:
                        alone(dve, turned, 4 * cs - 2 + 2 * x)
                    c, g = cols(s, x), win[w]
                    dve.wait_ge(exps, ONE + 4 * cs + 2 * x + 2)
                    for e, hs in enumerate(heads):
                        nc.vector.tensor_tensor(bk[x][hs, e, :, e, :], g[hs, A_B, x, :, c], Ei[x][hs, :, :],
                                                ALU.mult).then_inc(raised_done, 1)
                        nc.vector.tensor_tensor(bk[x][hs, e, :, 1 - e, :], g[hs, A_KD, x, :, c], Ei[x][hs, :, :],
                                                ALU.mult).then_inc(raised_done, 1)

                def scores(x):
                    if not now:
                        alone(dve, sy_done, 2 * cs - 1 + x)
                    mask = mA[:, x:x + 1, :, :].rearrange("p o a b -> p o (a b)").broadcast_to((P, UN, 2 * C))
                    for e in range(2):
                        dve.wait_ge(a_done, ONE + 4 * cs + 2 * x + e + 1)
                        nc.vector.tensor_tensor(Q[par][x][:, e, :, :, :].rearrange("p u a b -> p u (a b)"),
                                                ring[x][e][:, :].rearrange("p (u k) -> p u k", u=UN),
                                                mask, ALU.mult).then_inc(a_left, 1)

                if now:
                    for part in (decayed, raised, scores):
                        part(0)
                        part(1)
                return decayed, raised, scores

            def step(cs, s, nxt):
                par = s % 2
                decayed, raised, scores = nxt
                own = Chain(dve, dve_own, 4 * cs)

                def spread(dst, src, sem):
                    for h, hs in enumerate(heads):
                        nc.vector.tensor_copy(dst[hs, :, C * h:C * h + C], src[hs]).then_inc(sem, 1)

                def level(l):
                    def blocks(x):
                        dve.wait_ge(x_done, ONE + 12 * cs + 2 * l + x + 1)
                        nc.vector.tensor_tensor(X[x][:, :, :], px[x][:, :, :],
                                                mL[:, x, l:l + 1, :].broadcast_to((P, UN, C)), ALU.mult).then_inc(x_left, 1)

                    def spread_x(x):
                        dve.wait_ge(x_left, ONE + 12 * cs + 2 * l + x + 1)
                        spread(Xbd[x], X[x], xbd_done)

                    def spread_v(x):
                        if l:
                            dve.wait_ge(gv_left, ONE + 12 * cs + 2 * (l - 1) + x + 1)
                            spread(Vbd[x], GV[x][:, 1, :, :], vbd_done[x])

                    for x in range(2):
                        spread_v(x)
                        blocks(x)
                    for x in range(2):
                        spread_x(x)

                def split_n(x):
                    for h, hs in enumerate(heads):
                        dve.wait_ge(nh_done, ONE + 4 * cs + 2 * x + h + 1)
                        nc.vector.tensor_tensor(Nl[x][hs, :, C * h:C * h + C], Q[par][x][hs, h, :, 0, :],
                                                Nh[x][hs, :, C * h:C * h + C], ALU.subtract).then_inc(nl_done, 1)

                raised(0)
                level(0)
                split_n(0)
                split_n(1)
                level(1)
                run_s(cs, par, own, 0)
                level(2)
                run_s(cs, par, own, 1)
                run_y(cs, 0)
                level(3)
                decayed(0)
                raised(1)
                level(4)
                run_y(cs, 1)
                decayed(1)
                level(5)
                scores(0)
                for x in range(2):
                    dve.wait_ge(res_done, ONE + 2 * cs + x + 1)
                    nc.vector.tensor_tensor(X[x][:, :, :], ids[:, :].unsqueeze(1).broadcast_to((P, UN, C)),
                                            px[x][:, :, :], ALU.subtract).then_inc(res_left, 1)
                    dve.wait_ge(res_left, ONE + 2 * cs + x + 1)
                    spread(Xbd[x], X[x], rbd_done)
                scores(1)
                for x in range(2):
                    dve.wait_ge(dv_done, ONE + 2 * cs + x + 1)
                    for e, hs in enumerate(heads):
                        nc.vector.tensor_tensor(TI[par][x][hs, :, C * e:C * e + C], GV[x][hs, 1, :, :],
                                                pg[x][hs, 0, :, :], ALU.add).then_inc(inv_done, 1)

            def last_run(cs):
                own = Chain(dve, dve_own, 4 * cs)
                run_s(cs, 0, own, 0)
                run_s(cs, 0, own, 1)
                run_y(cs, 0)
                run_y(cs, 1)

            steps(dve, prep, step, last_run)
            dve.wait_ge(sy_left, ONE + 2 * NCH + 2)
            dve.wait_ge(s_placed, ONE + 4 * NCH + 4)

        @block.tensor
        def _(pe):
            pe.wait_ge(zeroed, ONE + N_ZERO)
            pe.wait_ge(const_in, ONE + 16 * N_CONST)

            def by_head(out, *terms):
                for e, hs in enumerate(heads):
                    for u in range(UN):
                        for n, (lhs, rhs) in enumerate(terms):
                            ins = nc.tensor.matmul(out[hs, u, :], lhs(e, u), rhs(e, u), start=n == 0,
                                                   stop=n == len(terms) - 1)
                return ins

            def run_x(cs, par, x):
                o = 1 - par
                if x == 0:
                    alone(pe, s_placed, 4 * cs)
                    alone(pe, kk_placed, 4 * cs)
                    alone(pe, t_left, 6 * cs)
                    alone(pe, sy_left, 2 * cs)
                by_head(pq[x], (lambda e, u: Q[o][x][:, e, u, 0, :], lambda e, u: Z[o][x][:, e, u, :])).then_inc(sx_done, 1)

            def run_u(cs, par, x):
                o = 1 - par
                alone(pe, sx_left, 2 * cs + x + 1)
                by_head(pq[x], (lambda e, u: TI[o][x][:, u, C * e:C * e + C], lambda e, u: Xs[x][:, u, :])).then_inc(su_done, 1)

            def run_s(cs, par, x):
                o = 1 - par
                alone(pe, su_left, 4 * cs + 2 * x + 2)
                by_head(pq[x], (lambda e, u: BT[o][x][:, e, u, :], lambda e, u: Z[o][x][:, e, u, :])).then_inc(ss_done, 1)

            def run_y(cs, par, x):
                o = 1 - par
                alone(pe, r_placed, 4 * cs)
                alone(pe, a_left, 4 * cs + 2 * x + 5)
                by_head(py[x], (lambda e, u: St[o][x][:, u, :], lambda e, u: Rz[o][x][:, e, u, :]),
                        (lambda e, u: Z[o][x][:, e, u, :], lambda e, u: Q[o][x][:, e, u, 1, :])).then_inc(sy_done, 1)

            def prep(cs, s, i, now=True):
                w, par = s // 2, s % 2

                def turn(x):
                    alone(pe, raised_done, 8 * cs + 4 * x + 4)
                    alone(pe, a_left, 4 * cs + 2 * x + 1)
                    if not now:
                        alone(pe, sy_left, 2 * cs - 1 + x)
                    for u in range(UN):
                        ins = nc.tensor.transpose(ring[x][0][0:C, P * u:P * u + P], win[w][:, A_V, x, u, cols(s, x)], idn[:, :])
                    ins.then_inc(turned, 1)
                    alone(pe, a_left, 4 * cs + 2 * x + 2)
                    for e, hs in enumerate(heads):
                        for u in range(UN):
                            at = C * (UN * e + u)
                            ins = nc.tensor.transpose(ring[x][1][:, at:at + C], bk[x][hs, e, u, :, :].rearrange("p a b -> p (a b)"),
                                                      idn[hs, hs])
                        if e == 0:
                            ins.then_inc(halfway, 1)
                            alone(pe, halfway, 2 * cs + x + 1)
                    ins.then_inc(turned, 1)

                def scores(x):
                    alone(pe, decayed_done, 6 * cs + 3 * x + 2)
                    for e in range(2):
                        alone(pe, t_left, 6 * cs + 3 * x + 2 + e)
                        for u in range(UN):
                            ins = nc.tensor.matmul(ring[x][e][:, P * u:P * u + P],
                                                   bk[x][:, e, u, :, :].rearrange("p a b -> p (a b)"),
                                                   kkr[x][:, u, :, :].rearrange("p a b -> p (a b)"), start=True, stop=True)
                        ins.then_inc(a_done, 1)

                if now:
                    for x in range(2):
                        turn(x)
                        scores(x)
                return turn, scores

            def step(cs, s, nxt):
                par = s % 2
                turn, scores = nxt

                def level_x(l):
                    for x in range(2):
                        if l == 0:
                            alone(pe, nh_done, 4 * cs + 2 * x + 2)
                        else:
                            alone(pe, gv_left, 12 * cs + 2 * (l - 1) + x + 1)
                        for u in range(UN):
                            g = GV[x][:, 0, u, :] if l else ids[:, :]
                            nc.tensor.matmul(px[x][:, u, :], idh[:, :], ids[:, :], start=True, stop=False)
                            ins = nc.tensor.matmul(px[x][:, u, :], Nh[x][:, u, :], g, start=False, stop=True)
                        ins.then_inc(x_done, 1)

                def level_g(l):
                    for x in range(2):
                        alone(pe, xbd_done, 24 * cs + 4 * l + 2 * x + 2)
                        if l:
                            alone(pe, vbd_done[x], 10 * cs + 2 * l)
                        for u in range(UN):
                            nc.tensor.matmul(pg[x][:, 0, u, :], Vbd[x][:, u, :] if l else idh[:, :], X[x][:, u, :],
                                             start=True, stop=True)
                            ins = nc.tensor.matmul(pg[x][:, 1, u, :], Xbd[x][:, u, :], GV[x][:, 1, u, :] if l else ids[:, :],
                                                   start=True, stop=True)
                        ins.then_inc(gv_done, 1)

                run_x(cs, par, 0)
                run_x(cs, par, 1)
                alone(pe, inv_done, 4 * cs)
                level_x(0)
                run_u(cs, par, 0)
                level_g(0)
                run_u(cs, par, 1)
                level_x(1)
                run_s(cs, par, 0)
                level_g(1)
                run_s(cs, par, 1)
                level_x(2)
                run_y(cs, par, 0)
                level_g(2)
                run_y(cs, par, 1)
                level_x(3)
                turn(0)
                level_g(3)
                level_x(4)
                scores(0)
                level_g(4)
                turn(1)
                level_x(5)
                scores(1)
                level_g(5)
                for x in range(2):
                    alone(pe, gv_left, 12 * cs + 2 * (LV - 1) + x + 1)
                    alone(pe, nl_done, 4 * cs + 2 * x + 2)
                    for u in range(UN):
                        for n, lhs in enumerate((Nh[x][:, u, :], Nl[x][:, u, :], idh[:, :])):
                            ins = nc.tensor.matmul(px[x][:, u, :], lhs, GV[x][:, 0, u, :], start=n == 0, stop=n == 2)
                    ins.then_inc(res_done, 1)
                for x in range(2):
                    alone(pe, rbd_done, 4 * cs + 2 * x + 2)
                    for u in range(UN):
                        ins = nc.tensor.matmul(pg[x][:, 0, u, :], Xbd[x][:, u, :], GV[x][:, 1, u, :], start=True, stop=True)
                    ins.then_inc(dv_done, 1)

            def last_run(cs):
                alone(pe, inv_done, 4 * cs)
                for run in (run_x, run_u, run_s, run_y):
                    for x in range(2):
                        run(cs, 0, x)

            steps(pe, prep, step, last_run)


def phase_groupnorm(nc, d, y, or_hi, or_lo, w_hi, w_lo, room):
    with ExitStack() as stack:
        sc = Scope(nc, stack, "gn")
        chan, ones = sc.sb("chan", [P, NCOL]), sc.sb("ones", [P, P])
        eps = sc.sb("eps", [P, 1])
        parts = [room[:, n // 2, 512 * (n % 2):512 * (n % 2) + 512] for n in range(4 * HP)]
        bon, gate = parts[0:HP], parts[HP:2 * HP]
        dev = parts[2 * HP:3 * HP]
        sq = parts[3 * HP:4 * HP]
        wst = [room[:, 2 * HP + k, :] for k in range(2)]
        pm = [sc.ps(f"mean{h}") for h in range(HP)]
        pv = [sc.ps(f"var{h}") for h in range(HP)]
        const_in, eps_set, ld = sc.sem("const_in"), sc.sem("eps_set"), sc.sem("ld")
        mean_done, dev_done, sq_done, var_done = (sc.sem(n) for n in ("mean_done", "dev_done", "sq_done", "var_done"))
        rooted, normed, scaled, o_done, hi_done, lo_done = (
            sc.sem(n) for n in ("rooted", "normed", "scaled", "o_done", "hi_done", "lo_done"))
        dve_own = sc.sem("dve_own")
        w_in, w_hi_done, w_lo_done = sc.sem("w_in"), sc.sem("w_hi_done"), sc.sem("w_lo_done")
        block = stack.enter_context(nc.Block())

        def tok(i):
            return bass.ds(i * 512, 512)

        @block.sync
        def _(sp):
            sc.start_at_one(sp)
            sp.dma_start(chan[:, :], d["chan"]).then_inc(const_in, 16)
            sp.dma_start(ones[:, :], d["ones"]).then_inc(const_in, 16)
            with sp.Fori(0, NB) as i:
                sp.wait_ge(w_lo_done, ONE + 2 * i)
                for k in range(2):
                    sp.dma_start(wst[k], d["w_out"][bass.ds((2 * i + k) * P, P), :]).then_inc(w_in, 16)
                for h in range(HP):
                    sp.wait_ge(o_done, ONE + HP * i)
                    sp.dma_start(bon[h][:, :], d["s_bonus"][h][:, tok(i)]).then_inc(ld, 16)
                    sp.dma_start(gate[h][:, :], d["s_g"][h][:, tok(i)]).then_inc(ld, 16)

        @block.gpsimd
        def _(pool):
            nc.gpsimd.memset(eps[:, :], GN_EPS).then_inc(eps_set, 1)

        @block.tensor
        def _(pe):
            pe.wait_ge(const_in, ONE + 32)
            with pe.Fori(0, NB) as i:
                for h in range(HP):
                    pe.wait_ge(dev_done, ONE + HP * i)
                    nc.tensor.matmul(pm[h][:, :], ones[:, :], y[:, h, bass.ds(i * 512 + C, 512)],
                                     start=True, stop=True).then_inc(mean_done, 1)
                for h in range(HP):
                    pe.wait_ge(rooted, ONE + HP * i)
                    pe.wait_ge(sq_done, ONE + HP * i + h + 1)
                    nc.tensor.matmul(pv[h][:, :], ones[:, :], sq[h][:, :], start=True, stop=True).then_inc(var_done, 1)

        @block.scalar
        def _(act):
            act.wait_ge(eps_set, ONE + 1)
            act.wait_ge(const_in, ONE + 32)
            with act.Fori(0, NB) as i:
                for h in range(HP):
                    act.wait_ge(dev_done, ONE + HP * i + h + 1)
                    nc.scalar.activation(sq[h][:, :], dev[h][:, :], ACT.Square).then_inc(sq_done, 1)
                for k in range(2):
                    act.wait_ge(w_in, ONE + 32 * i + 32)
                    nc.scalar.activation(w_hi[:, 2 * i + k, :], wst[k], ACT.Copy, scale=WS).then_inc(w_hi_done, 1)
                for h in range(HP):
                    act.wait_ge(var_done, ONE + HP * i + h + 1)
                    nc.scalar.activation(sq[h][:, :], pv[h][:, :], ACT.Sqrt, scale=1.0 / C,
                                         bias=eps[:, 0:1]).then_inc(rooted, 1)
                for h in range(HP):
                    act.wait_ge(normed, ONE + HP * i + h + 1)
                    nc.scalar.activation(dev[h][:, :], dev[h][:, :], ACT.Identity,
                                         scale=chan[:, h * NPC + GN_W:h * NPC + GN_W + 1],
                                         bias=chan[:, h * NPC + GN_B:h * NPC + GN_B + 1]).then_inc(scaled, 1)
                for h in range(HP):
                    act.wait_ge(o_done, ONE + HP * i + h + 1)
                    nc.scalar.activation(or_hi[:, h, tok(i)], dev[h][:, :], ACT.Copy).then_inc(hi_done, 1)

        @block.vector
        def _(dve):
            with dve.Fori(0, NB) as i:
                own = Chain(dve, dve_own, 2 * HP * i)
                for h in range(HP):
                    dve.wait_ge(mean_done, ONE + HP * i + h + 1)
                    dve.wait_ge(lo_done, ONE + HP * i)
                    nc.vector.scalar_tensor_tensor(out=dev[h][:, :], in0=pm[h][:, :], scalar=-1.0 / C,
                                                   in1=y[:, h, bass.ds(i * 512 + C, 512)], op0=ALU.mult,
                                                   op1=ALU.add).then_inc(dev_done, 1)
                for k in range(2):
                    dve.wait_ge(w_hi_done, ONE + 2 * i + k + 1)
                    nc.vector.scalar_tensor_tensor(out=w_lo[:, 2 * i + k, :], in0=wst[k], scalar=WS, in1=w_hi[:, 2 * i + k, :],
                                                   op0=ALU.mult, op1=ALU.subtract).then_inc(w_lo_done, 1)
                for h in range(HP):
                    dve.wait_ge(rooted, ONE + HP * i + h + 1)
                    own.link(nc.vector.reciprocal(sq[h][:, :], sq[h][:, :]))
                    nc.vector.tensor_tensor(dev[h][:, :], dev[h][:, :], sq[h][:, :], ALU.mult).then_inc(normed, 1)
                for h in range(HP):
                    dve.wait_ge(scaled, ONE + HP * i + h + 1)
                    dve.wait_ge(ld, ONE + 32 * HP * (i + 1))
                    own.link(nc.vector.tensor_tensor(dev[h][:, :], dev[h][:, :], bon[h][:, :], ALU.add))
                    nc.vector.tensor_tensor(dev[h][:, :], dev[h][:, :], gate[h][:, :], ALU.mult).then_inc(o_done, 1)
                for h in range(HP):
                    dve.wait_ge(hi_done, ONE + HP * i + h + 1)
                    nc.vector.tensor_tensor(or_lo[:, h, tok(i)], dev[h][:, :], or_hi[:, h, tok(i)],
                                            ALU.subtract).then_inc(lo_done, 1)


def phase_outproj(nc, d, hi, lo, w_hi, w_lo, x1, spare):
    with ExitStack() as stack:
        sc = Scope(nc, stack, "op")
        rows = [spare[:, n * D:n * D + D] for n in range(5)]
        xt, xn, wrow = rows[0:2], rows[2:4], rows[4]
        idn = sc.sb("ident", [P, P])
        ss = [sc.sb(f"ss{s}", [P, 4]) for s in range(2)]
        pp = [[sc.ps(f"p{s}{g}") for g in range(2)] for s in range(2)]
        pt = [[sc.ps(f"t{s}{g}", (P, 4, P)) for g in range(2)] for s in range(2)]
        const_in = sc.sem("const_in")
        x_in = [sc.sem(f"x_in{s}") for s in range(2)]
        proj, added, squared, rooted, scaled = (sc.sem(n) for n in ("proj", "added", "squared", "rooted", "scaled"))
        var_done, turned, hi_done, lo_done, dve_own = (sc.sem(n) for n in ("var_done", "turned", "hi_done", "lo_done", "dve_own"))
        block = stack.enter_context(nc.Block())

        def at(i, s):
            return bass.ds((2 * i + s) * P, P)

        @block.sync
        def _(sp):
            sc.start_at_one(sp)
            sp.dma_start(idn[:, :], d["ident"]).then_inc(const_in, 16)
            sp.dma_start(wrow[:, :], d["norm2_w"].partition_broadcast(P)).then_inc(const_in, 16)
            for s in range(2):
                sp.dma_start(xt[s][:, :], d["x"][s * P:(s + 1) * P, :]).then_inc(x_in[s], 16)
            with sp.Fori(1, TT // 2) as i:
                for s in range(2):
                    sp.wait_ge(added, ONE + 4 * i + 2 * s - 2)
                    sp.dma_start(xt[s][:, :], d["x"][at(i, s), :]).then_inc(x_in[s], 16)

        @block.scalar
        def _(act):

            def norms(i):
                for s in range(2):
                    act.wait_ge(added, ONE + 4 * i + 2 * s + 2)
                    act.wait_ge(turned, ONE + 4 * i)
                    nc.scalar.activation(xn[s][:, :], x1[:, 2 * i + s, :], ACT.Square,
                                         accum_out=ss[s][:, 0:1]).then_inc(squared, 1)
                    act.wait_ge(var_done, ONE + 2 * i + s + 1)
                    nc.scalar.activation(ss[s][:, 2:3], ss[s][:, 1:2], ACT.Sqrt).then_inc(rooted, 1)

            def split_hi(i):
                for s in range(2):
                    for g in range(2):
                        act.wait_ge(turned, ONE + 4 * i + 2 * s + g + 1)
                        nc.scalar.activation(hi[g][:, :, at(i, s)], pt[s][g][:, :, :], ACT.Copy).then_inc(hi_done, 1)

            norms(0)
            with act.Fori(1, TT // 2) as i:
                norms(i)
                split_hi(i - 1)
            split_hi(TT // 2 - 1)

        @block.vector
        def _(dve):
            dve.wait_ge(const_in, ONE + 32)

            def residual(i):
                own = Chain(dve, dve_own, 2 * i)
                for s in range(2):
                    dve.wait_ge(x_in[s], ONE + 16 * i + 16)
                    for g in range(2):
                        dve.wait_ge(proj, ONE + 4 * i + 2 * s + g + 1)
                        nc.vector.scalar_tensor_tensor(
                            out=x1[:, 2 * i + s, 512 * g:512 * g + 512], in0=pp[s][g][:, :], scalar=1 / WS,
                            in1=xt[s][:, 512 * g:512 * g + 512], op0=ALU.mult, op1=ALU.add).then_inc(added, 1)
                    dve.wait_ge(squared, ONE + 2 * i + s + 1)
                    nc.vector.tensor_scalar(ss[s][:, 1:2], ss[s][:, 0:1], 1.0 / D, RMS_EPS,
                                            ALU.mult, ALU.add).then_inc(var_done, 1)
                    dve.wait_ge(rooted, ONE + 2 * i + s + 1)
                    own.link(nc.vector.reciprocal(ss[s][:, 3:4], ss[s][:, 2:3]))
                    nc.vector.scalar_tensor_tensor(out=xn[s][:, :], in0=x1[:, 2 * i + s, :], scalar=ss[s][:, 3:4],
                                                   in1=wrow[:, :], op0=ALU.mult, op1=ALU.mult).then_inc(scaled, 1)

            def split_lo(i):
                for s in range(2):
                    for g in range(2):
                        dve.wait_ge(hi_done, ONE + 4 * i + 2 * s + g + 1)
                        nc.vector.tensor_tensor(lo[g][:, :, at(i, s)], pt[s][g][:, :, :], hi[g][:, :, at(i, s)],
                                                ALU.subtract).then_inc(lo_done, 1)

            residual(0)
            with dve.Fori(1, TT // 2) as i:
                residual(i)
                split_lo(i - 1)
            split_lo(TT // 2 - 1)

        @block.tensor
        def _(pe):
            pe.wait_ge(const_in, ONE + 32)

            def project(i):
                for s in range(2):
                    pe.wait_ge(added, ONE + 4 * i)
                    for g in range(2):
                        for k in range(KT):
                            for w, o in ((w_hi, hi), (w_lo, hi), (w_hi, lo)):
                                ins = nc.tensor.matmul(pp[s][g][:, :], o[k // 4][:, k % 4, at(i, s)],
                                                       w[:, k, 512 * g:512 * g + 512],
                                                       start=(k == 0 and w is w_hi and o is hi),
                                                       stop=(k == KT - 1 and o is lo))
                        ins.then_inc(proj, 1)

            def turn(i):
                pe.wait_ge(lo_done, ONE + 4 * i)
                for s in range(2):
                    pe.wait_ge(scaled, ONE + 2 * i + s + 1)
                    for g in range(2):
                        for k in range(4):
                            kt = 4 * g + k
                            ins = nc.tensor.transpose(pt[s][g][:, k, :], xn[s][:, kt * P:(kt + 1) * P], idn[:, :])
                        ins.then_inc(turned, 1)

            project(0)
            with pe.Fori(1, TT // 2) as i:
                project(i)
                turn(i - 1)
            turn(TT // 2 - 1)


def phase_ffn(nc, d, hi, lo, x1, spare):
    G = 2
    NG = FT // G
    with ExitStack() as stack:
        sc = Scope(nc, stack, "ff")
        st_g, st_u, st_d = (spare[:, n * 2 * D:n * 2 * D + 2 * D] for n in range(3))
        st_g, st_u = (t.rearrange("p (k n) -> p k n", k=KT) for t in (st_g, st_u))
        g_hi, g_lo = sc.sb("g_hi", [P, KT, G * P], F16), sc.sb("g_lo", [P, KT, G * P], F16)
        u_hi, u_lo = sc.sb("u_hi", [P, KT, G * P], F16), sc.sb("u_lo", [P, KT, G * P], F16)
        d_hi, d_lo = sc.sb("d_hi", [P, G, D], F16), sc.sb("d_lo", [P, G, D], F16)
        st_d = st_d.rearrange("p (g n) -> p g n", g=G)
        a_hi, a_lo = sc.sb("a_hi", [P, G, S], F16), sc.sb("a_lo", [P, G, S], F16)
        sig = [sc.sb(f"sig{n}", [P, 512]) for n in range(2)]
        pg, pu = [sc.ps(f"g{n}") for n in range(2)], [sc.ps(f"u{n}") for n in range(2)]
        pd = [sc.ps(f"d{n}") for n in range(4)]
        gu_in, dn_in = sc.sem("gu_in"), sc.sem("dn_in")
        gu_hi, gu_lo, dn_hi, dn_lo = (sc.sem(n) for n in ("gu_hi", "gu_lo", "dn_hi", "dn_lo"))
        gate_done, up_done, down_done = (sc.sem(n) for n in ("gate_done", "up_done", "down_done"))
        sig_done, prod_done, a_hi_done, a_lo_done = (sc.sem(n) for n in ("sig_done", "prod_done", "a_hi_done", "a_lo_done"))
        added, dve_own = sc.sem("added"), sc.sem("dve_own")
        NGU = NB * G
        ND = TT * 2
        block = stack.enter_context(nc.Block())

        @block.sync
        def _(sp):
            sc.start_at_one(sp)
            with sp.Fori(0, NG) as i:
                sp.wait_ge(gu_lo, ONE + 2 * i)
                sp.dma_start(st_g[:, :, :], d["w_gate"][i]).then_inc(gu_in, 16)
                sp.dma_start(st_u[:, :, :], d["w_up"][i]).then_inc(gu_in, 16)
                sp.wait_ge(dn_lo, ONE + i)
                sp.dma_start(st_d[:, :, :], d["w_down"][i].rearrange("g p n -> p g n")).then_inc(dn_in, 16)

        @block.scalar
        def _(act):
            with act.Fori(0, NG) as i:
                act.wait_ge(gu_in, ONE + 32 * i + 32)
                act.wait_ge(up_done, ONE + NGU * i)
                nc.scalar.activation(g_hi[:, :, :], st_g[:, :, :], ACT.Copy, scale=WS).then_inc(gu_hi, 1)
                nc.scalar.activation(u_hi[:, :, :], st_u[:, :, :], ACT.Copy, scale=WS).then_inc(gu_hi, 1)
                act.wait_ge(dn_in, ONE + 16 * i + 16)
                act.wait_ge(down_done, ONE + ND * i)
                nc.scalar.activation(d_hi[:, :, :], st_d[:, :, :], ACT.Copy, scale=WS).then_inc(dn_hi, 1)
                for n in range(NGU):
                    b, f = n // G, n % G
                    act.wait_ge(gate_done, ONE + NGU * i + n + 1)
                    act.wait_ge(a_lo_done, ONE + (NGU * i if n < 2 else NGU * i + n - 1))
                    nc.scalar.activation(sig[n % 2][:, :], pg[n % 2][:, :], ACT.Sigmoid, scale=1 / WS).then_inc(sig_done, 1)
                    act.wait_ge(prod_done, ONE + NGU * i + n + 1)
                    nc.scalar.activation(a_hi[:, f, 512 * b:512 * b + 512], sig[n % 2][:, :], ACT.Copy).then_inc(a_hi_done, 1)

        @block.vector
        def _(dve):
            def split_gu(i):
                for n, (lo_, st, hi_) in enumerate(((g_lo, st_g, g_hi), (u_lo, st_u, u_hi))):
                    dve.wait_ge(gu_hi, ONE + 2 * i + n + 1)
                    nc.vector.scalar_tensor_tensor(out=lo_[:, :, :], in0=st[:, :, :], scalar=WS, in1=hi_[:, :, :],
                                                   op0=ALU.mult, op1=ALU.subtract).then_inc(gu_lo, 1)

            def group(i, last):
                own = Chain(dve, dve_own, NGU * i)

                def add(t, g):
                    m = 2 * t + g
                    dve.wait_ge(down_done, ONE + ND * i + m + 1)
                    nc.vector.scalar_tensor_tensor(
                        out=x1[:, t, 512 * g:512 * g + 512], in0=pd[m % 4][:, :], scalar=1 / WS,
                        in1=x1[:, t, 512 * g:512 * g + 512], op0=ALU.mult, op1=ALU.add).then_inc(added, 1)

                dve.wait_ge(dn_hi, ONE + i + 1)
                nc.vector.scalar_tensor_tensor(out=d_lo[:, :, :], in0=st_d[:, :, :], scalar=WS, in1=d_hi[:, :, :],
                                               op0=ALU.mult, op1=ALU.subtract).then_inc(dn_lo, 1)
                for n in range(NGU):
                    b, f = n // G, n % G
                    dve.wait_ge(sig_done, ONE + NGU * i + n + 1)
                    own.link(nc.vector.scalar_tensor_tensor(out=sig[n % 2][:, :], in0=pg[n % 2][:, :], scalar=1 / WS,
                                                            in1=sig[n % 2][:, :], op0=ALU.mult, op1=ALU.mult))
                    dve.wait_ge(up_done, ONE + NGU * i + n + 1)
                    nc.vector.scalar_tensor_tensor(out=sig[n % 2][:, :], in0=pu[n % 2][:, :], scalar=1 / WS,
                                                   in1=sig[n % 2][:, :], op0=ALU.mult, op1=ALU.mult).then_inc(prod_done, 1)
                    dve.wait_ge(a_hi_done, ONE + NGU * i + n + 1)
                    nc.vector.tensor_tensor(a_lo[:, f, 512 * b:512 * b + 512], sig[n % 2][:, :],
                                            a_hi[:, f, 512 * b:512 * b + 512], ALU.subtract).then_inc(a_lo_done, 1)
                dve.wait_ge(added, ONE + ND * i)
                for t in range(TT):
                    for g in range(2):
                        add(t, g)
                    if t == TT // 2 and not last:
                        split_gu(i + 1)

            split_gu(0)
            with dve.Fori(0, NG - 1) as i:
                group(i, last=False)
            group(NG - 1, last=True)

        @block.tensor
        def _(pe):
            with pe.Fori(0, NG) as i:
                pe.wait_ge(gu_lo, ONE + 2 * i + 2)
                for n in range(NGU):
                    b, f = n // G, n % G
                    tok = slice(512 * b, 512 * b + 512)
                    pe.wait_ge(prod_done, ONE + (NGU * i if n < 2 else NGU * i + n - 1))
                    for w_hi, w_lo, bank, sem in ((g_hi, g_lo, pg, gate_done), (u_hi, u_lo, pu, up_done)):
                        for k in range(KT):
                            for w, h in ((w_hi, hi), (w_hi, lo), (w_lo, hi)):
                                ins = nc.tensor.matmul(bank[n % 2][:, :], w[:, k, f * P:f * P + P],
                                                       h[k // 4][:, k % 4, tok],
                                                       start=(k == 0 and w is w_hi and h is hi),
                                                       stop=(k == KT - 1 and w is w_lo))
                        ins.then_inc(sem, 1)
                pe.wait_ge(dn_lo, ONE + i + 1)
                for t in range(TT):
                    if t % (TT // NB) == 0:
                        pe.wait_ge(a_lo_done, ONE + NGU * i + G * (t // (TT // NB)) + G)
                    for g in range(2):
                        m = 2 * t + g
                        pe.wait_ge(added, ONE + (ND * i if m < 4 else ND * i + m - 3))
                        for f in range(G):
                            for a, w in ((a_hi, d_hi), (a_hi, d_lo), (a_lo, d_hi)):
                                ins = nc.tensor.matmul(pd[m % 4][:, :], a[:, f, t * P:t * P + P],
                                                       w[:, f, 512 * g:512 * g + 512],
                                                       start=(f == 0 and a is a_hi and w is d_hi),
                                                       stop=(f == G - 1 and a is a_lo))
                        ins.then_inc(down_done, 1)


def phase_final(nc, d, x1, out):
    T = 4
    with ExitStack() as stack:
        sc = Scope(nc, stack, "fin")
        wrow = sc.sb("wrow", [P, D])
        eps = sc.sb("eps", [P, 1])
        o = [sc.sb(f"o{s}", [P, D]) for s in range(T)]
        square = sc.sb("square", [P, D])
        ss = [sc.sb(f"ss{s}", [P, 3, T]) for s in range(2)]
        const_in, eps_set, act_own, rooted, o_done, dve_own = (
            sc.sem(n) for n in ("const_in", "eps_set", "act_own", "rooted", "o_done", "dve_own"))
        out_done = [sc.sem(f"out{s}") for s in range(2)]
        block = stack.enter_context(nc.Block())
        NI = TT // T

        @block.sync
        def _(sp):
            sc.start_at_one(sp)
            sp.dma_start(wrow[:, :], d["norm_f_w"].partition_broadcast(P)).then_inc(const_in, 16)
            with sp.Fori(0, NI) as i:
                for s in range(T):
                    sp.wait_ge(o_done, ONE + T * i + s + 1)
                    sp.dma_start(out[bass.ds((T * i + s) * P, P), :], o[s][:, :]).then_inc(out_done[s // 2], 16)
            for half in out_done:
                sp.wait_ge(half, ONE + 32 * NI)

        @block.gpsimd
        def _(pool):
            nc.gpsimd.memset(eps[:, :], RMS_EPS).then_inc(eps_set, 1)

        @block.scalar
        def _(act):
            act.wait_ge(eps_set, ONE + 1)
            act.wait_ge(const_in, ONE + 16)
            for i in range(NI):
                if i >= 2:
                    act.wait_ge(o_done, ONE + T * (i - 1))
                for s in range(T):
                    if s or i:
                        act.wait_ge(act_own, ONE + T * i + s)
                    nc.scalar.activation(square[:, :], x1[:, T * i + s, :], ACT.Square,
                                         accum_out=ss[i % 2][:, 0, s:s + 1]).then_inc(act_own, 1)
                act.wait_ge(act_own, ONE + T * i + T)
                nc.scalar.activation(ss[i % 2][:, 1, :], ss[i % 2][:, 0, :], ACT.Sqrt, scale=1.0 / D,
                                     bias=eps[:, 0:1]).then_inc(rooted, 1)

        @block.vector
        def _(dve):
            own = Chain(dve, dve_own)
            dve.wait_ge(const_in, ONE + 16)
            for i in range(NI):
                dve.wait_ge(rooted, ONE + i + 1)
                own.link(nc.vector.reciprocal(ss[i % 2][:, 2, :], ss[i % 2][:, 1, :]))
                for s in range(T):
                    if i:
                        dve.wait_ge(out_done[s // 2], ONE + 32 * i)
                    nc.vector.scalar_tensor_tensor(out=o[s][:, :], in0=x1[:, T * i + s, :], scalar=ss[i % 2][:, 2, s:s + 1],
                                                   in1=wrow[:, :], op0=ALU.mult, op1=ALU.mult).then_inc(o_done, 1)


def build(nc, d, out):
    for n, dirs in (("s_r", ()), ("s_kk", ()), ("s_v", ()), ("s_g", ()), ("s_bonus", ()),
                    ("s_cum", (2,)), ("s_kd", (2,)), ("s_b", (2,))):
        d[n] = nc.dram_tensor(n, (*dirs, HP, P, S), F32, kind="Internal").ap()
    with ExitStack() as whole:
        sc = Scope(nc, whole, "all")
        PASSED.append(sc.sem("passed"))
        oc_hi, oc_lo = sc.sb("oc_hi", [P, HP, S], F16), sc.sb("oc_lo", [P, HP, S], F16)
        with ExitStack() as st:
            s1 = Scope(nc, st, "h")
            hT_hi, hT_lo = s1.sb("hT_hi", [P, KT, S], F16), s1.sb("hT_lo", [P, KT, S], F16)
            phase_norm1(nc, d["x"], d["norm1_w"], d["ident"], hT_hi, hT_lo)
            phase_inproj(nc, d, hT_hi, hT_lo, oc_hi, oc_lo)
        y = sc.sb("y", [P, HP, S + 2 * C])
        phase_scan(nc, d, y)
        or_hi, or_lo = sc.sb("or_hi", [P, HP, S], F16), sc.sb("or_lo", [P, HP, S], F16)
        x1 = sc.sb("x1", [P, TT, D])
        spare = y[:, :, :].rearrange("p h t -> p (h t)")
        with ExitStack() as st:
            s1 = Scope(nc, st, "wo")
            w_hi, w_lo = s1.sb("w_hi", [P, KT, D], F16), s1.sb("w_lo", [P, KT, D], F16)
            phase_groupnorm(nc, d, y, or_hi, or_lo, w_hi, w_lo, x1)
            phase_outproj(nc, d, (or_hi, oc_hi), (or_lo, oc_lo), w_hi, w_lo, x1, spare)
        phase_ffn(nc, d, (or_hi, oc_hi), (or_lo, oc_lo), x1, spare)
        phase_final(nc, d, x1, out)


def layout(inputs):
    f = lambda n: np.asarray(inputs[n])
    L = {}
    L["x"] = f("x").reshape(S, D)
    L["norm1_w"] = f("norm1_w").reshape(1, D)
    w = f("w_in")[0]
    R5, LO, G1 = 512, 3 * 512, 3 * 512 + 256
    cut = lambda a, n: w[:, a:a + n]
    tiles = [cut(LO, P), cut(LO + P, P), np.concatenate([cut(G1, 32), np.zeros((D, P - 32), w.dtype)], 1)]
    CV = G1 + 32
    for h in range(HP):
        for base in (0, R5, 2 * R5, CV + R5, CV + 2 * R5, CV):
            tiles.append(cut(base + P * h, P))
    tiles.append(np.zeros((D, P), w.dtype))
    L["w_in"] = np.ascontiguousarray(np.stack(tiles).reshape(len(tiles), KT, P, P).transpose(0, 2, 1, 3))
    mu = f("mu_shift")[0]
    cols = []
    for h in range(HP):
        c = slice(P * h, P * h + P)
        row = [mu[0:512][c], mu[512:1024][c], mu[1024:1536][c]]
        row += [f(n).reshape(-1)[c] for n in ("k_k", "w0_f", "w0_b", "a0_f", "a0_b", "k_a_f", "k_a_b", "r_k_f", "r_k_b", "gn_w", "gn_b")]
        row += [f("conv_w")[0, t][c] for t in range(3)]
        cols += row
    cols += [mu[LO:LO + P], mu[LO + P:LO + 2 * P], np.concatenate([mu[G1:G1 + 32], np.zeros(P - 32, mu.dtype)])]
    L["chan"] = np.ascontiguousarray(np.stack(cols, 1))
    for n in ("w_up_f", "w_up_b", "a_up_f", "a_up_b", "g_up"):
        L[n] = f(n)[0]
    L["ident"] = np.eye(P, dtype=np.float32)
    L["ones"] = np.kron(np.eye(2, dtype=np.float32), np.ones((C, C), np.float32))
    L["norm2_w"], L["norm_f_w"] = f("norm2_w").reshape(1, D), f("norm_f_w").reshape(1, D)
    L["w_out"] = f("w_out")[0]
    for n in ("w_gate", "w_up"):
        L[n] = np.ascontiguousarray(f(n)[0].reshape(KT, P, FT // 2, 2 * P).transpose(2, 1, 0, 3))
    L["w_down"] = f("w_down")[0].reshape(FT // 2, 2, P, D)
    L["identh"] = np.eye(P, dtype=np.float16)
    L["idents"] = np.tile(np.eye(C, dtype=np.float16), (2, 1))
    row, cl = np.arange(P)[:, None] % C, np.arange(C)[None]
    L["maskA"] = np.stack([np.stack([cl > row, cl >= row], 1), np.stack([cl < row, cl <= row], 1)], 1).astype(np.float32)
    lv = []
    for way in range(2):
        for l in range(6):
            m = 2 ** l
            late_t, late_s = row // m % 2, cl // m % 2
            lv.append((row // (2 * m) == cl // (2 * m)) & (late_t == 1 - way) & (late_s == way))
    L["maskL"] = ((row == cl)[:, None] - np.stack(lv, 1).astype(np.float32)).reshape(P, 2, 6, C).astype(np.float32)
    L["keep"] = np.ascontiguousarray(np.broadcast_to((np.arange(512) % C != 0).astype(np.float16), (P, 512)))
    return L


def kernel(**inputs):
    import concourse.bacc as bacc
    from concourse.bass_utils import run_bass_kernel_spmd

    nc = bacc.Bacc("TRN2", target_bir_lowering=False, num_devices=1)
    arrays = layout(inputs)
    d = {n: nc.dram_tensor(n, a.shape, mybir.dt.from_np(a.dtype), kind="ExternalInput").ap() for n, a in arrays.items()}
    out = nc.dram_tensor("out", (S, D), F32, kind="ExternalOutput").ap()
    build(nc, d, out)
    r = run_bass_kernel_spmd(nc, [arrays], core_ids=[0])
    return r.results[0]["out"].reshape(1, S, D)
```
